# Optimizing a Trainium2 kernel written in Bass

```python
import jax, jax.numpy as jnp
from jax import lax
import numpy as np
import math

D_MODEL = 1024
BATCH = 1
SEQ = 256
DEPTH = 2

GRID_W = 64
CTX_LEN = 256
N_MIXERS = 2
GLA_HEADS = 4
GLA_DK = D_MODEL // 2
GLA_DV = D_MODEL
GLA_DK_HEAD = GLA_DK // GLA_HEADS
GLA_DV_HEAD = GLA_DV // GLA_HEADS
GLA_LOW_RANK = 16
GLA_GATE_NORM = 16.0
GLA_CHUNK = 64
ROPE_BASE = 10000.0
NA_HEADS = 16
NA_HEAD_DIM = D_MODEL // NA_HEADS
NA_KH = 8
NA_KW = 16
D_FF = 2816
CONV_W = 3
EPS = 1e-6


def rms_norm(x, g):
    xf = x.astype(jnp.float32)
    y = xf * lax.rsqrt(jnp.mean(xf * xf, axis=-1, keepdims=True) + EPS)
    return (y * g.astype(jnp.float32)).astype(x.dtype)

def modulate(x, g, shift, scale):
    return rms_norm(x, g) * (1 + scale) + shift

def rope_2d(x, rows, cols):
    half = x.shape[-1] // 2
    inv = 1.0 / (ROPE_BASE ** (jnp.arange(0, half, 2, dtype=jnp.float32) / half))

    def rot(xa, pos):
        ang = pos.astype(jnp.float32)[:, None] * inv[None, :]
        cos = jnp.cos(ang)[:, None, :].astype(x.dtype)
        sin = jnp.sin(ang)[:, None, :].astype(x.dtype)
        x1, x2 = jnp.split(xa, 2, axis=-1)
        return jnp.concatenate([x1 * cos - x2 * sin, x1 * sin + x2 * cos], axis=-1)

    return jnp.concatenate([rot(x[..., :half], rows), rot(x[..., half:], cols)], axis=-1)

def gla_chunked(q, k, v, g, s0):
    B, H, T, dk = q.shape
    dv = v.shape[-1]
    n = T // GLA_CHUNK

    def to_chunks(t):
        return jnp.moveaxis(t.reshape(B, H, n, GLA_CHUNK, t.shape[-1]), 2, 0)

    mask = jnp.tril(jnp.ones((GLA_CHUNK, GLA_CHUNK), dtype=bool))[:, :, None]

    def step(s, xs):
        qc, kc, vc, gc = xs
        b = jnp.cumsum(gc, axis=2)
        b_last = b[:, :, -1:, :]
        o_inter = jnp.einsum('bhid,bhde->bhie', qc * jnp.exp(b), s)
        diff = jnp.where(mask, b[:, :, :, None, :] - b[:, :, None, :, :], -jnp.inf)
        att = jnp.einsum('bhid,bhjd,bhijd->bhij', qc, kc, jnp.exp(diff))
        o = o_inter + jnp.einsum('bhij,bhje->bhie', att, vc)
        s_new = jnp.exp(b_last)[:, :, 0, :, None] * s + jnp.einsum('bhjd,bhje->bhde', kc * jnp.exp(b_last - b), vc)
        return s_new, o

    s_final, o = lax.scan(step, s0, (to_chunks(q), to_chunks(k), to_chunks(v), to_chunks(g)))
    o = jnp.moveaxis(o, 0, 2).reshape(B, H, T, dv)
    return o, s_final

def gla_mixer(h_ctx, h_lat, w_in, a_w1, a_w2, a_b, norm_g, w_out, with_ctx_out):
    B, N, _ = h_lat.shape
    L = h_ctx.shape[1]
    T = L + N
    h = jnp.concatenate([h_ctx, h_lat], axis=1)
    proj = h @ w_in
    q, k, v, r = jnp.split(proj, [GLA_DK, 2 * GLA_DK, 2 * GLA_DK + GLA_DV], axis=-1)
    q = q.reshape(B, T, GLA_HEADS, GLA_DK_HEAD)
    k = k.reshape(B, T, GLA_HEADS, GLA_DK_HEAD)
    v = v.reshape(B, T, GLA_HEADS, GLA_DV_HEAD)
    pos = jnp.arange(N)
    rows, cols = pos // GRID_W, pos % GRID_W
    q = jnp.concatenate([q[:, :L], rope_2d(q[:, L:], rows, cols)], axis=1) * (GLA_DK_HEAD ** -0.5)
    k = jnp.concatenate([k[:, :L], rope_2d(k[:, L:], rows, cols)], axis=1)
    to_bhtd = lambda t: jnp.transpose(t, (0, 2, 1, 3))
    q, k, v = to_bhtd(q), to_bhtd(k), to_bhtd(v)
    s0 = jnp.zeros((B, GLA_HEADS, GLA_DK_HEAD, GLA_DV_HEAD), dtype=q.dtype)
    flip = lambda t: jnp.flip(t, axis=2)

    o_sum = None
    for d in range(2):
        g = jax.nn.log_sigmoid((h @ a_w1[d]) @ a_w2[d] + a_b[d]) / GLA_GATE_NORM
        g = to_bhtd(g.reshape(B, T, GLA_HEADS, GLA_DK_HEAD))
        qd, kd, vd, gd = q, k, v, g
        if d == 1:
            qd, kd, vd, gd = flip(q), flip(k), flip(v), flip(g)
            o_c, s_c = gla_chunked(qd[:, :, N:], kd[:, :, N:], vd[:, :, N:], gd[:, :, N:], s0)
            o_l, _ = gla_chunked(qd[:, :, :N], kd[:, :, :N], vd[:, :, :N], gd[:, :, :N], s_c)
            o_d = jnp.concatenate([flip(o_c), flip(o_l)], axis=2)
        else:
            o_c, s_c = gla_chunked(qd[:, :, :L], kd[:, :, :L], vd[:, :, :L], gd[:, :, :L], s0)
            o_l, _ = gla_chunked(qd[:, :, L:], kd[:, :, L:], vd[:, :, L:], gd[:, :, L:], s_c)
            o_d = jnp.concatenate([o_c, o_l], axis=2)
        o_sum = o_d if o_sum is None else o_sum + o_d

    o = jnp.transpose(o_sum, (0, 2, 1, 3))
    r = r.reshape(B, T, GLA_HEADS, GLA_DV_HEAD)
    if not with_ctx_out:
        o, r = o[:, L:], r[:, L:]
    y = (rms_norm(o, norm_g) * jax.nn.silu(r)).reshape(B, -1, GLA_DV) @ w_out
    if with_ctx_out:
        return y[:, :L], y[:, L:]
    return None, y

def na_mixer(h_ctx, h_lat, w_qkv, rpb, w_out, with_ctx_out):
    B, N, _ = h_lat.shape
    L = h_ctx.shape[1]
    rows_n = N // GRID_W
    kh = min(NA_KH, rows_n)
    q_l, k_l, v_l = jnp.split(h_lat @ w_qkv, 3, axis=-1)
    q_c, k_c, v_c = jnp.split(h_ctx @ w_qkv, 3, axis=-1)
    sc = NA_HEAD_DIM ** -0.5
    q_g = (q_l * sc).reshape(B, rows_n, GRID_W, NA_HEADS, NA_HEAD_DIM)
    k_g = k_l.reshape(B, rows_n, GRID_W, NA_HEADS, NA_HEAD_DIM)
    v_g = v_l.reshape(B, rows_n, GRID_W, NA_HEADS, NA_HEAD_DIM)
    k_c = k_c.reshape(B, L, NA_HEADS, NA_HEAD_DIM)
    v_c = v_c.reshape(B, L, NA_HEADS, NA_HEAD_DIM)

    cpos = np.arange(GRID_W)
    col_start = np.clip(cpos - NA_KW // 2, 0, GRID_W - NA_KW)
    col_idx = col_start[:, None] + np.arange(NA_KW)[None, :]
    dc_idx = col_idx - cpos[:, None] + (NA_KW - 1)
    rpb_c = rpb[:, :, dc_idx]

    def row_block(r):
        rs = jnp.clip(r - kh // 2, 0, rows_n - kh)
        q_r = lax.dynamic_index_in_dim(q_g, r, axis=1, keepdims=False)
        k_rows = lax.dynamic_slice_in_dim(k_g, rs, kh, axis=1)
        v_rows = lax.dynamic_slice_in_dim(v_g, rs, kh, axis=1)
        k_win = k_rows[:, :, col_idx]
        v_win = v_rows[:, :, col_idx]
        s_nb = jnp.einsum('bchd,bicjhd->bhcij', q_r, k_win).reshape(B, NA_HEADS, GRID_W, kh * NA_KW)
        dr_idx = rs + jnp.arange(kh) - r + (NA_KH - 1)
        bias = jnp.take(rpb_c, dr_idx, axis=1)
        bias = jnp.transpose(bias, (0, 2, 1, 3)).reshape(NA_HEADS, GRID_W, kh * NA_KW)
        s_nb = s_nb + bias[None]
        s_cx = jnp.einsum('bchd,blhd->bhcl', q_r, k_c)
        p = jax.nn.softmax(jnp.concatenate([s_nb, s_cx], axis=-1).astype(jnp.float32), axis=-1).astype(v_l.dtype)
        p_nb = p[..., :kh * NA_KW].reshape(B, NA_HEADS, GRID_W, kh, NA_KW)
        p_cx = p[..., kh * NA_KW:]
        return jnp.einsum('bhcij,bicjhd->bchd', p_nb, v_win) + jnp.einsum('bhcl,blhd->bchd', p_cx, v_c)

    o = lax.map(row_block, jnp.arange(rows_n))
    o_lat = jnp.transpose(o, (1, 0, 2, 3, 4)).reshape(B, N, D_MODEL) @ w_out
    if not with_ctx_out:
        return None, o_lat
    qc = (q_c * sc).reshape(B, L, NA_HEADS, NA_HEAD_DIM)
    s = jnp.einsum('blhd,bmhd->bhlm', qc, k_c)
    p = jax.nn.softmax(s.astype(jnp.float32), axis=-1).astype(v_c.dtype)
    o_ctx = jnp.einsum('bhlm,bmhd->blhd', p, v_c).reshape(B, L, D_MODEL) @ w_out
    return o_ctx, o_lat

def conv_ffn(h, w_in, conv_w, conv_b, w_out):
    a, val = jnp.split(h @ w_in, 2, axis=-1)
    ap = jnp.pad(a, ((0, 0), (1, 1), (0, 0)))
    a = ap[:, :-2] * conv_w[0] + ap[:, 1:-1] * conv_w[1] + ap[:, 2:] * conv_w[2] + conv_b
    return (jax.nn.silu(a) * val) @ w_out

def first_inputs(seed: int = 0) -> dict:
    key = jax.random.key(seed)
    ks = jax.random.split(key, 24)
    n_gla = (DEPTH + N_MIXERS - 1) // N_MIXERS
    n_na = DEPTH // N_MIXERS
    D = D_MODEL

    def nrm(k, shape, scale):
        return jax.random.normal(k, shape, jnp.float32) * scale

    return {
        "x": nrm(ks[0], (BATCH, SEQ, D), 1.0),
        "c": nrm(ks[1], (BATCH, D), 1.0),
        "ctx": nrm(ks[2], (BATCH, CTX_LEN, D), 1.0),
        "c_ctx": nrm(ks[3], (D,), 1.0),
        "ada_w": nrm(ks[4], (DEPTH, D, 6 * D), 0.5 * D ** -0.5),
        "ada_b": nrm(ks[5], (DEPTH, 6 * D), 0.02),
        "norm1_g": 1.0 + nrm(ks[6], (DEPTH, D), 0.02),
        "norm2_g": 1.0 + nrm(ks[7], (DEPTH, D), 0.02),
        "ffn_w_in": nrm(ks[8], (DEPTH, D, 2 * D_FF), D ** -0.5),
        "ffn_conv_w": nrm(ks[9], (DEPTH, CONV_W, D_FF), CONV_W ** -0.5),
        "ffn_conv_b": nrm(ks[10], (DEPTH, D_FF), 0.02),
        "ffn_w_out": nrm(ks[11], (DEPTH, D_FF, D), D_FF ** -0.5),
        "gla_w_in": nrm(ks[12], (n_gla, D, 2 * GLA_DK + 2 * GLA_DV), D ** -0.5),
        "gla_a_w1": nrm(ks[13], (n_gla, 2, D, GLA_LOW_RANK), D ** -0.5),
        "gla_a_w2": nrm(ks[14], (n_gla, 2, GLA_LOW_RANK, GLA_DK), GLA_LOW_RANK ** -0.5),
        "gla_a_b": nrm(ks[15], (n_gla, 2, GLA_DK), 0.1),
        "gla_norm_g": 1.0 + nrm(ks[16], (n_gla, GLA_DV_HEAD), 0.02),
        "gla_w_out": nrm(ks[17], (n_gla, GLA_DV, D), GLA_DV ** -0.5),
        "na_w_qkv": nrm(ks[18], (n_na, D, 3 * D), D ** -0.5),
        "na_rpb": nrm(ks[19], (n_na, NA_HEADS, 2 * NA_KH - 1, 2 * NA_KW - 1), 0.1),
        "na_w_out": nrm(ks[20], (n_na, D, D), D ** -0.5),
        "final_g": 1.0 + nrm(ks[21], (D,), 0.02),
    }

def first_block(x, c, ctx, c_ctx, ada_w, ada_b, norm1_g, norm2_g, ffn_w_in, ffn_conv_w, ffn_conv_b, ffn_w_out,
              gla_w_in, gla_a_w1, gla_a_w2, gla_a_b, gla_norm_g, gla_w_out, na_w_qkv, na_rpb, na_w_out, final_g):
    x_lat, x_ctx = x, ctx
    sc_lat = jax.nn.silu(c)
    sc_ctx = jax.nn.silu(c_ctx)
    for i in range(DEPTH):
        last = i == DEPTH - 1
        j = i // N_MIXERS
        mod_l = (sc_lat @ ada_w[i] + ada_b[i])[:, None, :]
        mod_c = sc_ctx @ ada_w[i] + ada_b[i]
        sh1_l, s1_l, g1_l, sh2_l, s2_l, g2_l = jnp.split(mod_l, 6, axis=-1)
        sh1_c, s1_c, g1_c, sh2_c, s2_c, g2_c = jnp.split(mod_c, 6, axis=-1)

        h_l = modulate(x_lat, norm1_g[i], sh1_l, s1_l)
        h_c = modulate(x_ctx, norm1_g[i], sh1_c, s1_c)
        if i % N_MIXERS == 0:
            o_c, o_l = gla_mixer(h_c, h_l, gla_w_in[j], gla_a_w1[j], gla_a_w2[j], gla_a_b[j],
                                 gla_norm_g[j], gla_w_out[j], not last)
        else:
            o_c, o_l = na_mixer(h_c, h_l, na_w_qkv[j], na_rpb[j], na_w_out[j], not last)
        x_lat = x_lat + g1_l * o_l

        h_l = modulate(x_lat, norm2_g[i], sh2_l, s2_l)
        x_lat = x_lat + g2_l * conv_ffn(h_l, ffn_w_in[i], ffn_conv_w[i], ffn_conv_b[i], ffn_w_out[i])

        if not last:
            x_ctx = x_ctx + g1_c * o_c
            h_c = modulate(x_ctx, norm2_g[i], sh2_c, s2_c)
            x_ctx = x_ctx + g2_c * conv_ffn(h_c, ffn_w_in[i], ffn_conv_w[i], ffn_conv_b[i], ffn_w_out[i])
    return rms_norm(x_lat, final_g)


DEPTH_2 = 1

N_META = 16
D_MIX = D_MODEL
D_HYENA = D_MIX // 2
D_HGRN = D_MIX - D_HYENA
HYENA_ORDER = 2
SHORT_CONV = 3
FILTER_EMB = 33
FILTER_BANDS = (FILTER_EMB - 1) // 2
FILTER_HIDDEN = 64
DECAY_TARGET = 1e-2
FAST_DECAY_PCT = 0.3
SLOW_DECAY_PCT = 1.5
HGRN_HEAD_DIM = 128
HGRN_HEADS = D_HGRN // HGRN_HEAD_DIM
CHUNK = 64
N_GROUPS = 8
EXPERTS_PER_GROUP = 8
N_EXPERTS = N_GROUPS * EXPERTS_PER_GROUP
TOP_K = 2
D_EXPERT = D_MODEL // 2
MOE_BLOCK = 128
D_HYENA_PROJ = (HYENA_ORDER + 1) * D_HYENA
D_HGRN_PROJ = 5 * D_HGRN
D_IN_PROJ = D_HYENA_PROJ + D_HGRN_PROJ


def rms_norm_2(x, gain):
    xf = x.astype(jnp.float32)
    y = xf * lax.rsqrt(jnp.mean(xf * xf, axis=-1, keepdims=True) + EPS)
    return (y * gain.astype(jnp.float32)).astype(x.dtype)

def centred_short_conv(u, w, b):
    L = u.shape[1]
    half = SHORT_CONV // 2
    up = jnp.pad(u, ((0, 0), (half, SHORT_CONV - 1 - half), (0, 0)))
    y = b
    for j in range(SHORT_CONV):
        y = y + up[:, j:j + L] * w[j]
    return y

def hyena_filter_spectra(L, w1, b1, w2, b2, w3, freq):
    f32 = jnp.float32
    pos = jnp.arange(L, dtype=f32)
    t = pos / max(L - 1, 1)
    bands = jnp.linspace(1e-4, FILTER_BANDS - 1, FILTER_BANDS, dtype=f32)
    ang = (2.0 * math.pi / L) * pos[:, None] * bands[None, :]
    z = jnp.concatenate([t[:, None], jnp.cos(ang), -jnp.sin(ang)], axis=-1)
    fr = freq.astype(f32)
    hid = jnp.sin(fr * (z @ w1.astype(f32) + b1.astype(f32)))
    hid = jnp.sin(fr * (hid @ w2.astype(f32) + b2.astype(f32)))
    filt = (hid @ w3.astype(f32)).reshape(L, 2, HYENA_ORDER, D_HYENA)
    deltas = jnp.abs(jnp.linspace(math.log(DECAY_TARGET) / SLOW_DECAY_PCT,
                                  math.log(DECAY_TARGET) / FAST_DECAY_PCT, D_HYENA, dtype=f32))
    window = jnp.exp(-t[:, None] * deltas[None, :])
    filt = filt * window[:, None, None, :]
    h_fwd, h_bwd = filt[:, 0], filt[:, 1]
    two_sided = jnp.concatenate([h_fwd, jnp.zeros_like(h_fwd[:1]), h_bwd[:0:-1]], axis=0)
    return jnp.fft.rfft(two_sided, axis=0)

def fft_long_conv(u, spec, skip):
    L = u.shape[1]
    uf = u.astype(jnp.float32)
    y = jnp.fft.irfft(jnp.fft.rfft(uf, n=2 * L, axis=1) * spec[None], n=2 * L, axis=1)[:, :L]
    return (y + uf * skip.astype(jnp.float32)).astype(u.dtype)

def hyena_mixer(p, conv_w, conv_b, w1, b1, w2, b2, w3, freq, skip):
    L = p.shape[1]
    u = centred_short_conv(p, conv_w, conv_b)
    z = u[..., :D_HYENA]
    spectra = hyena_filter_spectra(L, w1, b1, w2, b2, w3, freq)
    for n in range(HYENA_ORDER):
        gate = u[..., (n + 1) * D_HYENA:(n + 2) * D_HYENA]
        z = gate * fft_long_conv(z, spectra[:, n], skip[n])
    return z

def chunked_gated_linear_scan(q, k, v, log_f):
    B, T, H, DK = q.shape
    DV = v.shape[-1]
    N = T // CHUNK
    q, k, v, log_f = [a.reshape(B, N, CHUNK, H, a.shape[-1]) for a in (q, k, v, log_f)]
    b = jnp.cumsum(log_f, axis=2)
    b_last = b[:, :, -1]
    b_mid = b[:, :, CHUNK // 2][:, :, None]
    scores = jnp.einsum('bnthd,bnshd->bnhts', q * jnp.exp(b - b_mid), k * jnp.exp(b_mid - b))
    lower_tri = jnp.tril(jnp.ones((CHUNK, CHUNK), dtype=bool))
    scores = jnp.where(lower_tri, scores, 0.0)
    o_intra = jnp.einsum('bnhts,bnshv->bnthv', scores, v)
    chunk_state = jnp.einsum('bnshd,bnshv->bnhdv', k * jnp.exp(b_last[:, :, None] - b), v)
    chunk_decay = jnp.exp(b_last)

    def step(S, inp):
        dec, U = inp
        return dec[..., None] * S + U, S

    S0 = jnp.zeros((B, H, DK, DV), q.dtype)
    _, S_in = lax.scan(step, S0, (jnp.moveaxis(chunk_decay, 1, 0), jnp.moveaxis(chunk_state, 1, 0)))
    S_in = jnp.moveaxis(S_in, 0, 1)
    o_inter = jnp.einsum('bnthd,bnhdv->bnthv', q * jnp.exp(b), S_in)
    return (o_intra + o_inter).reshape(B, T, H, DV)

def hgrn2_mixer(p, lb_f, lb_b, norm_w):
    f32 = jnp.float32
    B, L, _ = p.shape
    q, f_fwd, f_bwd, i_in, g = [p[..., j * D_HGRN:(j + 1) * D_HGRN] for j in range(5)]

    def heads(a):
        return a.reshape(B, L, HGRN_HEADS, HGRN_HEAD_DIM)

    qh = heads(jax.nn.silu(q.astype(f32)))
    vh = heads(i_in.astype(f32))

    def forget(logit, lb):
        lb = lb.astype(f32)
        f = lb + (1.0 - lb) * jax.nn.sigmoid(logit.astype(f32))
        return heads(1.0 - f), heads(jnp.log(f))

    k_f, lf_f = forget(f_fwd, lb_f)
    k_b, lf_b = forget(f_bwd, lb_b)
    n_pad = (-N_META) % CHUNK

    def pad(a):
        return jnp.pad(a, ((0, 0), (n_pad, 0), (0, 0), (0, 0)))

    def flip(a):
        return a[:, ::-1]

    qp, vp = pad(qh), pad(vh)
    o_f = chunked_gated_linear_scan(qp, pad(k_f), vp, pad(lf_f))
    o_b = flip(chunked_gated_linear_scan(flip(qp), flip(pad(k_b)), flip(vp), flip(pad(lf_b))))
    o = (o_f + o_b)[:, n_pad:]
    o = o * lax.rsqrt(jnp.mean(o * o, axis=-1, keepdims=True) + EPS)
    o = o.reshape(B, L, D_HGRN) * norm_w.astype(f32) * jax.nn.silu(g.astype(f32))
    return o.astype(p.dtype)

def hier_moe(h, w_rg, w_re, w_gate, w_up, w_down):
    f32 = jnp.float32
    B, L, D = h.shape
    n_tok = B * L
    hf = h.reshape(n_tok, D)
    g_logits = (hf @ w_rg).astype(f32)
    g_sel = jnp.argmax(g_logits, axis=-1)
    p_group = jnp.take_along_axis(jax.nn.softmax(g_logits, axis=-1), g_sel[:, None], axis=-1)
    e_logits = jnp.einsum('nd,dge->nge', hf, w_re).astype(f32)
    e_logits = e_logits[jnp.arange(n_tok), g_sel]
    p_top, e_top = lax.top_k(jax.nn.softmax(e_logits, axis=-1), TOP_K)
    gate = p_group * p_top / jnp.sum(p_top, axis=-1, keepdims=True)
    expert_id = (g_sel[:, None] * EXPERTS_PER_GROUP + e_top).reshape(-1).astype(jnp.int32)

    M = n_tok * TOP_K
    n_blocks = -(-M // MOE_BLOCK) + N_EXPERTS
    n_slots = n_blocks * MOE_BLOCK
    order = jnp.argsort(expert_id)
    eid_s = expert_id[order]
    tok_s = (jnp.arange(M, dtype=jnp.int32) // TOP_K)[order]
    gate_s = gate.reshape(-1)[order]
    counts = jnp.bincount(expert_id, length=N_EXPERTS)
    padded = (counts + MOE_BLOCK - 1) // MOE_BLOCK * MOE_BLOCK
    start = jnp.cumsum(counts) - counts
    pend = jnp.cumsum(padded)
    dest = (pend - padded)[eid_s] + jnp.arange(M, dtype=jnp.int32) - start[eid_s]
    tok_buf = jnp.zeros((n_slots,), jnp.int32).at[dest].set(tok_s)
    gate_buf = jnp.zeros((n_slots,), f32).at[dest].set(gate_s)
    block_eid = jnp.minimum(
        jnp.searchsorted(pend, jnp.arange(n_blocks, dtype=pend.dtype) * MOE_BLOCK, side='right'),
        N_EXPERTS - 1)
    xb = hf[tok_buf].reshape(n_blocks, MOE_BLOCK, D)

    def expert_block(args):
        xe, e = args
        return (jax.nn.silu(xe @ w_gate[e]) * (xe @ w_up[e])) @ w_down[e]

    yb = lax.map(expert_block, (xb, block_eid)).reshape(n_slots, D)
    y = jnp.zeros_like(hf).at[tok_buf].add(yb * gate_buf[:, None].astype(yb.dtype))
    return y.reshape(B, L, D)

def second_inputs(seed: int = 0) -> dict:
    key = jax.random.key(seed)
    ks = jax.random.split(key, 25)

    def nrm(k, shape, scale):
        return scale * jax.random.normal(k, shape, jnp.float32)

    return {
        'x': nrm(ks[0], (BATCH, SEQ, D_MODEL), 1.0),
        'meta_tokens': nrm(ks[1], (N_META, D_MODEL), 1.0),
        'w_in': nrm(ks[2], (DEPTH_2, D_MODEL, D_IN_PROJ), D_MODEL ** -0.5),
        'conv_w': nrm(ks[3], (DEPTH_2, SHORT_CONV, D_HYENA_PROJ), SHORT_CONV ** -0.5),
        'conv_b': nrm(ks[4], (DEPTH_2, D_HYENA_PROJ), 0.01),
        'filt_w1': nrm(ks[5], (DEPTH_2, FILTER_EMB, FILTER_HIDDEN), FILTER_EMB ** -0.5),
        'filt_b1': nrm(ks[6], (DEPTH_2, FILTER_HIDDEN), 0.1),
        'filt_w2': nrm(ks[7], (DEPTH_2, FILTER_HIDDEN, FILTER_HIDDEN), FILTER_HIDDEN ** -0.5),
        'filt_b2': nrm(ks[8], (DEPTH_2, FILTER_HIDDEN), 0.1),
        'filt_w3': nrm(ks[9], (DEPTH_2, FILTER_HIDDEN, 2 * HYENA_ORDER * D_HYENA), 0.02),
        'filt_freq': 1.0 + nrm(ks[10], (DEPTH_2, FILTER_HIDDEN), 0.01),
        'filt_skip': nrm(ks[11], (DEPTH_2, HYENA_ORDER, D_HYENA), 1.0),
        'hyena_norm': 1.0 + nrm(ks[12], (DEPTH_2, D_HYENA), 0.01),
        'lb_fwd': nrm(ks[13], (DEPTH_2 + 1, D_HGRN), 0.1),
        'lb_bwd': nrm(ks[14], (DEPTH_2 + 1, D_HGRN), 0.1),
        'hgrn_norm': 1.0 + nrm(ks[15], (DEPTH_2, D_HGRN), 0.01),
        'w_out': nrm(ks[16], (DEPTH_2, D_MIX, D_MODEL), D_MIX ** -0.5),
        'norm_mix': 1.0 + nrm(ks[17], (DEPTH_2, D_MODEL), 0.01),
        'norm_ffn': 1.0 + nrm(ks[18], (DEPTH_2, D_MODEL), 0.01),
        'w_router_group': nrm(ks[19], (DEPTH_2, D_MODEL, N_GROUPS), D_MODEL ** -0.5),
        'w_router_expert': nrm(ks[20], (DEPTH_2, D_MODEL, N_GROUPS, EXPERTS_PER_GROUP), D_MODEL ** -0.5),
        'w_gate': nrm(ks[21], (DEPTH_2, N_EXPERTS, D_MODEL, D_EXPERT), D_MODEL ** -0.5),
        'w_up': nrm(ks[22], (DEPTH_2, N_EXPERTS, D_MODEL, D_EXPERT), D_MODEL ** -0.5),
        'w_down': nrm(ks[23], (DEPTH_2, N_EXPERTS, D_EXPERT, D_MODEL), D_EXPERT ** -0.5),
        'norm_final': 1.0 + nrm(ks[24], (D_MODEL,), 0.01),
    }

def second_block(x, meta_tokens, w_in, conv_w, conv_b, filt_w1, filt_b1, filt_w2, filt_b2, filt_w3,
              filt_freq, filt_skip, hyena_norm, lb_fwd, lb_bwd, hgrn_norm, w_out, norm_mix, norm_ffn,
              w_router_group, w_router_expert, w_gate, w_up, w_down, norm_final):
    B = x.shape[0]
    meta = jnp.broadcast_to(meta_tokens[None].astype(x.dtype), (B, N_META, x.shape[-1]))
    h = jnp.concatenate([meta, x], axis=1)
    lbf_all = jnp.cumsum(jax.nn.softmax(lb_fwd.astype(jnp.float32), axis=0), axis=0)
    lbb_all = jnp.cumsum(jax.nn.softmax(lb_bwd.astype(jnp.float32), axis=0), axis=0)
    for l in range(DEPTH_2):
        a = rms_norm_2(h, norm_mix[l])
        p = a @ w_in[l]
        y_hy = hyena_mixer(p[..., :D_HYENA_PROJ], conv_w[l], conv_b[l], filt_w1[l], filt_b1[l],
                           filt_w2[l], filt_b2[l], filt_w3[l], filt_freq[l], filt_skip[l])
        y_hy = rms_norm_2(y_hy, hyena_norm[l])
        y_hg = hgrn2_mixer(p[..., D_HYENA_PROJ:], lbf_all[l], lbb_all[l], hgrn_norm[l])
        h = h + jnp.concatenate([y_hy, y_hg], axis=-1) @ w_out[l]
        h = h + hier_moe(rms_norm_2(h, norm_ffn[l]), w_router_group[l], w_router_expert[l],
                         w_gate[l], w_up[l], w_down[l])
    h = rms_norm_2(h, norm_final)
    return h[:, N_META:]


def setup_inputs(seed=0):
    out = dict(first_inputs(seed))
    for name, value in second_inputs(seed + 1).items():
        if name != "x":
            out[name + "_2"] = value
    return out


def reference(
    x, c, ctx, c_ctx, ada_w, ada_b, norm1_g, norm2_g, ffn_w_in, ffn_conv_w, ffn_conv_b,
    ffn_w_out, gla_w_in, gla_a_w1, gla_a_w2, gla_a_b, gla_norm_g, gla_w_out, na_w_qkv, na_rpb,
    na_w_out, final_g, meta_tokens_2, w_in_2, conv_w_2, conv_b_2, filt_w1_2, filt_b1_2,
    filt_w2_2, filt_b2_2, filt_w3_2, filt_freq_2, filt_skip_2, hyena_norm_2, lb_fwd_2, lb_bwd_2,
    hgrn_norm_2, w_out_2, norm_mix_2, norm_ffn_2, w_router_group_2, w_router_expert_2, w_gate_2,
    w_up_2, w_down_2, norm_final_2,
):
    x = first_block(
        x, c, ctx, c_ctx, ada_w, ada_b, norm1_g, norm2_g, ffn_w_in, ffn_conv_w, ffn_conv_b,
        ffn_w_out, gla_w_in, gla_a_w1, gla_a_w2, gla_a_b, gla_norm_g, gla_w_out, na_w_qkv,
        na_rpb, na_w_out, final_g,
    )
    return second_block(
        x, meta_tokens_2, w_in_2, conv_w_2, conv_b_2, filt_w1_2, filt_b1_2, filt_w2_2,
        filt_b2_2, filt_w3_2, filt_freq_2, filt_skip_2, hyena_norm_2, lb_fwd_2, lb_bwd_2,
        hgrn_norm_2, w_out_2, norm_mix_2, norm_ffn_2, w_router_group_2, w_router_expert_2,
        w_gate_2, w_up_2, w_down_2, norm_final_2,
    )


_drawn_inputs = setup_inputs


def setup_inputs(seed=0):
    import zlib

    import numpy as np

    out = dict(_drawn_inputs(seed))
    spreads = {}
    factors = {'norm1_g': 3.395,
     'norm2_g': 3.411,
     'ffn_conv_b': 3.646,
     'gla_a_b': 3.18,
     'gla_norm_g': 5.121,
     'na_rpb': 7.567,
     'conv_b_2': 2.674,
     'filt_freq_2': 6.135,
     'hyena_norm_2': 5.34,
     'lb_fwd_2': 8.0,
     'lb_bwd_2': 8.0,
     'hgrn_norm_2': 6.954,
     'norm_mix_2': 3.166,
     'norm_ffn_2': 4.088,
     'norm_final_2': 5.642}
    for name, (base, spread) in spreads.items():
        noise = np.random.default_rng([zlib.crc32(name.encode()), seed]).standard_normal(out[name].shape)
        drawn = base * np.exp(spread * noise) if base else spread * noise
        out[name] = __import__('jax').numpy.asarray(drawn.astype(out[name].dtype))
    for name, factor in factors.items():
        out[name] = (out[name] * factor).astype(out[name].dtype)
    return out
```

```python
from contextlib import ExitStack

import numpy as np

import concourse.bass as bass
from concourse import mybir

F32 = mybir.dt.float32
I32 = mybir.dt.int32
U32 = mybir.dt.uint32
ALU = mybir.AluOpType
ACT = mybir.ActivationFunctionType
AX_X = mybir.AxisListType.X

P = 128
D = 1024
DC = D // P
NT = 256
TT = 512
D_FF = 2816
FC = D_FF // P
HEADS = 4
CH = 64
GRID = 64
NA_H, NA_KH, NA_KW = 16, 8, 16
N_META = 16
T2 = N_META + NT
NFFT = 2 * T2
NF = T2 + 1
HY = 512
HC = HY // P
EMB, HID = 33, 64
NE, NG, EPG = 64, 8, 8
DE = 512
WIN = 128
SLOTS = 2 * T2
EXTRA = SLOTS // WIN
EPS = 1e-6
GATE_NORM = 16.0
FT = [(0, 128), (128, 128), (256, NF - 256)]
TTILE = [(0, 128), (128, 128), (256, T2 - 256)]
STILE = [(s, min(128, SLOTS - s)) for s in range(0, SLOTS, 128)]

COLS = [("c2", 2 * DC), ("n1", 2 * DC), ("n2", 2 * DC), ("fin", DC), ("ada_b", 2 * 48),
        ("fcw", 2 * 3 * FC), ("fcb", 2 * FC), ("gab", 2 * HEADS), ("gng", 2),
        ("cw2", 3 * 12), ("cb2", 12), ("skip", 2 * HC), ("hyn", HC), ("lb", 16), ("hgn", HEADS),
        ("nmix", DC), ("nffn", DC), ("nfin", DC), ("fb1", 1), ("fb2", 1), ("ffr", 1)]
COL = {}
NCOL = 0
for _name, _n in COLS:
    COL[_name] = (NCOL, _n)
    NCOL += _n

KA_N = 6 * 128
KG = {"perm": (0, 128), "cos": (128, 256), "sin": (384, 256), "scan": (640, 512)}
KG_N = 1152
KR = {"desc": (0, 8), "valid": (8, 3), "eio": (11, 64), "iota": (75, SLOTS)}
KR_N = 75 + SLOTS


def first_block_slabs(d):
    def cols(w, c0, n):
        return w[:, c0:c0 + n].rearrange("(c p) n -> p c n", p=P)

    out = []
    for l in range(2):
        for s in range(12):
            out.append(([(0, 512, cols(d["ada_w"][l], 512 * s, 512))], DC, 512, ("ada_mm", 12 * l + s + 1)))

    def ffn(l):
        for j in range(FC // 2):
            out.append(([(0, 256, cols(d["ffn_w_in"][l], 256 * j, 256)),
                         (256, 256, cols(d["ffn_w_in"][l], D_FF + 256 * j, 256))], DC, 512, ("ffn_in_mm", 44 * l + 4 * j + 4)))
        for m in range(DC):
            out.append(([(0, P, cols(d["ffn_w_out"][l], P * m, P))], FC, P, ("ffn_out_mm", 8 * l + m + 1)))

    def wide(w, names):
        for s, free in enumerate(names):
            out.append(([(0, 512, cols(w, 512 * s, 512))], DC, 512, free))

    wide(d["gla_w_in"], [("gla_qk_mm", 4), ("gla_qk_mm", 8), ("gla_v_mm", 4), ("gla_v_mm", 8),
                         ("gla_r_mm", 4), ("gla_r_mm", 8)])
    wide(d["gla_w_out"], [("proj_mm", 4), ("proj_mm", 8)])
    ffn(0)
    wide(d["na_w_qkv"], [("na_q_mm", 4), ("na_q_mm", 8), ("na_k_mm", 4), ("na_k_mm", 8), ("na_v_mm", 4), ("na_v_mm", 8)])
    wide(d["na_w_out"], [("proj_mm", 12), ("proj_mm", 16)])
    ffn(1)
    wide(d["w_in_2"], [("hy_mm", 4), ("hy_mm", 8), ("hy_mm", 12), ("hg_mm", 4), ("hg_mm", 8), ("hg_mm", 12),
                       ("hg_v_mm", 3), ("hg_mm", 16)])
    wide(d["w_out_2"], [("proj_mm", 20), ("proj_mm", 24)])
    return out


def build(nc, d, out):
    ctx = ExitStack()
    with ctx:
        def sb(name, shape, dt=F32):
            return ctx.enter_context(nc.sbuf_tensor("s_" + name, shape, dt))

        class Sems(dict):
            def __missing__(self, name):
                self[name] = ctx.enter_context(nc.semaphore(name))
                return self[name]

        S = Sems()
        pb = [ctx.enter_context(nc.psum_tensor(f"bank{i}", [P, 512], F32)) for i in range(8)]

        NRING = 5
        ring = sb("ring", [P, NRING, 4096])
        xT = sb("xT", [P, DC, TT])
        hT = sb("hT", [P, DC, TT])
        sq = sb("sq", [P, 2, TT])
        rstd = sb("rstd", [P, TT])
        cols = sb("cols", [P, NCOL])
        ka = sb("ka", [P, KA_N])
        ones = sb("ones", [P, 4, P])
        one1 = sb("one1", [P, P])
        eps = sb("eps", [P, 1])
        sc = sb("sc", [P, 2 * DC])
        mod = sb("mod", [P, 2, 48, 2])
        modA = sb("modA", [P, 2, 2, DC, 2])
        AW = (nc.sbuf_bytes_remaining // 4 if not callable(nc.sbuf_bytes_remaining) else nc.sbuf_bytes_remaining() // 4) - 64
        arena = sb("arena", [P, AW])

        def carve(start=0, tensor=None, limit=None):
            at = [start]
            flat = arena if tensor is None else tensor

            def take(*shape):
                n = int(np.prod(shape))
                v = flat[:, at[0]:at[0] + n]
                at[0] += n
                assert at[0] <= (limit or AW), (at[0], AW)
                if len(shape) == 2:
                    v = v.rearrange("p (a b) -> p a b", b=shape[1])
                if len(shape) == 3:
                    v = v.rearrange("p (a b c) -> p a b c", b=shape[1], c=shape[2])
                return v
            take.at = at
            return take

        def col(name, i, n=1, rows=P):
            o = COL[name][0] + i
            return cols[0:rows, o:o + n]

        ident = ka[:, 0:128]
        m_half = [ka[:, 128:256], ka[:, 384:512]]
        m_cross = [ka[:, 256:384], ka[:, 512:640]]
        striu = ka[:, 640:768]
        ON = {1024: ones[:, 0, :], 256: ones[:, 1, :], 128: ones[:, 2, :], 512: ones[:, 3, :]}

        t = carve()
        g_qk, g_v, g_S = t(8, TT), t(4, D), t(2, 8, 256)
        kg, g_low, g_aw2 = t(KG_N), t(TT), t(512)
        g_tm, g_tg, g_tb, g_e2, g_e3, g_dm, g_dk = t(TT), t(TT), t(TT), t(TT), t(2, TT), t(TT), t(TT)
        g_e5, g_att, g_sr = t(2, 8), t(2, 4 * P), t(2, TT)
        g_aw1 = g_sr.rearrange("p a b -> p (a b)")[:, 0:2 * DC * 16].rearrange("p (a b c) -> p a b c", b=DC, c=16)
        g_kdt = kg[:, 0:4 * P].rearrange("p (a b) -> p a b", b=P)
        ada_row = g_S[0:2, 0, :, :].rearrange("p a b -> p (a b)").rearrange("p (a b) -> p a b", b=512)[:, 0:2, :]
        t = carve()
        f_act, f_t1 = t(FC, TT), t(4, TT)
        t = carve()
        n_q, n_k, n_v, n_o = t(DC, NT), t(DC, TT), t(4, D), t(DC, NT)
        n_bias, n_s, n_pt = t(4, TT), t(3, TT), t(2, TT)
        n_mx, n_rs = t(3, 4), t(3, 4)
        hflat = hT[:, :, :].rearrange("p a b -> p (a b)")
        xflat = xT[:, :, :].rearrange("p a b -> p (a b)")
        zT = hflat[:, 0:DC * T2].rearrange("p (a b) -> p a b", b=T2)
        h2T = xflat[:, 0:DC * T2].rearrange("p (a b) -> p a b", b=T2)
        w_dft = hflat[:, DC * T2:DC * T2 + 3 * 2 * NF].rearrange("p (a b) -> p a b", b=2 * NF)
        w_inv = xflat[:, DC * T2:DC * T2 + 6 * T2].rearrange("p (a b) -> p a b", b=T2)
        t = carve()
        y_cat, hy_u = t(DC, T2), t(12, T2)
        b2_at = t.at[0]
        q_q, q_k, q_lf, q_g, q_v = t(HEADS, T2), t(8, T2), t(8, T2), t(HEADS, T2), t(3, HY)
        q_tm, q_tg, q_tb, q_e2, q_e3, q_dm, q_dk = t(T2), t(T2), t(T2), t(T2), t(2, T2), t(T2), t(T2)
        q_e5, q_att, q_kdt, q_S, q_scan = t(2, 8), t(2, 3 * P), t(3, P), t(2, 5, P), t(T2)
        lbv = t(16)
        t = carve(b2_at)
        spec = t(2, 6, HY)
        spec_at = t.at[0]
        win, fw3, f_hs, f_hd = t(3, 2, HY), t(4, HY), t(3, HY), t(3, HY)
        f_h, f_z, f_w12, f_k = t(T2), t(T2), t(2, HID), t(T2)
        f_b = sq[:, 0, :]
        t = carve(spec_at)
        u_tok, yf, hy_tmp = t(3, HY), t(6, HY), t(2, HY)
        slot5 = AW - 4096
        t = carve(limit=slot5)
        r_at = t.at[0]
        r_h2, r_S, r_Sg = t(3, D), t(3, SLOTS), t(3, SLOTS)
        t2 = carve(r_at, limit=slot5)
        e_xw, e_sg, e_hid = t2(2, DC, WIN), t2(2, DE), t2(2, DE)
        e_hT, e_y = t2(2, 4, WIN), t2(2, D)
        t.at[0] = max(t.at[0], t2.at[0])
        r_SgT, xg_at = t(5, T2), t.at[0]
        xg = t(DC, SLOTS + WIN)
        r_sel = t(T2)
        t3 = carve(DC * T2, tensor=xflat, limit=DC * TT)
        kr, wr = t3(KR_N), t3(DC, NG + NE)
        r_lg, r_t1, r_t2 = t(3, NG + NE), t(3, NE), t(3, NE)
        r_sm = t(40, 3)
        r_oh = t(6, 24)
        r_M = t(3, 3, NE)
        r_cnt, r_row, r_ti = t(6, NE), t(2, NE), t(2 * 72)
        y_s = carve(xg_at, limit=slot5)(5, D)

        def slot(n):
            return ring[:, n, :] if n < NRING else arena[:, slot5:slot5 + 4096]

        ysort = nc.dram_tensor("ysort", (SLOTS + 2 * WIN, D), F32, kind="Internal").ap()

        slabs = first_block_slabs(d)
        place, landed, free, owner, count = [], [], [], {}, {}
        for n, (parts, kc, w, f) in enumerate(slabs):
            s = n % NRING
            count[s] = count.get(s, 0) + 16 * len(parts)
            place.append(slot(s)[:, 0:kc * w].rearrange("p (c n) -> p c n", n=w))
            landed.append((f"slab_in{s}", count[s]))
            free.append(owner.get(s))
            owner[s] = f
        FIRST = {}
        n = 0
        for name, k in (("ada", 24), ("gla", 6), ("gla_out", 2), ("ffn0", 11), ("ffn0_out", 8), ("na", 6), ("na_out", 2),
                        ("ffn1", 11), ("ffn1_out", 8), ("in2", 8), ("out2", 2)):
            FIRST[name] = n
            n += k
        assert n == len(slabs)

        NB = NE + EXTRA
        e_slot0 = len(slabs) % NRING

        def eslot(b, part):
            i = 3 * b + part if (b == 0 and part < 2) else (3 * b - 1 + part if part < 2 else 3 * b + 4)
            return i % 6, i // 6
        e_in = [f"expert_in{i}" for i in range(6)]

        sems = S
        block = ctx.enter_context(nc.Block())

        class G:
            T, DV, m0, nc_, tail, scale, base = TT, 256, 0, 8, None, 1.0 / GATE_NORM, 0
            q = staticmethod(lambda h: g_qk[:, h, :])
            k = staticmethod(lambda h, dr: g_qk[:, 4 + h, :])
            S, tm, tg, tb, e2, e3, e5, att, kdt, dm, dk = g_S, g_tm, g_tg, g_tb, g_e2, g_e3, g_e5, g_att, g_kdt, g_dm, g_dk
            scan = kg[:, KG["scan"][0]:KG["scan"][0] + TT]
            tiles = [(128 * i, 128) for i in range(4)]
            chunks = [(CH * c, CH, c // 2, CH * (c % 2)) for c in range(8)]
            order = [[4, 5, 6, 7, 0, 1, 2, 3], [7, 6, 5, 4, 3, 2, 1, 0]]
            v = staticmethod(lambda tt, p0, n, h, e: g_v[p0:p0 + n, tt, 256 * h + 128 * e:256 * h + 128 * e + 128])
            vv = staticmethod(lambda tt, p0, n, h: g_v[p0:p0 + n, tt, 256 * h:256 * h + 256])
            o = staticmethod(lambda h, e: g_qk[:, 4 * e + h, :])
            y = staticmethod(lambda h, e: g_qk[:, 4 * e + h, :])
            gain = staticmethod(lambda h, e: col("gng", e))
            gate = staticmethod(lambda h, e: g_sr[:, e, :])

        class H:
            T, DV, m0, nc_, tail, scale, base = T2, 128, N_META, 4, (0, N_META), 1.0, 8
            q = staticmethod(lambda h: q_q[:, h, :])
            k = staticmethod(lambda h, dr: q_k[:, 4 * dr + h, :])
            S, tm, tg, tb, e2, e3, e5, att, kdt, dm, dk = q_S, q_tm, q_tg, q_tb, q_e2, q_e3, q_e5, q_att, q_kdt, q_dm, q_dk
            scan = q_scan
            tiles = [(N_META, 128), (N_META + 128, 128), (0, N_META)]
            chunks = [(N_META + CH * c, CH, c // 2, CH * (c % 2)) for c in range(4)] + [(0, N_META, 2, 0)]
            order = [[4, 0, 1, 2, 3], [3, 2, 1, 0, 4]]
            v = staticmethod(lambda tt, p0, n, h, e: q_v[p0:p0 + n, tt, 128 * h:128 * h + 128])
            vv = staticmethod(lambda tt, p0, n, h: q_v[p0:p0 + n, tt, 128 * h:128 * h + 128])
            o = staticmethod(lambda h, e: y_cat[:, 4 + h, :])
            y = staticmethod(lambda h, e: y_cat[:, 4 + h, :])
            gain = staticmethod(lambda h, e: col("hgn", h))
            gate = staticmethod(lambda h, e: q_g[:, h, :])

        NU = {G: 7, H: 4}

        def u_ahead(cf, hd):
            return (0 if cf is G else 8 * NU[G]) + hd * NU[cf]

        norms = {}
        seen = [0, 0]

        def norm_plan(name, chunks):
            norms[name] = (seen[0], seen[1])
            seen[0] += chunks
            seen[1] += 1
        norm_plan("n1_0", DC)
        for h in range(HEADS):
            norm_plan(f"gla{h}", 2)
        for name in ("n2_0", "n1_1", "n2_1", "fin", "mix"):
            norm_plan(name, DC)
        for h in range(HEADS):
            norm_plan(f"hgrn{h}", 1)
        norm_plan("hyena", HC)
        norm_plan("nffn", DC)
        norm_plan("nfin", DC)

        @block.sync
        def _(sp):
            for n, (parts, kc, w, f) in enumerate(slabs):
                if free[n]:
                    sp.wait_ge(S[free[n][0]], free[n][1])
                for o, wd, view in parts:
                    sp.dma_start(place[n][:, :, o:o + wd], view).then_inc(S[landed[n][0]], 16)

            def expert_slab(e, b, part, wait):
                s, k = eslot(b, part)
                dst = slot(s)
                src = [d["w_gate_2"], d["w_up_2"], d["w_down_2"]][part]
                if part < 2:
                    v = src[e, :, :].rearrange("(c p) n -> p c n", p=P)
                    dv = dst.rearrange("p (c n) -> p c n", n=DE)
                else:
                    v = src[e, :, :].rearrange("(c p) n -> p c n", p=P)
                    dv = dst.rearrange("p (c n) -> p c n", n=D)
                wait()
                sp.dma_start(dv, v).then_inc(S[e_in[s]], 16)

            def before_load(b, part):
                s, k = eslot(b, part)
                if k == 0:
                    if s < NRING:
                        last = max(i for i in range(len(slabs)) if i % NRING == s)
                        return lambda: sp.wait_ge(S[slabs[last][3][0]], slabs[last][3][1])
                    return lambda: sp.wait_ge(S["hyena_done"], 1)
                return None

            def used(b, part):
                i = 0 if (b, part) == (0, 0) else 1 if (b, part) == (0, 1) else (3 * b - 1 + part if part < 2 else 3 * b + 4)
                j = i - 6
                if j == 0 or j == 1:
                    return ("gu_mm", 1)
                bb, rr = divmod(j - 2, 3)
                return ("gu_mm", bb + 2) if rr < 2 else ("down_mm", bb + 1)

            def load(e, b, part):
                w = before_load(b, part)
                if w is None:
                    name, val = used(b, part)
                    w = lambda: sp.wait_ge(S[name], val)
                expert_slab(e, b, part, w)

            load(0, 0, 0)
            load(0, 0, 1)
            for b in range(2):
                load(b + 1, b + 1, 0)
                load(b + 1, b + 1, 1)
                load(b, b, 2)

            LOOPS = (NE - 4) // 2
            with sp.Fori(0, LOOPS) as i:
                for j in range(2):
                    b = 2 + j
                    for e0, part in ((b + 1, 0), (b + 1, 1), (b, 2)):
                        name, val = used(e0, part)
                        expert_slab(2 * i + e0, e0, part,
                                    lambda: sp.wait_ge(S[name], 2 * i + val))
            for b in range(2 + 2 * LOOPS, NB):
                for bb, part in ((b + 1, 0), (b + 1, 1), (b, 2)):
                    if bb >= NB:
                        continue
                    if bb == NE and part == 0:
                        sp.wait_ge(S["tables"], 1)
                    e = bb if bb < NE else sp.value_load(r_ti.bitcast(I32)[0:1, 72 + bb:73 + bb], min_val=0, max_val=NE - 1)
                    load(e, bb, part)

        @block.gpsimd
        def _(pool):
            pool.dma_start(xT[:, :, :], d["xT"].rearrange("(c p) t -> p c t", p=P)).then_inc(S["x_in"], 16)
            for i, n in enumerate((1024, 256, 128, 512)):
                pool.memset(ones[:, i, :], 1.0 / n).then_inc(S["ones_set"], 1)
            pool.memset(one1[:, :], 1.0).then_inc(S["ones_set"], 1)
            pool.memset(eps[:, :], EPS).then_inc(S["ones_set"], 1)
            pool.wait_ge(S["ffn_out_x"], 2 * DC)
            pool.memset(n_bias[:, :, :], 0.0).then_inc(S["zeroed"], 1)
            pool.wait_ge(S["zeroed"], 1)
            for i in range(2 * NA_H):
                if i >= 4:
                    pool.wait_ge(S["na_add"], i - 3)
                pool.dma_start(n_bias[:, i % 4, 0:NT], d["na_bias"][i // 2, i % 2]).then_inc(S[f"na_bias_in{i % 4}"], 16)
            pool.wait_ge(S["ffn_out_x"], 3 * DC)
            pool.dma_start(q_scan, d["k_scan2"]).then_inc(S["b2_in"], 16)
            pool.wait_ge(S["fin_h"], DC)
            pool.dma_start(zT[:, :, 0:N_META], d["metaT"].rearrange("(c p) t -> p c t", p=P)).then_inc(S["meta_in"], 16)
            for i, (t0, n) in enumerate(TTILE):
                pool.dma_start(w_dft[0:n, i, :], d["k_dft"][t0:t0 + n, :]).then_inc(S["dft_in"], 16)
            for i in range(6):
                f0, n = FT[i % 3]
                pool.dma_start(w_inv[0:n, i, :], d["k_idft"][(i // 3) * NF + f0:(i // 3) * NF + f0 + n, :]).then_inc(S["dft_in"], 16)
            pool.wait_ge(S["gate_y"], 8 + 4)
            for i, (t0, n) in enumerate(TTILE):
                pool.dma_start(win[0:n, i, :, :], d["k_win"][t0:t0 + n, :, :]).then_inc(S["filt_in"], 16)
            pool.dma_start(fw3[0:HID, :, :], d["filt_w3_2"].rearrange("p (a n) -> p a n", n=HY)).then_inc(S["filt_in"], 16)
            pool.dma_start(f_z[0:EMB, :], d["k_zT"]).then_inc(S["filt_in"], 16)
            pool.dma_start(f_w12[0:EMB, 0, :], d["filt_w1_2"]).then_inc(S["filt_in"], 16)
            pool.dma_start(f_w12[0:HID, 1, :], d["filt_w2_2"]).then_inc(S["filt_in"], 16)
            pool.wait_ge(S["proj_x"], 4 * DC)
            pool.dma_start(kr, d["k_route"]).then_inc(S["route_in"], 16)
            pool.dma_start(wr, d["w_route"].rearrange("(c p) n -> p c n", p=P)).then_inc(S["route_in"], 16)
            pool.memset(xg[:, :, SLOTS:SLOTS + WIN], 0.0).then_inc(S["zeroed"], 1)
            pool.memset(r_lg, 0.0).then_inc(S["zeroed"], 1)

        @block.tensor
        def _(pe):
            mm = pe.matmul

            def got(n):
                pe.wait_ge(S[landed[n][0]], landed[n][1])
                return place[n]

            def norm_sum(name, chunks, bank, T, n):
                q0, i = norms[name]
                for c in range(chunks):
                    pe.wait_ge(S["sq_ready"], q0 + c + 1)
                    mm(pb[bank][:, 0:T], ON[n], sq[:, (q0 + c) % 2, 0:T], start=c == 0, stop=c == chunks - 1)\
                        .then_inc(S["sq_used"], 1)

            def ffn(l, T):
                n0 = FIRST[f"ffn{l}"]
                pe.wait_ge(S["mod_h"], DC * (2 * l + 2))
                for j in range(FC // 2):
                    w = got(n0 + j)
                    for u in range(4):
                        i = 4 * j + u
                        if i >= 8:
                            if u % 2 == 0:
                                pe.wait_ge(S["ffn_conv"], 22 * l + (i - 8) // 2 + 1)
                            else:
                                pe.wait_ge(S["ffn_act"], 22 * l + (i - 8) // 2 + 1)
                        o = 128 * (u // 2) + 256 * (u % 2)
                        for c in range(DC):
                            last = mm(pb[i % 8][:, 0:T], w[:, c, o:o + 128], hT[:, c, 0:T], start=c == 0, stop=c == DC - 1)
                        last.then_inc(S["ffn_in_mm"], 1)
                pe.wait_ge(S["ffn_act"], 22 * l + FC)
                halves = 2 if T == TT else 1
                for m in range(DC):
                    w = got(FIRST[f"ffn{l}_out"] + m)
                    if m >= 4:
                        pe.wait_ge(S["ffn_out_x"], 16 * l + halves * (m - 3))
                    for c in range(FC):
                        last = mm(pb[m % 4][:, 0:T], w[:, c, :], f_act[:, c, 0:T], start=c == 0, stop=c == FC - 1)
                    last.then_inc(S["ffn_out_mm"], 1)

            def project(slab, src, T, ahead, per):
                for m in range(DC):
                    w = got(FIRST[slab] + m // 4)
                    if m >= 4:
                        pe.wait_ge(S["proj_x"], ahead + per * (m - 3))
                    for c in range(DC):
                        last = mm(pb[m % 4][:, 0:T], w[:, c, 128 * (m % 4):128 * (m % 4) + 128], src(c),
                                  start=c == 0, stop=c == DC - 1)
                    last.then_inc(S["proj_mm"], 1)

            pe.wait_ge(S["ka_in"], 16)
            pe.wait_ge(S["sc_ready"], 1)

            def ada_turn(g):
                pe.wait_ge(S["ada_row"], g + 1)
                for j in range(4):
                    o = (4 * (g % 12) + j) * 2
                    last = pe.transpose(pb[2 + g // 12][:, o:o + 2], ada_row[:, g % 2, 128 * j:128 * j + 128], ident[0:2, 0:2])
                last.then_inc(S["ada_tr"], 1)
            for g in range(24):
                w = got(FIRST["ada"] + g)
                if g >= 2:
                    pe.wait_ge(S["ada_row"], g - 1)
                for c in range(DC):
                    last = mm(pb[g % 2][0:2, :], sc[:, 2 * c:2 * c + 2], w[:, c, :], start=c == 0, stop=c == DC - 1)
                last.then_inc(S["ada_mm"], 1)
                if g >= 1:
                    ada_turn(g - 1)
            ada_turn(23)

            pe.wait_ge(S["ones_set"], 6)
            norm_sum("n1_0", DC, 4, TT, 1024)
            pe.wait_ge(S["mod_h"], DC)
            pe.wait_ge(S["mod_ready"], 2)

            def rope_turn(u):
                pe.wait_ge(S["gla_qk_ev"], u + 1)
                if u >= 2:
                    pe.wait_ge(S["rope_s"], u - 1)
                mm(pb[4 + u % 2][:, 0:NT], kg[:, 0:128], g_qk[:, u, 0:NT], start=True, stop=True).then_inc(S["rope_mm"], 1)
            pe.wait_ge(S["gla_in"], 80)
            for u in range(8):
                w = got(FIRST["gla"] + u // 4)
                if u >= 4:
                    pe.wait_ge(S["gla_qk_ev"], u - 3)
                for c in range(DC):
                    last = mm(pb[u % 4][:, :], w[:, c, 128 * (u % 4):128 * (u % 4) + 128], hT[:, c, :], start=c == 0, stop=c == DC - 1)
                last.then_inc(S["gla_qk_mm"], 1)
                if u >= 1:
                    rope_turn(u - 1)
            rope_turn(7)
            pe.wait_ge(S["gla_qk_ev"], 8)
            for u in range(8):
                w = got(FIRST["gla"] + 2 + u // 4)
                if u >= 4:
                    pe.wait_ge(S["gla_v_ev"], u - 3)
                for c in range(DC):
                    last = mm(pb[u % 4][:, :], hT[:, c, 128 * (u % 4):128 * (u % 4) + 128], w[:, c, :], start=c == 0, stop=c == DC - 1)
                last.then_inc(S["gla_v_mm"], 1)
            pe.wait_ge(S["rope_s"], 8)
            for dr in range(2):
                for c in range(DC):
                    last = mm(pb[6 + dr][32 * dr:32 * dr + 16, :], g_aw1[:, dr, c, :], hT[:, c, :], start=c == 0, stop=c == DC - 1)
                last.then_inc(S["low_mm"], 1)
            pe.wait_ge(S["low_ev"], 2)
            pe.wait_ge(S["gla_v_ev"], 8)

            def gate_logits(hd):
                h, dr = hd // 2, hd % 2
                if hd >= 1:
                    pe.wait_ge(S["gl_min"], hd)
                mm(pb[0][:, :], g_aw2[32 * dr:32 * dr + 16, 128 * h:128 * h + 128], g_low[32 * dr:32 * dr + 16, :], start=True, stop=True)\
                    .then_inc(S["gl_mm"], 1)

            def scan_head(cf, hd):
                h, dr = hd // 2, hd % 2
                n = cf.base + hd
                pe.wait_ge(S["decayed"], 6 * (n + 1))
                if n >= 1:
                    pe.wait_ge(S["att_cp"], n)
                for tt, (t0, m) in enumerate(cf.tiles):
                    last = mm(pb[2][0:m, P * tt:P * tt + m], cf.e2[:, t0:t0 + m], cf.tg[:, t0:t0 + m], start=True, stop=True)
                for tt, (t0, m) in enumerate(cf.tiles[:cf.nc_ // 2]):
                    last = mm(pb[7][0:m, P * tt:P * tt + m], cf.dk[:, t0:t0 + m], cf.dm[:, t0:t0 + m], start=True, stop=True)
                last.then_inc(S["att_mm"], 1)
                if n >= 1:
                    pe.wait_ge(S["kd_cp"], n)
                for i, (t0, m) in enumerate(cf.tiles):
                    last = pe.transpose(pb[3][0:m, 128 * i:128 * i + 128], cf.tm[:, t0:t0 + m], ident)
                last.then_inc(S["kd_tr"], 1)

            def scan_updates(cf, hd):
                h, dr = hd // 2, hd % 2
                pe.wait_ge(S["kd_cp"], cf.base + hd + 1)
                for i, c in enumerate(cf.order[dr][:-1]):
                    _, m, tt, p0 = cf.chunks[c]
                    u = u_ahead(cf, hd) + i
                    if u >= 2:
                        pe.wait_ge(S["state"], u - 1)
                    mm(pb[4 + u % 2][:, 0:cf.DV], cf.kdt[p0:p0 + m, tt, :], cf.vv(tt, p0, m, h), start=True, stop=True)\
                        .then_inc(S["u_mm"], 1)

            def scan_out(cf, h):
                pe.wait_ge(S["att_cp"], cf.base + 2 * h + 2)
                pe.wait_ge(S["state"], u_ahead(cf, 2 * h + 2))
                no = h if cf is G else HEADS + h
                for e in range(cf.DV // 128):
                    if no >= 1 and e == 0:
                        pe.wait_ge(S["o_ev"], 2 * h if cf is G else 8 + h)
                    for tt, (t0, tn) in enumerate(cf.tiles):
                        terms = [(t0, tn, cf.v(tt, 0, tn, h, e), cf.att[0:tn, dr, P * tt:P * tt + tn]) for dr in range(2)]
                        for ci, (c0, m, ct, _) in enumerate(cf.chunks):
                            for dr in range(2):
                                if ct == tt and ci != cf.order[dr][0]:
                                    terms.append((c0, m, cf.S[:, dr, ci, 128 * e:128 * e + 128], cf.e3[:, dr, c0:c0 + m]))
                        for i, (c0, m, l, r) in enumerate(terms):
                            last = mm(pb[6 + e][:, c0:c0 + m], l, r, start=i == 0, stop=i == len(terms) - 1, skip_group_check=True)
                last.then_inc(S["o_mm"], 1)

            gate_logits(0)
            for hd in range(8):
                scan_head(G, hd)
                if hd < 7:
                    gate_logits(hd + 1)
                if hd >= 1:
                    pe.wait_ge(S["gla_r_ev"], hd)
                w = got(FIRST["gla"] + 4 + hd // 4)
                for c in range(DC):
                    last = mm(pb[1][:, :], w[:, c, 128 * (hd % 4):128 * (hd % 4) + 128], hT[:, c, :], start=c == 0, stop=c == DC - 1)
                last.then_inc(S["gla_r_mm"], 1)
                scan_updates(G, hd)
                if hd % 2:
                    scan_out(G, hd // 2)
                    if hd < 7:
                        pe.wait_ge(S["att_cp"], hd + 1)
                    pe.wait_ge(S["kd_cp"], hd + 1)
                    norm_sum(f"gla{hd // 2}", 2, 3, TT, 256)
                    pe.wait_ge(S["rs_sqrt"], norms[f"gla{hd // 2}"][1] + 1)
            pe.wait_ge(S["gate_y"], 8)
            project("gla_out", lambda k: g_qk[:, 4 * (k % 2) + k // 2, :], TT, 0, 2)
            pe.wait_ge(S["proj_x"], 2 * DC)
            norm_sum("n2_0", DC, 7, TT, 1024)
            pe.wait_ge(S["rs_sqrt"], norms["n2_0"][1] + 1)
            ffn(0, TT)

            norm_sum("n1_1", DC, 7, TT, 1024)
            pe.wait_ge(S["rs_sqrt"], norms["n1_1"][1] + 1)
            pe.wait_ge(S["mod_h"], 3 * DC)
            pe.wait_ge(S["ffn_out_x"], 2 * DC)
            for part, (name, T) in enumerate((("na_q", NT), ("na_k", TT))):
                for u in range(8):
                    w = got(FIRST["na"] + 2 * part + u // 4)
                    if u >= 4:
                        pe.wait_ge(S[name + "_ev"], u - 3)
                    elif part:
                        pe.wait_ge(S["na_q_ev"], u + 5)
                    for c in range(DC):
                        last = mm(pb[u % 4][:, 0:T], w[:, c, 128 * (u % 4):128 * (u % 4) + 128], hT[:, c, 0:T], start=c == 0, stop=c == DC - 1)
                    last.then_inc(S[name + "_mm"], 1)
            for u in range(8):
                w = got(FIRST["na"] + 4 + u // 4)
                if u >= 4:
                    pe.wait_ge(S["na_v_ev"], u - 3)
                else:
                    pe.wait_ge(S["na_k_ev"], u + 5)
                for c in range(DC):
                    last = mm(pb[u % 4][:, :], hT[:, c, 128 * (u % 4):128 * (u % 4) + 128], w[:, c, :], start=c == 0, stop=c == DC - 1)
                last.then_inc(S["na_v_mm"], 1)
            pe.wait_ge(S["na_v_ev"], 8)

            def na_scores(i):
                h, qt = i // 2, i % 2
                p0 = 64 * (h % 2)
                if i >= 2:
                    pe.wait_ge(S["na_add"], i - 1)
                mm(pb[i % 2][:, :], n_q[p0:p0 + 64, h // 2, 128 * qt:128 * qt + 128], n_k[p0:p0 + 64, h // 2, :], start=True, stop=True)\
                    .then_inc(S["na_s_mm"], 1)
            na_scores(0)
            for i in range(2 * NA_H):
                h, qt = i // 2, i % 2
                if i + 1 < 2 * NA_H:
                    na_scores(i + 1)
                pe.wait_ge(S["na_p"], i + 1)
                if i >= 2:
                    pe.wait_ge(S["na_pt"], i - 1)
                for k in range(4):
                    last = pe.transpose(pb[2 + i % 2][:, 128 * k:128 * k + 128], n_s[:, i % 3, 128 * k:128 * k + 128], ident)
                last.then_inc(S["na_tr"], 1)
                pe.wait_ge(S["na_pt"], i + 1)
                if i >= 2:
                    pe.wait_ge(S["na_o_ev"], i - 1)
                p0 = 64 * (h % 2)
                for k in range(4):
                    last = mm(pb[4 + i % 2][p0:p0 + 64, 0:128], n_v[:, k, 64 * h:64 * h + 64], n_pt[:, i % 2, 128 * k:128 * k + 128], start=k == 0, stop=k == 3)
                last.then_inc(S["na_o_mm"], 1)
            pe.wait_ge(S["na_o_ev"], 2 * NA_H)
            project("na_out", lambda k: n_o[:, k, :], NT, 2 * DC, 1)
            pe.wait_ge(S["proj_x"], 3 * DC)
            norm_sum("n2_1", DC, 7, NT, 1024)
            pe.wait_ge(S["rs_sqrt"], norms["n2_1"][1] + 1)
            ffn(1, NT)

            pe.wait_ge(S["ffn_out_x"], 3 * DC)
            norm_sum("fin", DC, 7, NT, 1024)
            pe.wait_ge(S["rs_sqrt"], norms["fin"][1] + 1)
            norm_sum("mix", DC, 7, T2, 1024)
            pe.wait_ge(S["rs_sqrt"], norms["mix"][1] + 1)
            pe.wait_ge(S["mix_h"], DC)

            def in2(slab, units, name, ev, prev, ahead=0):
                for u in range(units):
                    w = got(FIRST["in2"] + slab + u // 4)
                    if u >= 4:
                        pe.wait_ge(S[ev], ahead + u - 3)
                    elif prev:
                        pe.wait_ge(S[prev[0]], prev[1] - 3 + u)
                    for c in range(DC):
                        last = mm(pb[u % 4][:, 0:T2], w[:, c, 128 * (u % 4):128 * (u % 4) + 128], h2T[:, c, :], start=c == 0, stop=c == DC - 1)
                    last.then_inc(S[name], 1)
            in2(0, 12, "hy_mm", "hy_conv", None)
            in2(3, 4, "hg_mm", "hg_ev", ("hy_conv", 12))
            in2(4, 8, "hg_mm", "hg_ev", ("hg_ev", 4), 4)
            pe.wait_ge(S["hg_ev"], 12)
            w = got(FIRST["in2"] + 6)
            for u, (t0, m) in enumerate(H.tiles):
                for c in range(DC):
                    last = mm(pb[u][0:m, :], h2T[:, c, t0:t0 + m], w[:, c, :], start=c == 0, stop=c == DC - 1)
                last.then_inc(S["hg_v_mm"], 1)
            pe.wait_ge(S["hg_v_ev"], 3)
            in2(7, 4, "hg_mm", "hg_ev", None, 12)
            pe.wait_ge(S["hg_ev"], 16)
            for hd in range(8):
                scan_head(H, hd)
                scan_updates(H, hd)
                if hd % 2:
                    scan_out(H, hd // 2)
                    norm_sum(f"hgrn{hd // 2}", 1, 7, T2, 128)
                    pe.wait_ge(S["rs_sqrt"], norms[f"hgrn{hd // 2}"][1] + 1)

            pe.wait_ge(S["filt_in"], 7 * 16)
            pe.wait_ge(S["att_cp"], 16)
            mm(pb[0][0:HID, 0:T2], f_w12[0:EMB, 0, :], f_z[0:EMB, :], start=True, stop=True).then_inc(S["filt_mm"], 1)
            pe.wait_ge(S["filt_sin"], 1)
            mm(pb[1][0:HID, 0:T2], f_w12[0:HID, 1, :], f_h[0:HID, :], start=True, stop=True).then_inc(S["filt_mm"], 1)
            pe.wait_ge(S["filt_sin"], 2)
            pe.wait_ge(S["dft_in"], 9 * 16)
            for od in range(2):
                for i, (t0, n) in enumerate(TTILE):
                    g = 3 * od + i
                    if g >= 1:
                        pe.wait_ge(S["filt_hd"], g)
                    for dr in range(2):
                        last = mm(pb[2 + dr][0:n, :], f_h[0:HID, t0:t0 + n], fw3[0:HID, 2 * dr + od, :], start=True, stop=True)
                    last.then_inc(S["filt3_mm"], 1)
                pe.wait_ge(S["filt_hd"], 3 * od + 3)
                for i in range(6):
                    f0, m = FT[i % 3]
                    src = f_hs if i < 3 else f_hd
                    g = 6 * od + i
                    if g >= 2:
                        pe.wait_ge(S["spec_ev"], g - 1)
                    for k, (t0, n) in enumerate(TTILE):
                        last = mm(pb[4 + g % 2][0:m, :], w_dft[0:n, k, (i // 3) * NF + f0:(i // 3) * NF + f0 + m], src[0:n, k, :], start=k == 0, stop=k == 2)
                    last.then_inc(S["spec_mm"], 1)
            pe.wait_ge(S["spec_ev"], 12)
            for od in range(2):
                if od:
                    pe.wait_ge(S["hy_z"], HC)
                for i, (t0, n) in enumerate(TTILE):
                    for c in range(HC):
                        last = pe.transpose(pb[i][0:n, 128 * c:128 * c + 128], hy_u[:, c, t0:t0 + n], ident)
                    last.then_inc(S["u_tr"], 1)
                for i in range(3):
                    f0, m = FT[i]
                    pe.wait_ge(S["u_cp"], 3 * od + 3)
                    for ri in range(2):
                        b = 3 + 2 * (i % 2) + ri
                        g = 3 * od + i
                        if i == 2 or od:
                            pe.wait_ge(S["yf"], 3 * od + (i - 1 if i == 2 else 0))
                        for k, (t0, n) in enumerate(TTILE):
                            last = mm(pb[b][0:m, :], w_dft[0:n, k, ri * NF + f0:ri * NF + f0 + m], u_tok[0:n, k, :], start=k == 0, stop=k == 2)
                    last.then_inc(S["dft_mm"], 1)
                pe.wait_ge(S["yf"], 3 * od + 3)
                for c in range(HC):
                    for i in range(6):
                        f0, m = FT[i % 3]
                        last = mm(pb[c][:, 0:T2], yf[0:m, i, 128 * c:128 * c + 128], w_inv[0:m, i, :], start=i == 0, stop=i == 5)
                    last.then_inc(S["idft_mm"], 1)
            pe.wait_ge(S["hy_z"], 2 * HC)
            norm_sum("hyena", HC, 7, T2, 512)
            pe.wait_ge(S["rs_sqrt"], norms["hyena"][1] + 1)
            pe.wait_ge(S["hyena_y"], HC)
            project("out2", lambda k: y_cat[:, k, :], T2, 3 * DC, 1)
            pe.wait_ge(S["proj_x"], 4 * DC)

            norm_sum("nffn", DC, 7, T2, 1024)
            pe.wait_ge(S["rs_sqrt"], norms["nffn"][1] + 1)
            pe.wait_ge(S["nffn_h"], DC)
            for i, (t0, n) in enumerate(TTILE):
                for hf in range(2):
                    for c in range(4):
                        last = pe.transpose(pb[2 * i + hf][0:n, 128 * c:128 * c + 128], h2T[:, 4 * hf + c, t0:t0 + n], ident)
                    last.then_inc(S["h2_tr"], 1)
            pe.wait_ge(S["route_in"], 32)
            for i, (t0, n) in enumerate(TTILE):
                for c in range(DC):
                    last = mm(pb[7][0:n, 72 * i:72 * i + 72], h2T[:, c, t0:t0 + n], wr[:, c, :], start=c == 0, stop=c == DC - 1)
            last.then_inc(S["route_mm"], 1)
            pe.wait_ge(S["route_M"], 1)
            pe.wait_ge(S["h2_cp"], 6)
            for i in range(3):
                for j in range(i + 1):
                    last = mm(pb[6][:, 64 * i:64 * i + 64], striu if j == i else one1[:, :], r_M[:, 2, j, :], start=j == 0, stop=j == i)
            for j in range(3):
                last = mm(pb[6][:, 192:256], one1[:, :], r_M[:, 2, j, :], start=j == 0, stop=j == 2)
            last.then_inc(S["pos_mm"], 1)
            pe.wait_ge(S["route_S"], 1)
            for c in range(DC):
                for hf in range(2):
                    g = 2 * c + hf
                    if g >= 4:
                        pe.wait_ge(S["xg_ev"], g - 3)
                    for k, (t0, n) in enumerate(TTILE):
                        last = mm(pb[g % 4][:, 0:T2], r_h2[0:n, k, 128 * c:128 * c + 128], r_S[0:n, k, T2 * hf:T2 * hf + T2], start=k == 0, stop=k == 2)
                    last.then_inc(S["xg_mm"], 1)
            pe.wait_ge(S["route_S"], 2)
            for s, (s0, m) in enumerate(STILE):
                if s >= 2:
                    pe.wait_ge(S["sgt_ev"], s - 1)
                for k, (t0, n) in enumerate(TTILE):
                    last = pe.transpose(pb[4 + s % 2][0:m, t0:t0 + n], r_Sg[0:n, k, s0:s0 + m], ident[0:n, 0:n])
                last.then_inc(S["sgt_tr"], 1)
            pe.wait_ge(S["xg_ev"], 16)
            pe.wait_ge(S["sgt_ev"], 5)

            def arrived(b, part, k):
                s, k0 = eslot(b, part)
                pe.wait_ge(S[e_in[s]], 16 * k + 16 * (k0 + 1))
                return slot(s)

            def gate_up(b, j, k, i=0):
                pe.wait_ge(S["xw"], i + b + 1)
                for part in range(2):
                    w = arrived(b, part, k).rearrange("p (c n) -> p c n", n=DE)
                    if b >= 2:
                        pe.wait_ge(S["hid"], i + b - 1)
                    for c in range(DC):
                        last = mm(pb[2 * j + part][:, :], e_xw[:, j, c, :], w[:, c, :], start=c == 0, stop=c == DC - 1)
                last.then_inc(S["gu_mm"], 1)

            def turn(b, j, i=0):
                pe.wait_ge(S["hid"], i + b + 1)
                if b >= 1:
                    pe.wait_ge(S["hT_cp"], i + b)
                for c in range(4):
                    last = pe.transpose(pb[4][:, 128 * c:128 * c + 128], e_hid[:, j, 128 * c:128 * c + 128], ident)
                last.then_inc(S["hid_tr"], 1)

            def down(b, j, k, i=0):
                w = arrived(b, 2, k).rearrange("p (c n) -> p c n", n=D)
                pe.wait_ge(S["hT_cp"], i + b + 1)
                if b >= 1:
                    pe.wait_ge(S["y_cp"], i + b)
                for hf in range(2):
                    for c in range(4):
                        last = mm(pb[5 + hf][:, :], e_hT[:, j, c, :], w[:, c, 512 * hf:512 * hf + 512], start=c == 0, stop=c == 3)
                last.then_inc(S["down_mm"], 1)
            gate_up(0, 0, 0)
            for b in range(2):
                turn(b, b % 2)
                gate_up(b + 1, (b + 1) % 2, 0)
                down(b, b % 2, 0)
            LOOPS = (NE - 4) // 2
            with pe.Fori(0, LOOPS) as i:
                for b in (2, 3):
                    turn(b, b % 2, 2 * i)
                    gate_up(b + 1, (b + 1) % 2, i, 2 * i)
                    down(b, b % 2, i, 2 * i)
            for b in range(2 + 2 * LOOPS, NB):
                turn(b, b % 2)
                if b + 1 < NB:
                    gate_up(b + 1, (b + 1) % 2, 0)
                down(b, b % 2, 0)
            pe.wait_ge(S["ys_in"], 5 * 16)
            pe.wait_ge(S["y_cp"], NB)
            for m in range(DC):
                if m >= 4:
                    pe.wait_ge(S["moe_x"], m - 3)
                for s, (s0, n) in enumerate(STILE):
                    last = mm(pb[m % 4][:, 0:T2], y_s[0:n, s, 128 * m:128 * m + 128], r_SgT[0:n, s, :], start=s == 0, stop=s == len(STILE) - 1)
                last.then_inc(S["comb_mm"], 1)
            pe.wait_ge(S["moe_x"], DC)
            norm_sum("nfin", DC, 7, T2, 1024)

        @block.scalar
        def _(act):
            A = act.activation
            act.dma_start(cols[:, :], d["cols"]).then_inc(S["cols_in"], 16)
            act.dma_start(ka[:, :], d["k_a"]).then_inc(S["ka_in"], 16)
            act.dma_start(kg, d["k_g"]).then_inc(S["gla_in"], 16)
            act.dma_start(g_aw1[:, 0, :, :], d["gla_a_w1"][0].rearrange("(c p) n -> p c n", p=P)).then_inc(S["gla_in"], 16)
            act.dma_start(g_aw1[:, 1, :, :], d["gla_a_w1"][1].rearrange("(c p) n -> p c n", p=P)).then_inc(S["gla_in"], 16)
            for dr in range(2):
                act.dma_start(g_aw2[32 * dr:32 * dr + 16, :], d["gla_a_w2"][dr]).then_inc(S["gla_in"], 16)
            act.wait_ge(S["cols_in"], 16)
            A(sc[:, :], col("c2", 0, 2 * DC), ACT.Silu).then_inc(S["sc_ready"], 1)

            def copies(n, mmsem, evsem, bank, dst, func=ACT.Copy, scale=None, ahead=0):
                for u in range(n):
                    act.wait_ge(S[mmsem], ahead + u + 1)
                    o = dst(u)
                    b = bank(u)
                    A(o, b, func, **({} if scale is None else {"scale": scale(u)})).then_inc(S[evsem], 1)

            def squares(name, chunks, src):
                q0, _ = norms[name]
                for c in range(chunks):
                    if q0 + c >= 2:
                        act.wait_ge(S["sq_used"], q0 + c - 1)
                    s = src(c)
                    A(sq[:, (q0 + c) % 2, 0:s.shape[1]], s, ACT.Square).then_inc(S["sq_ready"], 1)

            def sqrt(name, chunks, bank, T):
                q0, i = norms[name]
                act.wait_ge(S["ones_set"], 6)
                act.wait_ge(S["sq_used"], q0 + chunks)
                if i >= 1:
                    act.wait_ge(S["norm_done"], i)
                A(rstd[:, 0:T], pb[bank][:, 0:T], ACT.Sqrt, bias=eps[:, 0:1]).then_inc(S["rs_sqrt"], 1)

            def modulate(name, l, which, T):
                for c in range(DC):
                    act.wait_ge(S["mod_xr"], DC * (2 * l + which) + c + 1)
                    for hf in range(T // NT):
                        v = hT[:, c, NT * hf:NT * hf + NT]
                        last = A(v, v, ACT.Identity, bias=mod[:, l, 24 * which + c, hf:hf + 1], scale=modA[:, l, which, c, hf:hf + 1])
                    last.then_inc(S["mod_h"], 1)

            def ffn(l, T):
                for i in range(FC):
                    j, u = i // 2, i % 2
                    act.wait_ge(S["ffn_in_mm"], 44 * l + 4 * j + 2 * u + 1)
                    if i >= 4:
                        act.wait_ge(S["ffn_act"], 22 * l + i - 3)
                    A(f_t1[:, i % 4, 0:T], pb[(4 * j + 2 * u) % 8][:, 0:T], ACT.Identity, bias=col("fcb", FC * l + i),
                      scale=col("fcw", (3 * l + 1) * FC + i)).then_inc(S["ffn_mid"], 1)
                    act.wait_ge(S["ffn_conv"], 22 * l + i + 1)
                    A(f_t1[:, i % 4, 0:T], f_t1[:, i % 4, 0:T], ACT.Silu).then_inc(S["ffn_silu"], 1)

            for g in range(24):
                act.wait_ge(S["ada_mm"], g + 1)
                if g >= 2:
                    act.wait_ge(S["ada_tr"], g - 1)
                A(ada_row[:, g % 2, :], pb[g % 2][0:2, :], ACT.Copy).then_inc(S["ada_row"], 1)
            act.wait_ge(S["x_in"], 16)
            squares("n1_0", DC, lambda c: xT[:, c, :])
            sqrt("n1_0", DC, 4, TT)
            act.wait_ge(S["mod_ready"], 2)
            modulate("n1_0", 0, 0, TT)
            copies(8, "gla_qk_mm", "gla_qk_ev", lambda u: pb[u % 4][:, :], lambda u: g_qk[:, u, :], scale=lambda u: 128.0 ** -0.5 if u < 4 else 1.0)
            copies(8, "gla_v_mm", "gla_v_ev", lambda u: pb[u % 4][:, :], lambda u: g_v[:, u % 4, 512 * (u // 4):512 * (u // 4) + 512])
            copies(2, "low_mm", "low_ev", lambda u: pb[6 + u][32 * u:32 * u + 16, :], lambda u: g_low[32 * u:32 * u + 16, :])

            def gate_log(hd):
                h, dr = hd // 2, hd % 2
                act.wait_ge(S["gl_mm"], hd + 1)
                if hd >= 1:
                    act.wait_ge(S["att_mm"], hd)
                A(g_e2, pb[0][:, :], ACT.Abs, bias=col("gab", HEADS * dr + h)).then_inc(S["gl_abs"], 1)
                act.wait_ge(S["gl_abs"], hd + 1)
                A(g_e2, g_e2, ACT.Exp, scale=-1.0).then_inc(S["gl_exp"], 1)
                act.wait_ge(S["gl_exp"], hd + 1)
                A(g_e2, g_e2, ACT.Ln, bias=one1[:, 0:1]).then_inc(S["gl_ln"], 1)

            def decays(cf, hd):
                h, dr = hd // 2, hd % 2
                n = cf.base + hd
                act.wait_ge(S["cum"], n + 1)
                if cf is H and hd >= 1:
                    act.wait_ge(S["att_mm"], n)
                A(cf.e2, cf.tg, ACT.Exp, scale=-cf.scale).then_inc(S["decay"], 1)
                A(cf.tg, cf.tg, ACT.Exp, scale=cf.scale).then_inc(S["decay"], 1)
                a, b = cf.m0, cf.m0 + cf.nc_ * CH
                A(cf.dk[:, a:b], cf.dm[:, a:b], ACT.Exp, scale=-cf.scale).then_inc(S["decay"], 1)
                A(cf.dm[:, a:b], cf.dm[:, a:b], ACT.Exp, scale=cf.scale).then_inc(S["decay"], 1)
                if hd >= 2:
                    act.wait_ge(S["o_mm"], n // 2)
                A(cf.e3[:, dr, :], cf.tb, ACT.Exp, scale=cf.scale).then_inc(S["decay"], 1)
                A(cf.tm, cf.tm, ACT.Exp, scale=cf.scale).then_inc(S["decay"], 1)
                v = cf.tb[:, cf.m0:cf.m0 + cf.nc_ * CH].rearrange("p (c n) -> p c n", n=CH)
                if cf.tail:
                    e = cf.tail[1] - 1 if dr == 0 else 0
                    A(cf.e5[:, dr, cf.nc_:cf.nc_ + 1], cf.tb[:, e:e + 1], ACT.Exp, scale=cf.scale)
                A(cf.e5[:, dr, 0:cf.nc_], v[:, :, CH - 1 if dr == 0 else 0], ACT.Exp, scale=cf.scale).then_inc(S["decay"], 1)

            def keys_turned(cf, hd):
                n = cf.base + hd
                act.wait_ge(S["kd_tr"], n + 1)
                if hd >= 1:
                    act.wait_ge(S["u_mm"], u_ahead(cf, hd))
                for i, (t0, m) in enumerate(cf.tiles):
                    last = A(cf.kdt[0:m, i, :], pb[3][0:m, 128 * i:128 * i + 128], ACT.Copy)
                last.then_inc(S["kd_cp"], 1)

            def scan_read(cf, h):
                no = h if cf is G else HEADS + h
                act.wait_ge(S["o_mm"], no + 1)
                for e in range(cf.DV // 128):
                    A(cf.o(h, e), pb[6 + e][:, 0:cf.T], ACT.Copy).then_inc(S["o_ev"], 1)
                act.wait_ge(S["o_ev"], 2 * h + 2 if cf is G else 8 + h + 1)

            gate_log(0)
            for hd in range(8):
                decays(G, hd)
                keys_turned(G, hd)
                if hd < 7:
                    gate_log(hd + 1)
                act.wait_ge(S["gla_r_mm"], hd + 1)
                if hd >= 2:
                    act.wait_ge(S["gate_y"], 2 * (hd // 2))
                A(g_sr[:, hd % 2, :], pb[1][:, :], ACT.Silu).then_inc(S["gla_r_ev"], 1)
                if hd % 2:
                    scan_read(G, hd // 2)
                    squares(f"gla{hd // 2}", 2, lambda e: G.o(hd // 2, e))
                    sqrt(f"gla{hd // 2}", 2, 3, TT)
            act.wait_ge(S["proj_x"], 2 * DC)
            squares("n2_0", DC, lambda c: xT[:, c, :])
            sqrt("n2_0", DC, 7, TT)
            modulate("n2_0", 0, 1, TT)
            ffn(0, TT)
            act.wait_ge(S["ffn_out_x"], 2 * DC)
            squares("n1_1", DC, lambda c: xT[:, c, :])
            sqrt("n1_1", DC, 7, TT)
            modulate("n1_1", 1, 0, TT)
            copies(8, "na_q_mm", "na_q_ev", lambda u: pb[u % 4][:, 0:NT], lambda u: n_q[:, u, :], scale=lambda u: 64.0 ** -0.5)
            copies(8, "na_k_mm", "na_k_ev", lambda u: pb[u % 4][:, :], lambda u: n_k[:, u, :])
            copies(8, "na_v_mm", "na_v_ev", lambda u: pb[u % 4][:, :], lambda u: n_v[:, u % 4, 512 * (u // 4):512 * (u // 4) + 512])

            def na_exp(i):
                act.wait_ge(S["na_max"], i + 1)
                A(n_s[:, i % 3, :], n_s[:, i % 3, :], ACT.Exp, bias=n_mx[:, i % 3, 1:2], accum_out=n_rs[:, i % 3, 0:1]).then_inc(S["na_exp"], 1)
            na_exp(0)
            for i in range(2 * NA_H):
                h, qt = i // 2, i % 2
                if i + 1 < 2 * NA_H:
                    na_exp(i + 1)
                act.wait_ge(S["na_tr"], i + 1)
                if i >= 2:
                    act.wait_ge(S["na_o_mm"], i - 1)
                A(n_pt[:, i % 2, :], pb[2 + i % 2][:, :], ACT.Copy).then_inc(S["na_pt"], 1)
                act.wait_ge(S["na_o_mm"], i + 1)
                p0 = 64 * (h % 2)
                A(n_o[p0:p0 + 64, h // 2, 128 * qt:128 * qt + 128], pb[4 + i % 2][p0:p0 + 64, 0:128], ACT.Copy).then_inc(S["na_o_ev"], 1)
            act.wait_ge(S["proj_x"], 3 * DC)
            squares("n2_1", DC, lambda c: xT[:, c, 0:NT])
            sqrt("n2_1", DC, 7, NT)
            modulate("n2_1", 1, 1, NT)
            ffn(1, NT)
            act.wait_ge(S["ffn_out_x"], 3 * DC)
            squares("fin", DC, lambda c: xT[:, c, 0:NT])
            sqrt("fin", DC, 7, NT)

            act.wait_ge(S["fin_h"], DC)
            act.wait_ge(S["meta_in"], 16)
            squares("mix", DC, lambda c: zT[:, c, :])
            sqrt("mix", DC, 7, T2)
            for u in range(12):
                act.wait_ge(S["hy_mm"], u + 1)
                A(hy_u[:, u, :], pb[u % 4][:, 0:T2], ACT.Identity, bias=col("cb2", u), scale=col("cw2", 12 + u)).then_inc(S["hy_mid"], 1)
            copies(4, "hg_mm", "hg_ev", lambda u: pb[u % 4][:, 0:T2], lambda u: q_q[:, u, :], func=ACT.Silu)
            act.wait_ge(S["lb_diff"], 1)
            A(lbv[:, 0:8], lbv[:, 0:8], ACT.Exp).then_inc(S["lb_exp"], 1)
            copies(8, "hg_mm", "hg_ev", lambda u: pb[u % 4][:, 0:T2], lambda u: q_lf[:, u, :], func=ACT.Sigmoid, ahead=4)
            copies(3, "hg_v_mm", "hg_v_ev", lambda u: pb[u][0:H.tiles[u][1], :], lambda u: q_v[0:H.tiles[u][1], u, :])
            copies(4, "hg_mm", "hg_ev", lambda u: pb[u % 4][:, 0:T2], lambda u: q_g[:, u, :], func=ACT.Silu, ahead=12)
            act.wait_ge(S["hg_k"], 8)
            for u in range(8):
                A(q_lf[:, u, :], q_lf[:, u, :], ACT.Ln).then_inc(S["hg_lf"], 1)
            for hd in range(8):
                decays(H, hd)
                keys_turned(H, hd)
                if hd % 2:
                    scan_read(H, hd // 2)
                    squares(f"hgrn{hd // 2}", 1, lambda e: H.o(hd // 2, e))
                    sqrt(f"hgrn{hd // 2}", 1, 7, T2)
            for i in range(2):
                act.wait_ge(S["filt_arg"], i + 1)
                A(f_h[0:HID, :], f_k[0:HID, :], ACT.Sin).then_inc(S["filt_sin"], 1)
            for g in range(12):
                od, i = g // 6, g % 6
                m = FT[i % 3][1]
                act.wait_ge(S["spec_mm"], g + 1)
                A(spec[0:m, od, i, :], pb[4 + g % 2][0:m, :], ACT.Copy).then_inc(S["spec_ev"], 1)
            for od in range(2):
                for i, (t0, n) in enumerate(TTILE):
                    act.wait_ge(S["u_tr"], 3 * od + i + 1)
                    if od == 1 and i == 0:
                        act.wait_ge(S["dft_mm"], 3)
                    if od == 0 and i == 0:
                        act.wait_ge(S["spec_mm"], 12)
                    A(u_tok[0:n, i, :], pb[i][0:n, :], ACT.Copy).then_inc(S["u_cp"], 1)
            act.wait_ge(S["hy_z"], 2 * HC)
            squares("hyena", HC, lambda c: hy_u[:, c, :])
            sqrt("hyena", HC, 7, T2)
            act.wait_ge(S["proj_x"], 4 * DC)
            squares("nffn", DC, lambda c: zT[:, c, :])
            sqrt("nffn", DC, 7, T2)

            for i, (t0, n) in enumerate(TTILE):
                for hf in range(2):
                    act.wait_ge(S["h2_tr"], 2 * i + hf + 1)
                    A(r_h2[0:n, i, 512 * hf:512 * hf + 512], pb[2 * i + hf][0:n, :], ACT.Copy).then_inc(S["h2_cp"], 1)
            act.wait_ge(S["r_diff"], 1)
            A(r_oh[:, 4, :], r_oh[:, 4, :], ACT.Exp).then_inc(S["r_exp"], 1)
            act.wait_ge(S["r_diff"], 2)
            A(r_oh[:, 5, :], r_oh[:, 5, :], ACT.Exp).then_inc(S["r_exp"], 1)
            for c in range(DC):
                for hf in range(2):
                    g = 2 * c + hf
                    act.wait_ge(S["xg_mm"], g + 1)
                    A(xg[:, c, T2 * hf:T2 * hf + T2], pb[g % 4][:, 0:T2], ACT.Copy).then_inc(S["xg_ev"], 1)
            for s, (s0, m) in enumerate(STILE):
                act.wait_ge(S["sgt_tr"], s + 1)
                A(r_SgT[0:m, s, :], pb[4 + s % 2][0:m, 0:T2], ACT.Copy).then_inc(S["sgt_ev"], 1)

            act.wait_ge(S["tables"], 1)
            rows = r_ti.bitcast(I32)

            def silu(b, j, i=0):
                act.wait_ge(S["gu_mm"], i + b + 1)
                if b >= 2:
                    act.wait_ge(S["hid"], i + b - 1)
                A(e_sg[:, j, :], pb[2 * j][:, :], ACT.Silu).then_inc(S["silu"], 1)

            def turned(b, j, i=0):
                act.wait_ge(S["hid_tr"], i + b + 1)
                if b >= 2:
                    act.wait_ge(S["down_mm"], i + b - 1)
                A(e_hT[:, j, :, :].rearrange("p a b -> p (a b)"), pb[4][:, :], ACT.Copy).then_inc(S["hT_cp"], 1)

            def y_out(b, j, i=0):
                row = act.value_load(rows[0:1, bass.ds(i + b, 1)], min_val=0, max_val=SLOTS)
                act.wait_ge(S["y_cp"], i + b + 1)
                if b >= 1:
                    act.wait_ge(S["y_out"], 16 * i + 16 * b)
                act.dma_start(ysort[bass.ds(row, WIN), :], e_y[:, j, :]).then_inc(S["y_out"], 16)
            silu(0, 0)
            for b in range(2):
                turned(b, b % 2)
                silu(b + 1, (b + 1) % 2)
                y_out(b, b % 2)
            LOOPS = (NE - 4) // 2
            with act.Fori(0, LOOPS) as i:
                for b in (2, 3):
                    turned(b, b % 2, 2 * i)
                    silu(b + 1, (b + 1) % 2, 2 * i)
                    y_out(b, b % 2, 2 * i)
            for b in range(2 + 2 * LOOPS, NB):
                turned(b, b % 2)
                if b + 1 < NB:
                    silu(b + 1, (b + 1) % 2)
                y_out(b, b % 2)
            act.wait_ge(S["y_out"], 16 * NB)
            for s, (s0, n) in enumerate(STILE):
                act.dma_start(y_s[0:n, s, :], ysort[s0:s0 + n, :]).then_inc(S["ys_in"], 16)
            act.wait_ge(S["moe_x"], DC)
            squares("nfin", DC, lambda c: zT[:, c, :])
            sqrt("nfin", DC, 7, T2)
            act.wait_ge(S["nfin_h"], DC)
            act.dma_start(out.rearrange("(c p) t -> p c t", p=P), h2T[:, :, N_META:T2]).then_inc(S["stored"], 16)
            act.wait_ge(S["stored"], 16)

        @block.vector
        def _(dve):
            steps = [0]

            def step(ins):
                steps[0] += 1
                ins.then_inc(S["dve_step"], 1)
                dve.wait_ge(S["dve_step"], steps[0])

            TTn, STT, TS = dve.tensor_tensor, dve.scalar_tensor_tensor, dve.tensor_scalar

            def rsq(name, T):
                q0, i = norms[name]
                dve.wait_ge(S["rs_sqrt"], i + 1)
                step(dve.reciprocal(rstd[:, 0:T], rstd[:, 0:T]))

            def norm_mod(name, k, T):
                rsq(name, T)
                for c in range(DC):
                    TTn(hT[:, c, 0:T], xT[:, c, 0:T], rstd[:, 0:T], ALU.mult).then_inc(S["mod_xr"], 1)
                dve.wait_ge(S["mod_xr"], DC * (k + 1))
                dve.sem_inc(S["norm_done"], 1)

            def norm_plain(name, T, chunks, dst, src, gain, done):
                rsq(name, T)
                for c in range(chunks):
                    STT(out=dst(c), in0=src(c), scalar=gain(c), in1=rstd[:, 0:T], op0=ALU.mult, op1=ALU.mult).then_inc(S[done], 1)
                dve.wait_ge(S[done], chunks)
                dve.sem_inc(S["norm_done"], 1)

            def residual(m, mmsem, done, bank, T, l, part, ahead=0):
                dve.wait_ge(S[mmsem], ahead + m + 1)
                for hf in range(T // NT):
                    v = xT[:, m, NT * hf:NT * hf + NT]
                    STT(out=v, in0=pb[bank][:, NT * hf:NT * hf + NT], scalar=mod[:, l, 8 * part + m, hf:hf + 1], in1=v,
                        op0=ALU.mult, op1=ALU.add).then_inc(S[done], 1)

            def taps(dst, src, w0, w2, halves, done):
                n = dst.shape[1] // halves
                dv = dst.rearrange("p (a n) -> p a n", n=n)
                sv = src.rearrange("p (a n) -> p a n", n=n)
                step(STT(out=dv[:, :, 1:n], in0=sv[:, :, 0:n - 1], scalar=w0, in1=dv[:, :, 1:n], op0=ALU.mult, op1=ALU.add))
                STT(out=dv[:, :, 0:n - 1], in0=sv[:, :, 1:n], scalar=w2, in1=dv[:, :, 0:n - 1], op0=ALU.mult, op1=ALU.add)\
                    .then_inc(S[done], 1)

            def ffn(l, T):
                def conv(i):
                    j, u = i // 2, i % 2
                    dve.wait_ge(S["ffn_mid"], 22 * l + i + 1)
                    taps(f_t1[:, i % 4, 0:T], pb[(4 * j + 2 * u) % 8][:, 0:T], col("fcw", 3 * l * FC + i), col("fcw", (3 * l + 2) * FC + i),
                         T // NT, "ffn_conv")
                for i in range(FC):
                    j, u = i // 2, i % 2
                    conv(i)
                    dve.wait_ge(S["ffn_silu"], 22 * l + i + 1)
                    dve.wait_ge(S["ffn_in_mm"], 44 * l + 4 * j + 2 * u + 2)
                    TTn(f_act[:, i, 0:T], f_t1[:, i % 4, 0:T], pb[(4 * j + 2 * u + 1) % 8][:, 0:T], ALU.mult).then_inc(S["ffn_act"], 1)
                for m in range(DC):
                    residual(m, "ffn_out_mm", "ffn_out_x", m % 4, T, l, 5, DC * l)

            dve.wait_ge(S["cols_in"], 16)
            for l in range(2):
                dve.wait_ge(S["ada_tr"], 12 * (l + 1))
                step(TTn(mod[:, l, :, :], pb[2 + l][:, 0:96].rearrange("p (a b) -> p a b", b=2),
                         col("ada_b", 48 * l, 48).unsqueeze(2).to_broadcast([P, 48, 2]), ALU.add))
                for w, nm in enumerate(("n1", "n2")):
                    g = col(nm, DC * l, DC).unsqueeze(2).to_broadcast([P, DC, 2])
                    last = STT(out=modA[:, l, w, :, :], in0=mod[:, l, 24 * w + 8:24 * w + 16, :], scalar=1.0, in1=g, op0=ALU.add, op1=ALU.mult)
                    if w == 0:
                        step(last)
                last.then_inc(S["mod_ready"], 1)

            norm_mod("n1_0", 0, TT)
            cos, sin = kg[:, 128:384], kg[:, 384:640]
            dve.wait_ge(S["gla_in"], 80)
            for u in range(8):
                v = g_qk[:, u, 0:NT]
                dve.wait_ge(S["rope_mm"], u + 1)
                TTn(g_tm[:, 0:NT], pb[4 + u % 2][:, 0:NT], sin, ALU.mult).then_inc(S["rope_s"], 1)
                step(TTn(v, v, cos, ALU.mult))
                dve.wait_ge(S["rope_s"], u + 1)
                step(TTn(v, v, g_tm[:, 0:NT], ALU.add))
            step(dve.memset(g_att, 0.0))

            def gate_min(hd):
                h, dr = hd // 2, hd % 2
                dve.wait_ge(S["gl_abs"], hd + 1)
                if hd >= 1:
                    dve.wait_ge(S["kd_tr"], hd)
                TS(g_tm, pb[0][:, :], col("gab", HEADS * dr + h), 0.0, ALU.add, ALU.min).then_inc(S["gl_min"], 1)
                dve.wait_ge(S["gl_ln"], hd + 1)
                dve.wait_ge(S["gl_min"], hd + 1)
                if hd >= 1:
                    dve.wait_ge(S["att_mm"], hd)
                step(TTn(g_tg, g_tm, g_e2, ALU.subtract))
                return g_tg

            def cumulate(cf, hd, src):
                h, dr = hd // 2, hd % 2
                n = cf.base + hd
                if hd >= 1:
                    dve.wait_ge(S["decay"], 7 * n)
                step(dve.tensor_tensor_scan(cf.tb, cf.scan, src, 0.0, ALU.mult, ALU.add))
                parts = [(cf.m0, cf.nc_, CH)] + ([(cf.tail[0], 1, cf.tail[1])] if cf.tail else [])

                def v(x, part):
                    o, k, w = part
                    return x[:, o:o + k * w].rearrange("p (c n) -> p c n", n=w)

                def at(x, part, i):
                    o, k, w = part
                    return v(x, part)[:, :, i:i + 1].to_broadcast([P, k, w])
                if cf is H and hd >= 1:
                    dve.wait_ge(S["kd_tr"], n)
                    dve.wait_ge(S["att_mm"], n)
                if dr == 1:
                    for p in parts:
                        step(TTn(v(cf.tm, p), at(cf.tb, p, p[2] - 1), v(cf.tb, p), ALU.subtract))
                    step(TTn(cf.tb, cf.tm, src, ALU.add))
                main = parts[0]
                step(TTn(v(cf.dm, main), v(cf.tb, main), at(cf.tb, main, CH // 2 - dr), ALU.subtract))
                for p in parts:
                    end = p[2] - 1 if dr == 0 else 0
                    hp = (p[0], 2 * p[1], p[2] // 2) if p is main else p
                    step(TTn(v(cf.tg, hp), v(cf.tb, hp), at(cf.tb, hp, hp[2] // 2), ALU.subtract))
                    last = TTn(v(cf.tm, p), at(cf.tb, p, end), v(cf.tb, p), ALU.subtract)
                    if p is not parts[-1]:
                        step(last)
                last.then_inc(S["cum"], 1)

            def decayed(cf, hd):
                h, dr = hd // 2, hd % 2
                n = cf.base + hd
                a, z = cf.m0, cf.m0 + cf.nc_ * CH
                q, k = cf.q(h), cf.k(h, dr)
                for i, (b, x) in enumerate(((cf.e2, k), (cf.tg, q), (cf.dk[:, a:z], k[:, a:z]), (cf.dm[:, a:z], q[:, a:z]),
                                            (cf.e3[:, dr, :], q), (cf.tm, k))):
                    dve.wait_ge(S["decay"], 7 * n + i + 1)
                    if i in (2, 3):
                        STT(out=b, in0=b, scalar=1.0, in1=x, op0=ALU.min, op1=ALU.mult).then_inc(S["decayed"], 1)
                    else:
                        TTn(b, b, x, ALU.mult).then_inc(S["decayed"], 1)

            def mask_scores(cf, hd):
                h, dr = hd // 2, hd % 2
                n = cf.base + hd
                dve.wait_ge(S["att_mm"], n + 1)
                if hd >= 2:
                    dve.wait_ge(S["o_mm"], n // 2)
                k = cf.nc_ // 2
                for m, bank in ((m_half[dr], 2), (m_cross[dr], 7)):
                    step(dve.copy_predicated(cf.att[:, dr, 0:k * P].rearrange("p (a n) -> p a n", n=P),
                                             m.bitcast(U32).unsqueeze(1).to_broadcast([P, k, P]),
                                             pb[bank][:, 0:k * P].rearrange("p (a n) -> p a n", n=P)))
                if cf.tail:
                    w = cf.tail[1]
                    step(dve.copy_predicated(cf.att[0:w, dr, k * P:k * P + w], m_half[dr][0:w, 0:w].bitcast(U32), pb[2][0:w, k * P:k * P + w]))
                dve.sem_inc(S["att_cp"], 1)

            def states(cf, hd):
                h, dr = hd // 2, hd % 2
                dve.wait_ge(S["decay"], 7 * (cf.base + hd) + 7)
                od = cf.order[dr]
                for i, c in enumerate(od[:-1]):
                    u = u_ahead(cf, hd) + i
                    dve.wait_ge(S["u_mm"], u + 1)
                    nxt = cf.S[:, dr, od[i + 1], :]
                    if i == 0:
                        dve.tensor_copy(nxt, pb[4 + u % 2][:, 0:cf.DV]).then_inc(S["state"], 1)
                    else:
                        dve.wait_ge(S["state"], u)
                        STT(out=nxt, in0=cf.S[:, dr, c, :], scalar=cf.e5[:, dr, c:c + 1], in1=pb[4 + u % 2][:, 0:cf.DV],
                            op0=ALU.mult, op1=ALU.add).then_inc(S["state"], 1)

            def gated(cf, h, name, base):
                rsq(name, cf.T)
                E = cf.DV // 128
                for e in range(E):
                    step(STT(out=cf.y(h, e), in0=cf.o(h, e), scalar=cf.gain(h, e), in1=rstd[:, 0:cf.T], op0=ALU.mult, op1=ALU.mult))
                    if cf is G:
                        dve.wait_ge(S["gla_r_ev"], 2 * h + e + 1)
                    TTn(cf.y(h, e), cf.y(h, e), cf.gate(h, e), ALU.mult).then_inc(S["gate_y"], 1)
                dve.wait_ge(S["gate_y"], base + E * (h + 1))
                dve.sem_inc(S["norm_done"], 1)

            cumulate(G, 0, gate_min(0))
            for hd in range(8):
                decayed(G, hd)
                mask_scores(G, hd)
                if hd < 7:
                    cumulate(G, hd + 1, gate_min(hd + 1))
                states(G, hd)
                if hd % 2:
                    gated(G, hd // 2, f"gla{hd // 2}", 0)
            for m in range(DC):
                residual(m, "proj_mm", "proj_x", m % 4, TT, 0, 2)
            norm_mod("n2_0", 1, TT)
            ffn(0, TT)
            dve.wait_ge(S["ffn_out_x"], 2 * DC)
            norm_mod("n1_1", 2, TT)

            def na_add(i):
                dve.wait_ge(S["na_s_mm"], i + 1)
                dve.wait_ge(S[f"na_bias_in{i % 4}"], 16 * (i // 4 + 1))
                if i >= 3:
                    dve.wait_ge(S["na_tr"], i - 2)
                TTn(n_s[:, i % 3, :], pb[i % 2][:, :], n_bias[:, i % 4, :], ALU.add).then_inc(S["na_add"], 1)
                dve.wait_ge(S["na_add"], i + 1)
                step(dve.tensor_reduce(n_mx[:, i % 3, 0:1], n_s[:, i % 3, :], AX_X, ALU.max))
                TS(n_mx[:, i % 3, 1:2], n_mx[:, i % 3, 0:1], -1.0, None, ALU.mult).then_inc(S["na_max"], 1)
            na_add(0)
            for i in range(2 * NA_H):
                if i + 1 < 2 * NA_H:
                    na_add(i + 1)
                dve.wait_ge(S["na_exp"], i + 1)
                step(dve.reciprocal(n_rs[:, i % 3, 1:2], n_rs[:, i % 3, 0:1]))
                TS(n_s[:, i % 3, :], n_s[:, i % 3, :], n_rs[:, i % 3, 1:2], None, ALU.mult).then_inc(S["na_p"], 1)
            for m in range(DC):
                residual(m, "proj_mm", "proj_x", m % 4, NT, 1, 2, DC)
            norm_mod("n2_1", 3, NT)
            ffn(1, NT)
            dve.wait_ge(S["ffn_out_x"], 3 * DC)
            norm_plain("fin", NT, DC, lambda c: zT[:, c, N_META:T2], lambda c: xT[:, c, 0:NT], lambda c: col("fin", c), "fin_h")
            norm_plain("mix", T2, DC, lambda c: h2T[:, c, :], lambda c: zT[:, c, :], lambda c: col("nmix", c), "mix_h")

            for u in range(12):
                dve.wait_ge(S["hy_mid"], u + 1)
                taps(hy_u[:, u, :], pb[u % 4][:, 0:T2], col("cw2", u), col("cw2", 24 + u), 1, "hy_conv")
            lb = col("lb", 0, 16).rearrange("p (a r c) -> p a r c", r=2, c=4)
            lv = lbv.rearrange("p (a c) -> p a c", c=4)
            step(TTn(lv[:, 0:2, :], lb[:, :, 1, :], lb[:, :, 0, :], ALU.subtract))
            dve.sem_inc(S["lb_diff"], 1)
            dve.wait_ge(S["lb_exp"], 1)
            step(TS(lv[:, 0:2, :], lv[:, 0:2, :], 1.0, None, ALU.add))
            step(dve.reciprocal(lv[:, 0:2, :], lv[:, 0:2, :]))
            step(TS(lv[:, 2:4, :], lv[:, 0:2, :], -1.0, 1.0, ALU.mult, ALU.add))
            for u in range(8):
                dve.wait_ge(S["hg_ev"], 4 + u + 1)
                step(TS(q_lf[:, u, :], q_lf[:, u, :], lbv[:, 8 + u:9 + u], lbv[:, u:u + 1], ALU.mult, ALU.add))
                TS(q_k[:, u, :], q_lf[:, u, :], -1.0, 1.0, ALU.mult, ALU.add).then_inc(S["hg_k"], 1)
            dve.wait_ge(S["b2_in"], 16)
            step(dve.memset(q_att, 0.0))
            dve.wait_ge(S["hg_v_ev"], 3)
            dve.wait_ge(S["hg_ev"], 16)
            dve.wait_ge(S["hg_lf"], 8)
            for hd in range(8):
                cumulate(H, hd, q_lf[:, 4 * (hd % 2) + hd // 2, :])
                decayed(H, hd)
                mask_scores(H, hd)
                states(H, hd)
                if hd % 2:
                    gated(H, hd // 2, f"hgrn{hd // 2}", 8)

            TWO_PI = 2 * np.pi
            HI = float(np.float32(6.28125))
            LO = float(np.float32(TWO_PI - HI))
            BIG = float(1.5 * 2 ** 23)
            fr = col("ffr", 0, rows=HID)
            for i in range(2):
                dve.wait_ge(S["filt_mm"], i + 1)
                a, k = f_hs[0:HID, 0, 0:T2], f_k[0:HID, :]
                step(TS(a, pb[i][0:HID, 0:T2], col("fb1" if i == 0 else "fb2", 0, rows=HID), fr, ALU.add, ALU.mult))
                step(TS(k, a, float(1 / TWO_PI), BIG, ALU.mult, ALU.add))
                step(TS(k, k, BIG, None, ALU.subtract))
                step(STT(out=a, in0=k, scalar=-HI, in1=a, op0=ALU.mult, op1=ALU.add))
                step(STT(out=k, in0=k, scalar=-LO, in1=a, op0=ALU.mult, op1=ALU.add))
                TS(k, k, 3.1415925, -3.1415925, ALU.min, ALU.max).then_inc(S["filt_arg"], 1)
            for od in range(2):
                for i, (t0, n) in enumerate(TTILE):
                    g = 3 * od + i
                    dve.wait_ge(S["filt3_mm"], g + 1)
                    if od == 1 and i == 0:
                        dve.wait_ge(S["spec_mm"], 6)
                    step(TTn(f_hs[0:n, i, :], pb[2][0:n, :], win[0:n, i, 0, :], ALU.mult))
                    step(TTn(f_b[0:n, :], pb[3][0:n, :], win[0:n, i, 1, :], ALU.mult))
                    step(TTn(f_hd[0:n, i, :], f_hs[0:n, i, :], f_b[0:n, :], ALU.subtract))
                    TTn(f_hs[0:n, i, :], f_hs[0:n, i, :], f_b[0:n, :], ALU.add).then_inc(S["filt_hd"], 1)
            for od in range(2):
                for i in range(3):
                    m = FT[i][1]
                    dve.wait_ge(S["dft_mm"], 3 * od + i + 1)
                    if od + i:
                        dve.wait_ge(S["yf"], 3 * od + i)
                    if od == 0 and i == 0:
                        dve.wait_ge(S["spec_ev"], 12)
                    if od == 1 and i == 0:
                        dve.wait_ge(S["idft_mm"], HC)
                    b = 3 + 2 * (i % 2)
                    ur, ui = pb[b][0:m, :], pb[b + 1][0:m, :]
                    hr, hi = spec[0:m, od, i, :], spec[0:m, od, 3 + i, :]
                    t0_, t1_ = hy_tmp[0:m, 0, :], hy_tmp[0:m, 1, :]
                    step(TTn(t0_, ur, hr, ALU.mult))
                    step(TTn(t1_, ui, hi, ALU.mult))
                    step(TTn(yf[0:m, i, :], t0_, t1_, ALU.subtract))
                    step(TTn(t0_, ur, hi, ALU.mult))
                    step(TTn(t1_, ui, hr, ALU.mult))
                    TTn(yf[0:m, 3 + i, :], t0_, t1_, ALU.add).then_inc(S["yf"], 1)
                for c in range(HC):
                    dve.wait_ge(S["idft_mm"], HC * od + c + 1)
                    if od == 0 and c == 0:
                        dve.wait_ge(S["u_tr"], 3)
                    v = hy_u[:, c, :]
                    step(STT(out=v, in0=v, scalar=col("skip", HC * od + c), in1=pb[c][:, 0:T2], op0=ALU.mult, op1=ALU.add))
                    TTn(v, v, hy_u[:, 4 * (od + 1) + c, :], ALU.mult).then_inc(S["hy_z"], 1)
            dve.wait_ge(S["hy_z"], 2 * HC)
            norm_plain("hyena", T2, HC, lambda c: y_cat[:, c, :], lambda c: hy_u[:, c, :], lambda c: col("hyn", c), "hyena_y")
            dve.sem_inc(S["hyena_done"], 1)
            for m in range(DC):
                dve.wait_ge(S["proj_mm"], 2 * DC + m + 1)
                TTn(zT[:, m, :], zT[:, m, :], pb[m % 4][:, 0:T2], ALU.add).then_inc(S["proj_x"], 1)
            dve.wait_ge(S["proj_x"], 4 * DC)
            norm_plain("nffn", T2, DC, lambda c: h2T[:, c, :], lambda c: zT[:, c, :], lambda c: col("nffn", c), "nffn_h")

            dve.wait_ge(S["zeroed"], 3)
            dve.wait_ge(S["route_in"], 32)
            dve.wait_ge(S["route_mm"], 1)
            for i, (t0, n) in enumerate(TTILE):
                step(dve.tensor_copy(r_lg[0:n, i, :], pb[7][0:n, 72 * i:72 * i + 72]))
            desc = kr[:, 0:8].unsqueeze(1).to_broadcast([P, 3, 8])
            valid = kr[:, 8:11]
            sm = [r_sm[:, i, :] for i in range(40)]
            oh = [r_oh[:, i, :].rearrange("p (t e) -> p t e", e=8) for i in range(6)]
            gl = r_lg[:, :, 0:NG]

            def b8(x):
                return x.unsqueeze(2).to_broadcast([P, 3, 8])

            def first_max(vals, mx, o, tmp):
                step(dve.tensor_reduce(mx, vals, AX_X, ALU.max))
                step(TTn(o, vals, b8(mx), ALU.is_ge))
                step(TTn(o, o, desc, ALU.mult))
                step(dve.tensor_reduce(tmp, o, AX_X, ALU.max))
                step(TTn(o, o, b8(tmp), ALU.is_equal))
            first_max(gl, sm[0], oh[0], sm[1])
            step(TTn(oh[4], gl, b8(sm[0]), ALU.subtract))
            dve.sem_inc(S["r_diff"], 1)
            dve.wait_ge(S["r_exp"], 1)
            step(dve.tensor_reduce(sm[2], oh[4], AX_X, ALU.add))
            step(dve.reciprocal(sm[3], sm[2]))
            t1 = r_t1.rearrange("p t (g e) -> p t g e", e=8)
            for i in range(3):
                step(TTn(t1[:, i, :, :], r_lg[:, i, NG:].rearrange("p (g e) -> p g e", e=8),
                         oh[0][:, i, :].unsqueeze(2).to_broadcast([P, 8, 8]), ALU.mult))
                step(dve.tensor_reduce(oh[5][:, i, :], t1[:, i, :, :].rearrange("p g e -> p e g"), AX_X, ALU.add))
            step(dve.tensor_reduce(sm[4], oh[5], AX_X, ALU.max))
            step(TTn(oh[5], oh[5], b8(sm[4]), ALU.subtract))
            dve.sem_inc(S["r_diff"], 1)
            dve.wait_ge(S["r_exp"], 2)
            step(dve.tensor_reduce(sm[5], oh[5], AX_X, ALU.add))
            step(dve.reciprocal(sm[6], sm[5]))
            step(TTn(oh[5], oh[5], b8(sm[6]), ALU.mult))
            first_max(oh[5], sm[7], oh[1], sm[8])
            step(STT(out=oh[5], in0=oh[1], scalar=-2.0, in1=oh[5], op0=ALU.mult, op1=ALU.add))
            first_max(oh[5], sm[9], oh[2], sm[10])
            step(TTn(sm[11], sm[7], sm[9], ALU.add))
            step(dve.reciprocal(sm[12], sm[11]))
            step(TTn(sm[12], sm[12], sm[3], ALU.mult))
            step(TTn(sm[13], sm[12], sm[7], ALU.mult))
            step(TTn(sm[14], sm[12], sm[9], ALU.mult))
            step(TTn(oh[0], oh[0], b8(valid), ALU.mult))
            for k in range(2):
                for i in range(3):
                    step(TTn(r_M[:, k, i, :].rearrange("p (g e) -> p g e", e=8), oh[0][:, i, :].unsqueeze(2).to_broadcast([P, 8, 8]),
                             oh[1 + k][:, i, :].unsqueeze(1).to_broadcast([P, 8, 8]), ALU.mult))
            TTn(r_M[:, 2, :, :], r_M[:, 0, :, :], r_M[:, 1, :, :], ALU.add).then_inc(S["route_M"], 1)
            dve.wait_ge(S["pos_mm"], 1)
            cnt, incl, start = r_cnt[:, 0, :], r_cnt[:, 1, :], r_cnt[:, 2, :]
            step(dve.tensor_copy(cnt, pb[6][:, 192:256]))
            step(dve.tensor_tensor_scan(incl, one1[:, 0:NE], cnt, 0.0, ALU.mult, ALU.add))
            step(TTn(start, incl, cnt, ALU.subtract))
            step(TTn(r_t2, pb[6][:, 0:192].rearrange("p (t e) -> p t e", e=NE), start.unsqueeze(1).to_broadcast([P, 3, NE]), ALU.add))
            iota = kr[:, 75:75 + SLOTS]
            for k in range(2):
                step(TTn(r_t1, r_t2, r_M[:, k, :, :], ALU.mult))
                step(dve.tensor_reduce(sm[15 + k], r_t1, AX_X, ALU.add))
                step(TTn(sm[15 + k], sm[15 + k], valid, ALU.add))
                step(TS(sm[15 + k], sm[15 + k], -1.0, None, ALU.add))
            for i in range(3):
                step(TS(r_Sg[:, i, :], iota, sm[15][:, i:i + 1], None, ALU.is_equal))
                step(STT(out=r_S[:, i, :], in0=iota, scalar=sm[16][:, i:i + 1], in1=r_Sg[:, i, :], op0=ALU.is_equal, op1=ALU.add))
            dve.sem_inc(S["route_S"], 1)
            ex, exn, tmp, w_ = r_cnt[0:1, 3, :], r_cnt[0:1, 4, :], r_cnt[0:1, 5, :], r_row[0:1, 0, :]
            c0, s0, eio = cnt[0:1, :], start[0:1, :], kr[0:1, 11:75]
            tab_r, tab_e = r_ti[0:1, 0:72], r_ti[0:1, 72:144]
            step(TS(ex, c0, float(WIN), None, ALU.is_gt))
            step(STT(out=ex, in0=c0, scalar=float(2 * WIN), in1=ex, op0=ALU.is_gt, op1=ALU.add))
            step(dve.tensor_tensor_scan(exn, one1[0:1, 0:NE], ex, 0.0, ALU.mult, ALU.add))
            step(TTn(exn, exn, ex, ALU.subtract))
            for j in range(EXTRA):
                a, b = r_row[0:1, 1, :], tmp
                step(TTn(w_, exn, ex, ALU.add))
                step(TS(w_, w_, float(j), None, ALU.is_gt))
                step(STT(out=w_, in0=exn, scalar=float(j), in1=w_, op0=ALU.is_le, op1=ALU.mult))
                step(TS(a, exn, float(-WIN), float(WIN * (j + 1)), ALU.mult, ALU.add))
                step(TS(b, c0, float(-WIN), None, ALU.add))
                step(TTn(a, a, b, ALU.min))
                step(TTn(a, a, s0, ALU.add))
                step(TTn(a, a, w_, ALU.mult))
                step(dve.tensor_reduce(r_sm[0:1, 20 + j, 0:1], a, AX_X, ALU.add))
                step(TTn(a, eio, w_, ALU.mult))
                step(dve.tensor_reduce(r_sm[0:1, 20 + j, 1:2], a, AX_X, ALU.add))
                step(dve.tensor_reduce(r_sm[0:1, 20 + j, 2:3], w_, AX_X, ALU.add))
                step(TS(r_sm[0:1, 20 + j, 2:3], r_sm[0:1, 20 + j, 2:3], -float(SLOTS), float(SLOTS), ALU.mult, ALU.add))
                step(TTn(r_sm[0:1, 20 + j, 0:1], r_sm[0:1, 20 + j, 0:1], r_sm[0:1, 20 + j, 2:3], ALU.add))
                step(dve.tensor_copy(tab_r.bitcast(I32)[:, NE + j:NE + j + 1], r_sm[0:1, 20 + j, 0:1]))
                step(dve.tensor_copy(tab_e.bitcast(I32)[:, NE + j:NE + j + 1], r_sm[0:1, 20 + j, 1:2]))
            step(dve.tensor_copy(tab_r.bitcast(I32)[:, 0:NE], s0))
            dve.sem_inc(S["tables"], 1)
            for i in range(3):
                step(TS(r_Sg[:, i, :], iota, sm[15][:, i:i + 1], sm[13][:, i:i + 1], ALU.is_equal, ALU.mult))
                for hf in range(2):
                    o = T2 * hf
                    step(TS(r_sel, iota[:, o:o + T2], sm[16][:, i:i + 1], sm[14][:, i:i + 1], ALU.is_equal, ALU.mult))
                    step(TTn(r_Sg[:, i, o:o + T2], r_Sg[:, i, o:o + T2], r_sel, ALU.add))
            dve.sem_inc(S["route_S"], 1)

            dve.wait_ge(S["xg_ev"], 16)
            dve.wait_ge(S["zeroed"], 3)
            dve.wait_ge(S["sgt_ev"], 5)
            rows = r_ti.bitcast(I32)

            def window(b, j, i=0):
                row = dve.value_load(rows[0:1, bass.ds(i + b, 1)], min_val=0, max_val=SLOTS)
                if b >= 2:
                    dve.wait_ge(S["gu_mm"], i + b - 1)
                dve.tensor_copy(e_xw[:, j, :, :], xg[:, :, bass.ds(row, WIN)]).then_inc(S["xw"], 1)

            def hidden(b, j, i=0):
                dve.wait_ge(S["silu"], i + b + 1)
                if b >= 2:
                    dve.wait_ge(S["hid_tr"], i + b - 1)
                TTn(e_hid[:, j, :], e_sg[:, j, :], pb[2 * j + 1][:, :], ALU.mult).then_inc(S["hid"], 1)

            def y_copy(b, j, i=0):
                dve.wait_ge(S["down_mm"], i + b + 1)
                if b >= 2:
                    dve.wait_ge(S["y_out"], 16 * i + 16 * (b - 1))
                dve.tensor_copy(e_y[:, j, 0:512], pb[5][:, :])
                dve.tensor_copy(e_y[:, j, 512:1024], pb[6][:, :]).then_inc(S["y_cp"], 1)
            window(0, 0)
            window(1, 1)
            hidden(0, 0)
            for b in range(2):
                window(b + 2, b % 2)
                hidden(b + 1, (b + 1) % 2)
                y_copy(b, b % 2)
            LOOPS = (NE - 4) // 2
            with dve.Fori(0, LOOPS) as i:
                for b in (2, 3):
                    window(b + 2, b % 2, 2 * i)
                    hidden(b + 1, (b + 1) % 2, 2 * i)
                    y_copy(b, b % 2, 2 * i)
            for b in range(2 + 2 * LOOPS, NB):
                if b + 2 < NB:
                    window(b + 2, b % 2)
                if b + 1 < NB:
                    hidden(b + 1, (b + 1) % 2)
                y_copy(b, b % 2)
            for m in range(DC):
                dve.wait_ge(S["comb_mm"], m + 1)
                TTn(zT[:, m, :], zT[:, m, :], pb[m % 4][:, 0:T2], ALU.add).then_inc(S["moe_x"], 1)
            dve.wait_ge(S["moe_x"], DC)
            norm_plain("nfin", T2, DC, lambda c: h2T[:, c, :], lambda c: zT[:, c, :], lambda c: col("nfin", c), "nfin_h")


def channel_columns(i):
    def c(a, n=P):
        a = np.asarray(a, np.float32).reshape(-1, n)
        return np.pad(a, ((0, 0), (0, P - n)))
    parts = {"c2": np.stack([np.reshape(i["c"], (DC, P)), np.reshape(i["c_ctx"], (DC, P))], 1), "n1": i["norm1_g"], "n2": i["norm2_g"],
             "fin": i["final_g"], "ada_b": i["ada_b"], "fcw": i["ffn_conv_w"], "fcb": i["ffn_conv_b"], "gab": i["gla_a_b"],
             "gng": i["gla_norm_g"], "cw2": i["conv_w_2"], "cb2": i["conv_b_2"], "skip": i["filt_skip_2"], "hyn": i["hyena_norm_2"],
             "lb": np.stack([i["lb_fwd_2"], i["lb_bwd_2"]]), "hgn": i["hgrn_norm_2"], "nmix": i["norm_mix_2"],
             "nffn": i["norm_ffn_2"], "nfin": i["norm_final_2"], "fb1": i["filt_b1_2"], "fb2": i["filt_b2_2"], "ffr": i["filt_freq_2"]}
    return np.ascontiguousarray(np.concatenate([c(parts[n], HID if n in ("fb1", "fb2", "ffr") else P) for n, _ in COLS]).T)


def bias_windows(rpb):
    rows = NT // GRID
    out = np.full((NA_H, rows, GRID, rows, GRID), -1e30, np.float32)
    for r in range(rows):
        for k in range(rows):
            for c in range(GRID):
                s = min(max(c - NA_KW // 2, 0), GRID - NA_KW)
                out[:, r, c, k, s:s + NA_KW] = rpb[:, k - r + NA_KH - 1, s - c + NA_KW - 1:s - c + 2 * NA_KW - 1]
    return out.reshape(NA_H, 2, P, NT)


def constants():
    f = np.float32
    j = np.arange(CH)
    same = j[:, None] // (CH // 2) == j[None, :] // (CH // 2)
    masks = []
    for causal in (j[:, None] <= j[None, :], j[:, None] >= j[None, :]):
        masks += [np.kron(np.eye(2), causal & same).astype(f), np.kron(np.eye(2), causal & ~same).astype(f)]
    p = np.arange(P)
    k_a = np.concatenate([np.eye(P, dtype=f)] + masks + [(p[:, None] < p[None, :]).astype(f)], 1)
    perm = np.zeros((P, P), f)
    for q in range(P):
        if q % 64 < 32:
            perm[q + 32, q] = -1
        else:
            perm[q - 32, q] = 1
    half = P // 2
    inv = (1.0 / (f(10000.0) ** (np.arange(0, half, 2, dtype=f) / f(half)))).astype(f)
    pos = np.arange(NT)
    ang = np.where(p[:, None] < half, (pos // GRID)[None, :], (pos % GRID)[None, :]).astype(f) * inv[p % 32][:, None]
    scan = np.ones((P, TT), f)
    scan[:, ::CH] = 0
    k_g = np.concatenate([perm, np.cos(ang).astype(f), np.sin(ang).astype(f), scan], 1)
    scan2 = np.ones((P, T2), f)
    scan2[:, 0] = 0
    scan2[:, N_META::CH] = 0
    th = 2 * np.pi * ((np.arange(T2)[:, None] * np.arange(NF)[None, :]) % NFFT) / NFFT
    dft = np.concatenate([np.cos(th), -np.sin(th)], 1).astype(f)
    wt = np.full((NF, 1), 2.0 / NFFT)
    wt[0] = wt[-1] = 1.0 / NFFT
    idft = np.concatenate([wt * np.cos(th.T), -wt * np.sin(th.T)], 0).astype(f)
    t = np.arange(T2, dtype=f) / f(T2 - 1)
    bands = np.linspace(1e-4, (EMB - 1) // 2 - 1, (EMB - 1) // 2, dtype=f)
    a2 = (f(2.0 * np.pi / T2) * np.arange(T2, dtype=f))[:, None] * bands[None, :]
    z = np.concatenate([t[:, None], np.cos(a2), -np.sin(a2)], 1).astype(f)
    deltas = np.abs(np.linspace(np.log(1e-2) / 1.5, np.log(1e-2) / 0.3, HY, dtype=f))
    win = np.repeat(np.exp(-t[:, None] * deltas[None, :]).astype(f)[:, None, :], 2, 1)
    win[0, 1, :] = 0
    valid = np.zeros((P, 3), f)
    for i, (_, n) in enumerate(TTILE):
        valid[:n, i] = 1
    k_r = np.concatenate([np.tile(np.arange(8, 0, -1, dtype=f), (P, 1)), valid, np.tile(np.arange(NE, dtype=f), (P, 1)),
                          np.tile(np.arange(SLOTS, dtype=f), (P, 1))], 1)
    return {"k_a": k_a, "k_g": k_g, "k_scan2": scan2, "k_dft": dft, "k_idft": idft, "k_zT": z.T, "k_win": win, "k_route": k_r}


_PLAIN = ["ada_w", "ffn_w_in", "ffn_w_out"]
_FIRST = ["gla_w_in", "gla_w_out", "gla_a_w1", "gla_a_w2", "na_w_qkv", "na_w_out", "w_in_2", "w_out_2", "filt_w1_2", "filt_w2_2",
          "filt_w3_2", "w_gate_2", "w_up_2", "w_down_2"]


def kernel(**inputs):
    import concourse.bacc as bacc
    from concourse.bass_utils import run_bass_kernel_spmd as run

    i = {k: np.asarray(v) for k, v in inputs.items()}
    a = dict(constants())
    a["xT"] = np.concatenate([i["x"][0], i["ctx"][0]]).T
    a["metaT"] = i["meta_tokens_2"].T
    a["cols"] = channel_columns(i)
    a["na_bias"] = bias_windows(i["na_rpb"][0])
    a["w_route"] = np.concatenate([i["w_router_group_2"][0], i["w_router_expert_2"][0].reshape(D, NE)], 1)
    for n in _PLAIN:
        a[n] = i[n]
    for n in _FIRST:
        a[n] = i[n][0]
    nc = bacc.Bacc("TRN2", target_bir_lowering=False, num_devices=1)
    arrays = {f"in_{n}": np.ascontiguousarray(v) for n, v in a.items()}
    handles = {n: nc.dram_tensor(f"in_{n}", arrays[f"in_{n}"].shape, F32, kind="ExternalInput").ap() for n in a}
    out = nc.dram_tensor("out_yT", (D, NT), F32, kind="ExternalOutput").ap()
    build(nc, handles, out)
    r = run(nc, [arrays], core_ids=[0])
    return np.ascontiguousarray(r.results[0]["out_yT"].T)[None]
```

```python
from contextlib import ExitStack

import numpy as np

import concourse.bass as bass
from concourse import mybir

F32 = mybir.dt.float32
F32R = mybir.dt.float32r
I32 = mybir.dt.int32
U32 = mybir.dt.uint32
ALU = mybir.AluOpType
ACT = mybir.ActivationFunctionType
AX_X = mybir.AxisListType.X

P = 128
D = 1024
DC = D // P
NT = 256
TT = 512
D_FF = 2816
FC = D_FF // P
HEADS = 4
CH = 64
GRID = 64
NA_H, NA_KH, NA_KW = 16, 8, 16
N_META = 16
T2 = N_META + NT
NFFT = 2 * T2
NF = T2 + 1
HY = 512
HC = HY // P
EMB, HID = 33, 64
NE, NG, EPG = 64, 8, 8
DE = 512
W_STEPS = FC + DC
WIN = 64
SLOTS = 2 * T2
EXTRA = SLOTS // WIN
EPS = 1e-6
GATE_NORM = 16.0
FT = [(0, 128), (128, 128), (256, NF - 256)]
TTILE = [(0, 128), (128, 128), (256, T2 - 256)]
STILE = [(s, min(128, SLOTS - s)) for s in range(0, SLOTS, 128)]

COLS = [("c2", 2 * DC), ("n1", 2 * DC), ("n2", 2 * DC), ("fin", DC), ("ada_b", 2 * 48),
        ("fcw", 2 * 3 * FC), ("fcb", 2 * FC), ("gab", 2 * HEADS), ("gng", 2),
        ("cw2", 3 * 12), ("cb2", 12), ("skip", 2 * HC), ("hyn", HC), ("lb", 16), ("hgn", HEADS),
        ("nmix", DC), ("nffn", DC), ("nfin", DC), ("fb1", 1), ("fb2", 1), ("ffr", 1)]
COL = {}
NCOL = 0
for _name, _n in COLS:
    COL[_name] = (NCOL, _n)
    NCOL += _n

KA_N = 6 * 128
KG = {"perm": (0, 128), "cos": (128, 256), "sin": (384, 256), "scan": (640, 512)}
KG_N = 1152
KR = {"desc": (0, 8), "valid": (8, 3), "eio": (11, 64), "iota": (75, SLOTS)}
KR_N = 75 + SLOTS


def first_block_slabs(d):
    def cols(w, c0, n):
        return w[:, c0:c0 + n].rearrange("(c p) n -> p c n", p=P)

    out = []
    for l in range(2):
        for s in range(12):
            out.append(([(0, 512, cols(d["ada_w"][l], 512 * s, 512))], DC, 512, ("ada_mm", 12 * l + s + 1)))

    def ffn(l):
        for j in range(FC // 2):
            out.append(([(0, 256, cols(d["ffn_w_in"][l], 256 * j, 256)),
                         (256, 256, cols(d["ffn_w_in"][l], D_FF + 256 * j, 256))], DC, 512, ("ffn_in_mm", 44 * l + 4 * j + 4)))
        for m in range(DC):
            out.append(([(0, P, cols(d["ffn_w_out"][l], P * m, P))], FC, P, ("ffn_out_mm", 8 * l + m + 1)))

    def wide(w, names):
        for s, free in enumerate(names):
            out.append(([(0, 512, cols(w, 512 * s, 512))], DC, 512, free))

    wide(d["gla_w_in"], [("gla_qk_mm", 4), ("gla_qk_mm", 8), ("gla_v_mm", 4), ("gla_v_mm", 8),
                         ("gla_r_mm", 4), ("gla_r_mm", 8)])
    wide(d["gla_w_out"], [("proj_mm", 4), ("proj_mm", 8)])
    ffn(0)
    wide(d["na_w_qkv"], [("na_q_mm", 4), ("na_q_mm", 8), ("na_k_mm", 4), ("na_k_mm", 8), ("na_v_mm", 4), ("na_v_mm", 8)])
    wide(d["na_w_out"], [("proj_mm", 12), ("proj_mm", 16)])
    ffn(1)
    wide(d["w_in_2"], [("hy_mm", 4), ("hy_mm", 8), ("hy_mm", 12), ("hg_mm", 4), ("hg_mm", 8), ("hg_mm", 12),
                       ("hg_v_mm", 3), ("hg_mm", 16)])
    wide(d["w_out_2"], [("proj_mm", 20), ("proj_mm", 24)])
    return out


def build(nc, d, out):
    ctx = ExitStack()
    with ctx:
        def sb(name, shape, dt=F32):
            return ctx.enter_context(nc.sbuf_tensor("s_" + name, shape, dt))

        def sb_both(name, shape):
            with nc.sbuf_tensor("s_" + name, shape, F32) as plain:
                pass
            return plain, sb(name + "_r", shape, F32R)

        class Sems(dict):
            def __missing__(self, name):
                self[name] = ctx.enter_context(nc.semaphore(name))
                return self[name]

        S = Sems()
        pb = [ctx.enter_context(nc.psum_tensor(f"bank{i}", [P, 512], F32)) for i in range(8)]

        NRING = 4
        ring, ring_r = zip(*[sb_both(f"ring{k}", [P, 4096]) for k in range(NRING)])
        xT = sb("xT", [P, DC, TT])
        hT, hT_r = sb_both("hT", [P, DC, TT])
        sq = sb("sq", [P, 2, TT])
        rstd = sb("rstd", [P, TT])
        cols = sb("cols", [P, NCOL])
        ka = sb("ka", [P, KA_N])
        ones = sb("ones", [P, 4, P])
        one1 = sb("one1", [P, P])
        eps = sb("eps", [P, 1])
        sc = sb("sc", [P, 2 * DC])
        mod = sb("mod", [P, 2, 48, 2])
        modA = sb("modA", [P, 2, 2, DC, 2])
        AW = (nc.sbuf_bytes_remaining // 4 if not callable(nc.sbuf_bytes_remaining) else nc.sbuf_bytes_remaining() // 4) - 64
        arena, arena_r = sb_both("arena", [P, AW])

        def carve(start=0, tensor=None, limit=None):
            at = [start]
            flat = arena if tensor is None else tensor

            def take(*shape):
                n = int(np.prod(shape))
                v = flat[:, at[0]:at[0] + n]
                at[0] += n
                assert at[0] <= (limit or AW), (at[0], AW)
                if len(shape) == 2:
                    v = v.rearrange("p (a b) -> p a b", b=shape[1])
                if len(shape) == 3:
                    v = v.rearrange("p (a b c) -> p a b c", b=shape[1], c=shape[2])
                return v
            take.at = at
            return take

        def col(name, i, n=1, rows=P):
            o = COL[name][0] + i
            return cols[0:rows, o:o + n]

        ident = ka[:, 0:128]
        m_half = [ka[:, 128:256], ka[:, 384:512]]
        m_cross = [ka[:, 256:384], ka[:, 512:640]]
        striu = ka[:, 640:768]
        ON = {1024: ones[:, 0, :], 256: ones[:, 1, :], 128: ones[:, 2, :], 512: ones[:, 3, :]}

        NA_BANK = [pb[0], pb[1], pb[6]]

        t = carve()
        g_qk, g_v, g_S = t(8, TT), t(4, D), t(2, 8, 256)
        kg, g_low, g_aw2 = t(KG_N), t(TT), t(512)
        g_tm, g_tg, g_tb, g_e2, g_e3, g_dm, g_dk = t(2, TT), t(2, TT), t(2, TT), t(2, TT), t(4, TT), t(2, TT), t(2, TT)
        g_e5, g_att, g_sr = t(4, 8), t(2, 4 * P), t(2, TT)
        g_aw1 = g_sr.rearrange("p a b -> p (a b)")[:, 0:2 * DC * 16].rearrange("p (a b c) -> p a b c", b=DC, c=16)
        g_kdt = kg[:, 0:4 * P].rearrange("p (a b) -> p a b", b=P)
        ada_row = g_S[0:2, 0, :, :].rearrange("p a b -> p (a b)").rearrange("p (a b) -> p a b", b=512)[:, 0:2, :]
        t = carve()
        f_act, f_t1 = t(FC, TT), t(4, TT)
        f_at = t.at[0]
        t = carve(tensor=arena_r)
        f_lo = t(FC, TT)
        t.at[0] = f_at
        h_hi = t(DC, TT)
        f_hi_rest = carve(f_at - 4 * TT, tensor=arena_r)(FC - DC, TT)
        W_HALF, W_OUT = DC * 256, FC * P
        w_at = AW - 3 * W_HALF
        assert f_at + DC * TT <= w_at and f_at - 4 * TT + (FC - DC) * TT <= w_at
        w_hi = [arena_r[:, w_at + W_HALF * k:w_at + W_HALF * (k + 1)].rearrange("p (c a n) -> p c a n", a=2, n=P) for k in range(3)]
        wo_hi = [arena_r[:, o:o + W_OUT].rearrange("p (c n) -> p c n", n=P) for o in (AW - W_OUT, w_at)]

        def f_hi(c, T):
            return hT_r[:, c, 0:T] if c < DC else f_hi_rest[:, c - DC, 0:T]

        def halves_of(w, half):
            return w.rearrange("p c (a h n) -> p c a h n", a=2, h=2)[:, :, :, half, :]
        t = carve()
        n_q, n_k, n_v, n_o = t(DC, NT), t(DC, TT), t(4, D), t(DC, NT)
        n_bias, n_s, n_pt = t(4, TT), t(3, TT), t(2, TT)
        n_mx, n_rs = t(3, 4), t(3, 4)
        hflat = hT[:, :, :].rearrange("p a b -> p (a b)")
        xflat = xT[:, :, :].rearrange("p a b -> p (a b)")
        zT = hflat[:, 0:DC * T2].rearrange("p (a b) -> p a b", b=T2)
        h2T = xflat[:, 0:DC * T2].rearrange("p (a b) -> p a b", b=T2)
        w_dft = hflat[:, DC * T2:DC * T2 + 3 * 2 * NF].rearrange("p (a b) -> p a b", b=2 * NF)
        w_inv = xflat[:, DC * T2:DC * T2 + 6 * T2].rearrange("p (a b) -> p a b", b=T2)
        t = carve()
        y_cat, hy_u = t(DC, T2), t(12, T2)
        b2_at = t.at[0]
        q_q, q_k, q_lf, q_g, q_v = t(HEADS, T2), t(8, T2), t(8, T2), t(HEADS, T2), t(3, HY)
        q_tm, q_tg, q_tb, q_e2, q_e3, q_dm, q_dk = t(2, T2), t(2, T2), t(2, T2), t(2, T2), t(4, T2), t(2, T2), t(2, T2)
        q_e5, q_att, q_kdt, q_S, q_scan = t(4, 8), t(2, 3 * P), t(3, P), t(2, 5, P), t(T2)
        lbv = t(16)
        t = carve(b2_at)
        spec = t(2, 6, HY)
        spec_at = t.at[0]
        win, fw3, f_hs, f_hd = t(3, 2, HY), t(4, HY), t(3, HY), t(3, HY)
        f_h, f_z, f_w12, f_k = t(T2), t(T2), t(2, HID), t(T2)
        f_b = sq[:, 0, :]
        t = carve(spec_at)
        u_tok, yf, hy_tmp = t(3, HY), t(6, HY), t(2, HY)
        NB = NE + EXTRA
        tail = AW - 2 * 4096
        t = carve(limit=tail)
        r_at = t.at[0]
        r_h2, r_S, r_Sg = t(3, D), t(3, SLOTS), t(3, SLOTS)
        t2 = carve(r_at, limit=tail)
        e_xw, e_sg, e_hid = t2(2, DC, WIN), t2(2, DE), t2(2, DE)
        e_hT, e_y = t2(2, 4, WIN), t2(2, D // 2)
        t.at[0] = max(t.at[0], t2.at[0])
        r_SgT, xg_at = t(5, T2), t.at[0]
        xg = t(DC, SLOTS + WIN)
        r_sel = t(T2)
        t3 = carve(DC * T2, tensor=xflat, limit=DC * TT)
        kr, wr = t3(KR_N), t3(DC, NG + NE)
        r_lg, r_t1, r_t2 = t(3, NG + NE), t(3, NE), t(3, NE)
        r_sm = t(40, 3)
        r_oh = t(6, 24)
        r_M = t(3, 3, NE)
        r_cnt, r_row, r_ti = t(6, NE), t(2, NE), t(2 * NB + 1)
        y_s = carve(xg_at, limit=tail)(5, D)

        def slot(n):
            return ring[n][:, :] if n < NRING else arena[:, tail + 4096 * (n - NRING):tail + 4096 * (n - NRING + 1)]

        ysort = nc.dram_tensor("ysort", (SLOTS + 2 * WIN, D), F32, kind="Internal").ap()

        slabs = first_block_slabs(d)
        place, place_r, landed, free, owner, count = [], [], [], [], {}, {}
        for n, (parts, kc, w, f) in enumerate(slabs):
            s = n % NRING
            count[s] = count.get(s, 0) + 16 * len(parts)
            place.append(slot(s)[:, 0:kc * w].rearrange("p (c n) -> p c n", n=w))
            place_r.append(ring_r[s][:, 0:kc * w].rearrange("p (c n) -> p c n", n=w))
            landed.append((f"slab_in{s}", count[s]))
            free.append(owner.get(s))
            owner[s] = f
        FIRST = {}
        n = 0
        for name, k in (("ada", 24), ("gla", 6), ("gla_out", 2), ("ffn0", 11), ("ffn0_out", 8), ("na", 6), ("na_out", 2),
                        ("ffn1", 11), ("ffn1_out", 8), ("in2", 8), ("out2", 2)):
            FIRST[name] = n
            n += k
        assert n == len(slabs)


        def eslot(b, part):
            i = 3 * b + part if (b == 0 and part < 2) else (3 * b - 1 + part if part < 2 else 3 * b + 4)
            return i % 6, i // 6
        e_in = [f"expert_in{i}" for i in range(6)]

        sems = S
        block = ctx.enter_context(nc.Block())

        class G:
            T, DV, m0, nc_, tail, scale, base = TT, 256, 0, 8, None, 1.0 / GATE_NORM, 0
            q = staticmethod(lambda h: g_qk[:, h, :])
            k = staticmethod(lambda h, dr: g_qk[:, 4 + h, :])
            S, tm, tg, tb, e2, e3, e5, att, kdt, dm, dk = g_S, g_tm, g_tg, g_tb, g_e2, g_e3, g_e5, g_att, g_kdt, g_dm, g_dk
            scan = kg[:, KG["scan"][0]:KG["scan"][0] + TT]
            tiles = [(128 * i, 128) for i in range(4)]
            chunks = [(CH * c, CH, c // 2, CH * (c % 2)) for c in range(8)]
            order = [[4, 5, 6, 7, 0, 1, 2, 3], [7, 6, 5, 4, 3, 2, 1, 0]]
            v = staticmethod(lambda tt, p0, n, h, e: g_v[p0:p0 + n, tt, 256 * h + 128 * e:256 * h + 128 * e + 128])
            vv = staticmethod(lambda tt, p0, n, h: g_v[p0:p0 + n, tt, 256 * h:256 * h + 256])
            o = staticmethod(lambda h, e: g_qk[:, 4 * e + h, :])
            y = staticmethod(lambda h, e: g_qk[:, 4 * e + h, :])
            gain = staticmethod(lambda h, e: col("gng", e))
            gate = staticmethod(lambda h, e: g_sr[:, e, :])
            norm = staticmethod(lambda h: f"gla{h}")

        class H:
            T, DV, m0, nc_, tail, scale, base = T2, 128, N_META, 4, (0, N_META), 1.0, 8
            q = staticmethod(lambda h: q_q[:, h, :])
            k = staticmethod(lambda h, dr: q_k[:, 4 * dr + h, :])
            S, tm, tg, tb, e2, e3, e5, att, kdt, dm, dk = q_S, q_tm, q_tg, q_tb, q_e2, q_e3, q_e5, q_att, q_kdt, q_dm, q_dk
            scan = q_scan
            tiles = [(N_META, 128), (N_META + 128, 128), (0, N_META)]
            chunks = [(N_META + CH * c, CH, c // 2, CH * (c % 2)) for c in range(4)] + [(0, N_META, 2, 0)]
            order = [[4, 0, 1, 2, 3], [3, 2, 1, 0, 4]]
            v = staticmethod(lambda tt, p0, n, h, e: q_v[p0:p0 + n, tt, 128 * h:128 * h + 128])
            vv = staticmethod(lambda tt, p0, n, h: q_v[p0:p0 + n, tt, 128 * h:128 * h + 128])
            o = staticmethod(lambda h, e: y_cat[:, 4 + h, :])
            y = staticmethod(lambda h, e: y_cat[:, 4 + h, :])
            gain = staticmethod(lambda h, e: col("hgn", h))
            gate = staticmethod(lambda h, e: q_g[:, h, :])
            norm = staticmethod(lambda h: f"hgrn{h}")

        NU = {G: 7, H: 4}

        def u_ahead(cf, hd):
            return (0 if cf is G else 8 * NU[G]) + hd * NU[cf]

        norms = {}
        seen = [0, 0]

        def two(h, dr):
            return 2 * (h % 2) + dr

        def norm_plan(name, chunks):
            norms[name] = (seen[0], seen[1])
            seen[0] += chunks
            seen[1] += 1
        norm_plan("n1_0", DC)
        for h in range(HEADS):
            norm_plan(f"gla{h}", 2)
        for name in ("n2_0", "n1_1", "n2_1", "fin", "mix"):
            norm_plan(name, DC)
        for h in range(HEADS):
            norm_plan(f"hgrn{h}", 1)
        norm_plan("hyena", HC)
        norm_plan("nffn", DC)
        norm_plan("nfin", DC)

        @block.sync
        def _(sp):
            for n, (parts, kc, w, f) in enumerate(slabs):
                if free[n]:
                    sp.wait_ge(S[free[n][0]], free[n][1])
                for o, wd, view in parts:
                    sp.dma_start(place[n][:, :, o:o + wd], view).then_inc(S[landed[n][0]], 16)

            def expert_slab(e, b, part, wait):
                s, k = eslot(b, part)
                dst = slot(s)
                src = [d["w_gate_2"], d["w_up_2"], d["w_down_2"]][part]
                if part < 2:
                    v = src[e, :, :].rearrange("(c p) n -> p c n", p=P)
                    dv = dst.rearrange("p (c n) -> p c n", n=DE)
                else:
                    v = src[e, :, :].rearrange("(c p) n -> p c n", p=P)
                    dv = dst.rearrange("p (c n) -> p c n", n=D)
                wait()
                sp.dma_start(dv, v).then_inc(S[e_in[s]], 16)

            def before_load(b, part):
                s, k = eslot(b, part)
                if k == 0:
                    if s < NRING:
                        last = max(i for i in range(len(slabs)) if i % NRING == s)
                        return lambda: sp.wait_ge(S[slabs[last][3][0]], slabs[last][3][1])
                    return lambda: sp.wait_ge(S["hyena_done"], 1)
                return None

            def used(b, part):
                i = 0 if (b, part) == (0, 0) else 1 if (b, part) == (0, 1) else (3 * b - 1 + part if part < 2 else 3 * b + 4)
                j = i - 6
                if j == 0 or j == 1:
                    return ("gu_mm", 1)
                bb, rr = divmod(j - 2, 3)
                return ("gu_mm", bb + 2) if rr < 2 else ("down_mm", bb + 1)

            def load(e, b, part):
                w = before_load(b, part)
                if w is None:
                    name, val = used(b, part)
                    w = lambda: sp.wait_ge(S[name], val)
                expert_slab(e, b, part, w)

            load(0, 0, 0)
            load(0, 0, 1)
            for b in range(2):
                load(b + 1, b + 1, 0)
                load(b + 1, b + 1, 1)
                load(b, b, 2)

            LOOPS = (NE - 4) // 2
            with sp.Fori(0, LOOPS) as i:
                for j in range(2):
                    b = 2 + j
                    for e0, part in ((b + 1, 0), (b + 1, 1), (b, 2)):
                        name, val = used(e0, part)
                        expert_slab(2 * i + e0, e0, part,
                                    lambda: sp.wait_ge(S[name], 2 * i + val))
            for b in range(2 + 2 * LOOPS, NE):
                for bb, part in ((b + 1, 0), (b + 1, 1), (b, 2)):
                    if bb < NE:
                        load(bb, bb, part)
            sp.wait_ge(S["tables"], 1)
            table = r_ti.bitcast(I32)
            n_extra = sp.value_load(table[0:1, 2 * NB:2 * NB + 1], min_val=0, max_val=EXTRA)
            with sp.Fori(0, EXTRA) as j:
                with sp.If(j < n_extra):
                    e = sp.value_load(table[0:1, bass.ds(j + NB + NE, 1)], min_val=0, max_val=NE - 1)
                    sp.wait_ge(S["extra_free"], j + 1)
                    for part, src in enumerate((d["w_gate_2"], d["w_up_2"], d["w_down_2"])):
                        v = src[bass.ds(e, 1), :, :].rearrange("o (c p) n -> p (o c) n", p=P)
                        sp.dma_start(slot(part).rearrange("p (c n) -> p c n", n=src.shape[2]), v).then_inc(S["extra_in"], 16)

        @block.gpsimd
        def _(pool):
            pool.dma_start(xT[:, :, :], d["xT"].rearrange("(c p) t -> p c t", p=P)).then_inc(S["x_in"], 16)
            for i, n in enumerate((1024, 256, 128, 512)):
                pool.memset(ones[:, i, :], 1.0 / n).then_inc(S["ones_set"], 1)
            pool.memset(one1[:, :], 1.0).then_inc(S["ones_set"], 1)
            pool.memset(eps[:, :], EPS).then_inc(S["ones_set"], 1)
            pool.wait_ge(S["ffn_out_x"], 2 * DC)
            pool.memset(n_bias[:, :, :], 0.0).then_inc(S["zeroed"], 1)
            pool.wait_ge(S["zeroed"], 1)
            for i in range(2 * NA_H):
                if i >= 4:
                    pool.wait_ge(S["na_add"], i - 3)
                pool.dma_start(n_bias[:, i % 4, 0:NT], d["na_bias"][i // 2, i % 2]).then_inc(S[f"na_bias_in{i % 4}"], 16)
            pool.wait_ge(S["ffn_out_mm"], 2 * DC)
            pool.dma_start(zT[:, :, 0:N_META], d["metaT"].rearrange("(c p) t -> p c t", p=P)).then_inc(S["meta_in"], 16)
            pool.wait_ge(S["ffn_out_x"], 3 * DC)
            pool.dma_start(q_scan, d["k_scan2"]).then_inc(S["b2_in"], 16)
            pool.wait_ge(S["fin_h"], DC)
            for i, (t0, n) in enumerate(TTILE):
                pool.dma_start(w_dft[0:n, i, :], d["k_dft"][t0:t0 + n, :]).then_inc(S["dft_in"], 16)
            for i in range(6):
                f0, n = FT[i % 3]
                pool.dma_start(w_inv[0:n, i, :], d["k_idft"][(i // 3) * NF + f0:(i // 3) * NF + f0 + n, :]).then_inc(S["dft_in"], 16)
            pool.wait_ge(S["gate_y"], 8 + 4)
            for i, (t0, n) in enumerate(TTILE):
                pool.dma_start(win[0:n, i, :, :], d["k_win"][t0:t0 + n, :, :]).then_inc(S["filt_in"], 16)
            pool.dma_start(fw3[0:HID, :, :], d["filt_w3_2"].rearrange("p (a n) -> p a n", n=HY)).then_inc(S["filt_in"], 16)
            pool.dma_start(f_z[0:EMB, :], d["k_zT"]).then_inc(S["filt_in"], 16)
            pool.dma_start(f_w12[0:EMB, 0, :], d["filt_w1_2"]).then_inc(S["filt_in"], 16)
            pool.dma_start(f_w12[0:HID, 1, :], d["filt_w2_2"]).then_inc(S["filt_in"], 16)
            pool.wait_ge(S["proj_x"], 4 * DC)
            pool.dma_start(kr, d["k_route"]).then_inc(S["route_in"], 16)
            pool.dma_start(wr, d["w_route"].rearrange("(c p) n -> p c n", p=P)).then_inc(S["route_in"], 16)
            pool.memset(xg[:, :, SLOTS:SLOTS + WIN], 0.0).then_inc(S["zeroed"], 1)
            pool.memset(r_lg, 0.0).then_inc(S["zeroed"], 1)

        @block.tensor
        def _(pe):
            mm = pe.matmul

            def got(n):
                pe.wait_ge(S[landed[n][0]], landed[n][1])
                return place[n]

            def norm_chunk(name, c, chunks, bank, T, n):
                q0, _ = norms[name]
                pe.wait_ge(S["sq_ready"], q0 + c + 1)
                mm(pb[bank][:, 0:T], ON[n], sq[:, (q0 + c) % 2, 0:T], start=c == 0, stop=c == chunks - 1).then_inc(S["sq_used"], 1)

            def norm_sum(name, chunks, bank, T, n):
                for c in range(chunks):
                    norm_chunk(name, c, chunks, bank, T, n)

            def residual_norm(name, m, T):
                if m >= 1:
                    norm_chunk(name, m - 1, DC, 7, T, 1024)
                if m == DC - 1:
                    norm_chunk(name, m, DC, 7, T, 1024)

            def split_mm(out, w_hi_, w_lo_, x_hi_, x_lo_, start, stop):
                mm(out, w_hi_, x_hi_, start=start, stop=False)
                mm(out, w_hi_, x_lo_, start=False, stop=False)
                return mm(out, w_lo_, x_hi_, start=False, stop=stop)

            def ffn(l, T, norm):
                n0, m0 = FIRST[f"ffn{l}"], FIRST[f"ffn{l}_out"]
                for i in range(FC):
                    wl = halves_of(place_r[n0 + i // 2], i % 2)
                    pe.wait_ge(S["w_lo"], W_STEPS * l + i + 1)
                    for a in range(2):
                        b = (2 * i + a) % 8
                        if i >= 4:
                            pe.wait_ge(S["ffn_act" if a else "ffn_conv"], 22 * l + i - 3)
                        for c in range(DC):
                            if i + a == 0:
                                pe.wait_ge(S["h_lo"], DC * l + c + 1)
                            last = split_mm(pb[b][:, 0:T], w_hi[i % 3][:, c, a, :], wl[:, c, a, :], h_hi[:, c, 0:T], hT_r[:, c, 0:T],
                                            c == 0, c == DC - 1)
                        last.then_inc(S["ffn_in_mm"], 1)
                pe.wait_ge(S["ffn_act"], 22 * l + FC)
                halves = 2 if T == TT else 1
                for m in range(DC):
                    pe.wait_ge(S["w_lo"], W_STEPS * l + FC + m + 1)
                    if m >= 4:
                        pe.wait_ge(S["ffn_out_x"], 16 * l + halves * (m - 3))
                    for c in range(FC):
                        if m == 0:
                            pe.wait_ge(S["f_lo"], FC * l + c + 1)
                        last = split_mm(pb[m % 4][:, 0:T], wo_hi[m % 2][:, c, :], place_r[m0 + m][:, c, :], f_hi(c, T), f_lo[:, c, 0:T],
                                        c == 0, c == FC - 1)
                    last.then_inc(S["ffn_out_mm"], 1)
                    residual_norm(norm, m, T)

            def project(slab, src, T, ahead, per, norm):
                for m in range(DC):
                    w = got(FIRST[slab] + m // 4)
                    if m >= 4:
                        pe.wait_ge(S["proj_x"], ahead + per * (m - 3))
                    for c in range(DC):
                        last = mm(pb[m % 4][:, 0:T], w[:, c, 128 * (m % 4):128 * (m % 4) + 128], src(c),
                                  start=c == 0, stop=c == DC - 1)
                    last.then_inc(S["proj_mm"], 1)
                    residual_norm(norm, m, T)

            pe.wait_ge(S["ka_in"], 16)
            pe.wait_ge(S["sc_ready"], 1)

            def ada_turn(g):
                pe.wait_ge(S["ada_row"], g + 1)
                for j in range(4):
                    o = (4 * (g % 12) + j) * 2
                    last = pe.transpose(pb[2 + g // 12][:, o:o + 2], ada_row[:, g % 2, 128 * j:128 * j + 128], ident[0:2, 0:2])
                last.then_inc(S["ada_tr"], 1)
            for g in range(24):
                w = got(FIRST["ada"] + g)
                if g >= 2:
                    pe.wait_ge(S["ada_row"], g - 1)
                for c in range(DC):
                    last = mm(pb[g % 2][0:2, :], sc[:, 2 * c:2 * c + 2], w[:, c, :], start=c == 0, stop=c == DC - 1)
                last.then_inc(S["ada_mm"], 1)
                if g >= 1:
                    ada_turn(g - 1)
            ada_turn(23)

            pe.wait_ge(S["ones_set"], 6)
            norm_sum("n1_0", DC, 4, TT, 1024)
            pe.wait_ge(S["mod_h"], DC)
            pe.wait_ge(S["mod_ready"], 2)

            def rope_turn(u):
                pe.wait_ge(S["gla_qk_ev"], u + 1)
                if u >= 2:
                    pe.wait_ge(S["rope_s"], u - 1)
                mm(pb[4 + u % 2][:, 0:NT], kg[:, 0:128], g_qk[:, u, 0:NT], start=True, stop=True).then_inc(S["rope_mm"], 1)
            pe.wait_ge(S["gla_in"], 80)
            for u in range(8):
                w = got(FIRST["gla"] + u // 4)
                if u >= 4:
                    pe.wait_ge(S["gla_qk_ev"], u - 3)
                for c in range(DC):
                    last = mm(pb[u % 4][:, :], w[:, c, 128 * (u % 4):128 * (u % 4) + 128], hT[:, c, :], start=c == 0, stop=c == DC - 1)
                last.then_inc(S["gla_qk_mm"], 1)
                if u >= 1:
                    rope_turn(u - 1)
            rope_turn(7)
            pe.wait_ge(S["gla_qk_ev"], 8)
            for u in range(8):
                w = got(FIRST["gla"] + 2 + u // 4)
                if u >= 4:
                    pe.wait_ge(S["gla_v_ev"], u - 3)
                for c in range(DC):
                    last = mm(pb[u % 4][:, :], hT[:, c, 128 * (u % 4):128 * (u % 4) + 128], w[:, c, :], start=c == 0, stop=c == DC - 1)
                last.then_inc(S["gla_v_mm"], 1)
            pe.wait_ge(S["rope_s"], 8)
            for dr in range(2):
                for c in range(DC):
                    last = mm(pb[6 + dr][32 * dr:32 * dr + 16, :], g_aw1[:, dr, c, :], hT[:, c, :], start=c == 0, stop=c == DC - 1)
                last.then_inc(S["low_mm"], 1)
            pe.wait_ge(S["low_ev"], 2)
            pe.wait_ge(S["gla_v_ev"], 8)

            def gate_logits(hd):
                h, dr = hd // 2, hd % 2
                if hd >= 1:
                    pe.wait_ge(S["gl_min"], hd)
                mm(pb[0][:, :], g_aw2[32 * dr:32 * dr + 16, 128 * h:128 * h + 128], g_low[32 * dr:32 * dr + 16, :], start=True, stop=True)\
                    .then_inc(S["gl_mm"], 1)

            def scan_head(cf, hd):
                h, dr, p = hd // 2, hd % 2, hd % 2
                n = cf.base + hd
                pe.wait_ge(S["decayed"], 6 * (n + 1))
                if n >= 1:
                    pe.wait_ge(S["att_cp"], n)
                for tt, (t0, m) in enumerate(cf.tiles):
                    last = mm(pb[2][0:m, P * tt:P * tt + m], cf.e2[:, p, t0:t0 + m], cf.tg[:, p, t0:t0 + m], start=True, stop=True)
                if n >= 1:
                    pe.wait_ge(S["kd_cp"], n)
                if hd >= 3 and dr:
                    pe.wait_ge(S["rs_sqrt"], norms[cf.norm(h - 1)][1] + 1)
                for i, (t0, m) in enumerate(cf.tiles):
                    last = pe.transpose(pb[3][0:m, 128 * i:128 * i + 128], cf.tm[:, p, t0:t0 + m], ident)
                last.then_inc(S["kd_tr"], 1)
                if cf is G and h >= 1:
                    pe.wait_ge(S["o_ev"], 2 * h)
                for tt, (t0, m) in enumerate(cf.tiles[:cf.nc_ // 2]):
                    last = mm(pb[7][0:m, P * tt:P * tt + m], cf.dk[:, p, t0:t0 + m], cf.dm[:, p, t0:t0 + m], start=True, stop=True)
                last.then_inc(S["att_mm"], 1)

            def scan_norm(cf, h, hd):
                pe.wait_ge(S["kd_cp"], cf.base + hd + 1)
                norm_sum(cf.norm(h), cf.DV // 128, 3, cf.T, cf.DV)

            def scan_updates(cf, hd):
                h, dr = hd // 2, hd % 2
                pe.wait_ge(S["kd_cp"], cf.base + hd + 1)
                for i, c in enumerate(cf.order[dr][:-1]):
                    _, m, tt, p0 = cf.chunks[c]
                    u = u_ahead(cf, hd) + i
                    if u >= 2:
                        pe.wait_ge(S["state"], u - 1)
                    mm(pb[4 + u % 2][:, 0:cf.DV], cf.kdt[p0:p0 + m, tt, :], cf.vv(tt, p0, m, h), start=True, stop=True)\
                        .then_inc(S["u_mm"], 1)

            def scan_out(cf, h):
                pe.wait_ge(S["att_cp"], cf.base + 2 * h + 2)
                pe.wait_ge(S["state"], u_ahead(cf, 2 * h + 2))
                no = h if cf is G else HEADS + h
                for e in range(cf.DV // 128):
                    if no >= 1 and e == 0:
                        pe.wait_ge(S["o_ev"], 2 * h if cf is G else 8 + h)
                    for tt, (t0, tn) in enumerate(cf.tiles):
                        terms = [(t0, tn, cf.v(tt, 0, tn, h, e), cf.att[0:tn, dr, P * tt:P * tt + tn]) for dr in range(2)]
                        for ci, (c0, m, ct, _) in enumerate(cf.chunks):
                            for dr in range(2):
                                if ct == tt and ci != cf.order[dr][0]:
                                    terms.append((c0, m, cf.S[:, dr, ci, 128 * e:128 * e + 128], cf.e3[:, two(h, dr), c0:c0 + m]))
                        for i, (c0, m, l, r) in enumerate(terms):
                            last = mm(pb[6 + e][:, c0:c0 + m], l, r, start=i == 0, stop=i == len(terms) - 1, skip_group_check=True)
                last.then_inc(S["o_mm"], 1)

            gate_logits(0)
            gate_logits(1)
            for hd in range(8):
                scan_head(G, hd)
                if hd + 2 < 8:
                    gate_logits(hd + 2)
                if hd >= 1:
                    pe.wait_ge(S["gla_r_ev"], hd)
                w = got(FIRST["gla"] + 4 + hd // 4)
                for c in range(DC):
                    last = mm(pb[1][:, :], w[:, c, 128 * (hd % 4):128 * (hd % 4) + 128], hT[:, c, :], start=c == 0, stop=c == DC - 1)
                last.then_inc(S["gla_r_mm"], 1)
                if hd >= 2 and hd % 2 == 0:
                    scan_norm(G, hd // 2 - 1, hd)
                scan_updates(G, hd)
                if hd % 2:
                    scan_out(G, hd // 2)
            scan_norm(G, HEADS - 1, 7)
            pe.wait_ge(S["gate_y"], 8)
            project("gla_out", lambda k: g_qk[:, 4 * (k % 2) + k // 2, :], TT, 0, 2, "n2_0")
            pe.wait_ge(S["proj_x"], 2 * DC)
            pe.wait_ge(S["rs_sqrt"], norms["n2_0"][1] + 1)
            ffn(0, TT, "n1_1")

            pe.wait_ge(S["rs_sqrt"], norms["n1_1"][1] + 1)
            pe.wait_ge(S["ffn_out_x"], 2 * DC)
            for part, (name, T) in enumerate((("na_q", NT), ("na_k", TT))):
                for u in range(8):
                    w = got(FIRST["na"] + 2 * part + u // 4)
                    if u >= 4:
                        pe.wait_ge(S[name + "_ev"], u - 3)
                    elif part:
                        pe.wait_ge(S["na_q_ev"], u + 5)
                    for c in range(DC):
                        if part + u == 0:
                            pe.wait_ge(S["mod_h"], 2 * DC + c + 1)
                        last = mm(pb[u % 4][:, 0:T], w[:, c, 128 * (u % 4):128 * (u % 4) + 128], hT[:, c, 0:T], start=c == 0, stop=c == DC - 1)
                    last.then_inc(S[name + "_mm"], 1)
            for u in range(8):
                w = got(FIRST["na"] + 4 + u // 4)
                if u >= 4:
                    pe.wait_ge(S["na_v_ev"], u - 3)
                else:
                    pe.wait_ge(S["na_k_ev"], u + 5)
                for c in range(DC):
                    last = mm(pb[u % 4][:, :], hT[:, c, 128 * (u % 4):128 * (u % 4) + 128], w[:, c, :], start=c == 0, stop=c == DC - 1)
                last.then_inc(S["na_v_mm"], 1)
            pe.wait_ge(S["na_v_ev"], 8)

            def na_scores(i):
                h, qt = i // 2, i % 2
                p0 = 64 * (h % 2)
                if i >= 3:
                    pe.wait_ge(S["na_add"], i - 2)
                mm(NA_BANK[i % 3][:, :], n_q[p0:p0 + 64, h // 2, 128 * qt:128 * qt + 128], n_k[p0:p0 + 64, h // 2, :], start=True, stop=True)\
                    .then_inc(S["na_s_mm"], 1)

            def na_out(i):
                h = i // 2
                pe.wait_ge(S["na_pt"], i + 1)
                if i >= 2:
                    pe.wait_ge(S["na_o_ev"], i - 1)
                p0 = 64 * (h % 2)
                for k in range(4):
                    last = mm(pb[4 + i % 2][p0:p0 + 64, 0:128], n_v[:, k, 64 * h:64 * h + 64], n_pt[:, i % 2, 128 * k:128 * k + 128], start=k == 0, stop=k == 3)
                last.then_inc(S["na_o_mm"], 1)
            na_scores(0)
            na_scores(1)
            for i in range(2 * NA_H):
                if i + 2 < 2 * NA_H:
                    na_scores(i + 2)
                pe.wait_ge(S["na_p"], i + 1)
                if i >= 2:
                    pe.wait_ge(S["na_pt"], i - 1)
                for k in range(4):
                    last = pe.transpose(pb[2 + i % 2][:, 128 * k:128 * k + 128], n_s[:, i % 3, 128 * k:128 * k + 128], ident)
                last.then_inc(S["na_tr"], 1)
                if i >= 1:
                    na_out(i - 1)
            na_out(2 * NA_H - 1)
            pe.wait_ge(S["na_o_ev"], 2 * NA_H)
            project("na_out", lambda k: n_o[:, k, :], NT, 2 * DC, 1, "n2_1")
            pe.wait_ge(S["proj_x"], 3 * DC)
            pe.wait_ge(S["rs_sqrt"], norms["n2_1"][1] + 1)
            ffn(1, NT, "fin")

            pe.wait_ge(S["ffn_out_x"], 3 * DC)
            pe.wait_ge(S["rs_sqrt"], norms["fin"][1] + 1)
            norm_sum("mix", DC, 7, T2, 1024)
            pe.wait_ge(S["rs_sqrt"], norms["mix"][1] + 1)

            def in2(slab, units, name, ev, prev, ahead=0):
                for u in range(units):
                    w = got(FIRST["in2"] + slab + u // 4)
                    if u >= 4:
                        pe.wait_ge(S[ev], ahead + u - 3)
                    elif prev:
                        pe.wait_ge(S[prev[0]], prev[1] - 3 + u)
                    for c in range(DC):
                        if slab + u == 0:
                            pe.wait_ge(S["mix_h"], c + 1)
                        last = mm(pb[u % 4][:, 0:T2], w[:, c, 128 * (u % 4):128 * (u % 4) + 128], h2T[:, c, :], start=c == 0, stop=c == DC - 1)
                    last.then_inc(S[name], 1)
            in2(0, 12, "hy_mm", "hy_conv", None)
            in2(3, 4, "hg_mm", "hg_ev", ("hy_conv", 12))
            in2(4, 8, "hg_mm", "hg_ev", ("hg_ev", 4), 4)
            pe.wait_ge(S["hg_ev"], 12)
            w = got(FIRST["in2"] + 6)
            for u, (t0, m) in enumerate(H.tiles):
                for c in range(DC):
                    last = mm(pb[u][0:m, :], h2T[:, c, t0:t0 + m], w[:, c, :], start=c == 0, stop=c == DC - 1)
                last.then_inc(S["hg_v_mm"], 1)
            pe.wait_ge(S["hg_v_ev"], 3)
            in2(7, 4, "hg_mm", "hg_ev", None, 12)
            pe.wait_ge(S["hg_ev"], 16)
            for hd in range(8):
                scan_head(H, hd)
                if hd >= 2 and hd % 2 == 0:
                    scan_norm(H, hd // 2 - 1, hd)
                scan_updates(H, hd)
                if hd % 2:
                    scan_out(H, hd // 2)
            scan_norm(H, HEADS - 1, 7)
            pe.wait_ge(S["rs_sqrt"], norms["hgrn3"][1] + 1)

            pe.wait_ge(S["filt_in"], 7 * 16)
            pe.wait_ge(S["att_cp"], 16)
            mm(pb[0][0:HID, 0:T2], f_w12[0:EMB, 0, :], f_z[0:EMB, :], start=True, stop=True).then_inc(S["filt_mm"], 1)
            pe.wait_ge(S["filt_sin"], 1)
            mm(pb[1][0:HID, 0:T2], f_w12[0:HID, 1, :], f_h[0:HID, :], start=True, stop=True).then_inc(S["filt_mm"], 1)
            pe.wait_ge(S["filt_sin"], 2)
            pe.wait_ge(S["dft_in"], 9 * 16)
            for od in range(2):
                for i, (t0, n) in enumerate(TTILE):
                    g = 3 * od + i
                    if g >= 1:
                        pe.wait_ge(S["filt_hd"], g)
                    for dr in range(2):
                        last = mm(pb[2 + dr][0:n, :], f_h[0:HID, t0:t0 + n], fw3[0:HID, 2 * dr + od, :], start=True, stop=True)
                    last.then_inc(S["filt3_mm"], 1)
                pe.wait_ge(S["filt_hd"], 3 * od + 3)
                for i in range(6):
                    f0, m = FT[i % 3]
                    src = f_hs if i < 3 else f_hd
                    g = 6 * od + i
                    if g >= 2:
                        pe.wait_ge(S["spec_ev"], g - 1)
                    for k, (t0, n) in enumerate(TTILE):
                        last = mm(pb[4 + g % 2][0:m, :], w_dft[0:n, k, (i // 3) * NF + f0:(i // 3) * NF + f0 + m], src[0:n, k, :], start=k == 0, stop=k == 2)
                    last.then_inc(S["spec_mm"], 1)
            pe.wait_ge(S["spec_ev"], 12)
            for od in range(2):
                if od:
                    pe.wait_ge(S["hy_z"], HC)
                for i, (t0, n) in enumerate(TTILE):
                    for c in range(HC):
                        last = pe.transpose(pb[i][0:n, 128 * c:128 * c + 128], hy_u[:, c, t0:t0 + n], ident)
                    last.then_inc(S["u_tr"], 1)
                for i in range(3):
                    f0, m = FT[i]
                    pe.wait_ge(S["u_cp"], 3 * od + 3)
                    for ri in range(2):
                        b = 3 + 2 * (i % 2) + ri
                        g = 3 * od + i
                        if i == 2 or od:
                            pe.wait_ge(S["yf"], 3 * od + (i - 1 if i == 2 else 0))
                        for k, (t0, n) in enumerate(TTILE):
                            last = mm(pb[b][0:m, :], w_dft[0:n, k, ri * NF + f0:ri * NF + f0 + m], u_tok[0:n, k, :], start=k == 0, stop=k == 2)
                    last.then_inc(S["dft_mm"], 1)
                pe.wait_ge(S["yf"], 3 * od + 3)
                for c in range(HC):
                    for i in range(6):
                        f0, m = FT[i % 3]
                        last = mm(pb[c][:, 0:T2], yf[0:m, i, 128 * c:128 * c + 128], w_inv[0:m, i, :], start=i == 0, stop=i == 5)
                    last.then_inc(S["idft_mm"], 1)
            pe.wait_ge(S["hy_z"], 2 * HC)
            norm_sum("hyena", HC, 7, T2, 512)
            pe.wait_ge(S["rs_sqrt"], norms["hyena"][1] + 1)
            pe.wait_ge(S["hyena_y"], HC)
            project("out2", lambda k: y_cat[:, k, :], T2, 3 * DC, 1, "nffn")
            pe.wait_ge(S["proj_x"], 4 * DC)

            pe.wait_ge(S["rs_sqrt"], norms["nffn"][1] + 1)
            for i, (t0, n) in enumerate(TTILE):
                for hf in range(2):
                    for c in range(4):
                        if i == 0:
                            pe.wait_ge(S["nffn_h"], 4 * hf + c + 1)
                        last = pe.transpose(pb[2 * i + hf][0:n, 128 * c:128 * c + 128], h2T[:, 4 * hf + c, t0:t0 + n], ident)
                    last.then_inc(S["h2_tr"], 1)
            pe.wait_ge(S["route_in"], 32)
            for i, (t0, n) in enumerate(TTILE):
                for c in range(DC):
                    last = mm(pb[7][0:n, 72 * i:72 * i + 72], h2T[:, c, t0:t0 + n], wr[:, c, :], start=c == 0, stop=c == DC - 1)
            last.then_inc(S["route_mm"], 1)
            pe.wait_ge(S["route_M"], 1)
            pe.wait_ge(S["h2_cp"], 6)
            for i in range(3):
                for j in range(i + 1):
                    last = mm(pb[6][:, 64 * i:64 * i + 64], striu if j == i else one1[:, :], r_M[:, 2, j, :], start=j == 0, stop=j == i)
            for j in range(3):
                last = mm(pb[6][:, 192:256], one1[:, :], r_M[:, 2, j, :], start=j == 0, stop=j == 2)
            last.then_inc(S["pos_mm"], 1)
            pe.wait_ge(S["route_S"], 1)
            for c in range(DC):
                for hf in range(2):
                    g = 2 * c + hf
                    if g >= 4:
                        pe.wait_ge(S["xg_ev"], g - 3)
                    for k, (t0, n) in enumerate(TTILE):
                        last = mm(pb[g % 4][:, 0:T2], r_h2[0:n, k, 128 * c:128 * c + 128], r_S[0:n, k, T2 * hf:T2 * hf + T2], start=k == 0, stop=k == 2)
                    last.then_inc(S["xg_mm"], 1)
            pe.wait_ge(S["route_S"], 2)
            for s, (s0, m) in enumerate(STILE):
                if s >= 2:
                    pe.wait_ge(S["sgt_ev"], s - 1)
                for k, (t0, n) in enumerate(TTILE):
                    last = pe.transpose(pb[4 + s % 2][0:m, t0:t0 + n], r_Sg[0:n, k, s0:s0 + m], ident[0:n, 0:n])
                last.then_inc(S["sgt_tr"], 1)
            pe.wait_ge(S["xg_ev"], 16)
            pe.wait_ge(S["sgt_ev"], 5)

            pe.wait_ge(S["zeroed"], 4)

            def arrived(b, part, k):
                s, k0 = eslot(b, part)
                pe.wait_ge(S[e_in[s]], 16 * k + 16 * (k0 + 1))
                return slot(s)

            def gate_up(j, w):
                for c in range(DC):
                    for part in range(2):
                        last = mm(pb[j][64 * part:64 * part + 64, :], e_xw[:, j, c, :], w[part][:, c, :], start=c == 0, stop=c == DC - 1,
                                  skip_group_check=True)
                last.then_inc(S["gu_mm"], 1)

            def turn(j):
                for c in range(4):
                    last = pe.transpose(pb[4][:, 128 * c:128 * c + 128], e_hid[:, j, 128 * c:128 * c + 128], ident)
                last.then_inc(S["hid_tr"], 1)

            def down(j, w):
                for c in range(4):
                    for hf in range(2):
                        last = mm(pb[5 + j][64 * hf:64 * hf + 64, :], e_hT[:, j, c, :], w[:, c, 512 * hf:512 * hf + 512], start=c == 0, stop=c == 3,
                                  skip_group_check=True)
                last.then_inc(S["down_mm"], 1)

            def gate_up_pass(b, j, k, i=0):
                pe.wait_ge(S["xw"], i + b + 1)
                w = [arrived(b, part, k).rearrange("p (c n) -> p c n", n=DE) for part in range(2)]
                if b >= 2:
                    pe.wait_ge(S["hid"], i + b - 1)
                gate_up(j, w)

            def turn_pass(b, j, i=0):
                pe.wait_ge(S["hid"], i + b + 1)
                if b >= 1:
                    pe.wait_ge(S["hT_cp"], i + b)
                turn(j)

            def down_pass(b, j, k, i=0):
                w = arrived(b, 2, k).rearrange("p (c n) -> p c n", n=D)
                pe.wait_ge(S["hT_cp"], i + b + 1)
                if b >= 2:
                    pe.wait_ge(S["y_cp"], i + b - 1)
                down(j, w)
            gate_up_pass(0, 0, 0)
            for b in range(2):
                turn_pass(b, b % 2)
                gate_up_pass(b + 1, (b + 1) % 2, 0)
                down_pass(b, b % 2, 0)
            LOOPS = (NE - 4) // 2
            with pe.Fori(0, LOOPS) as i:
                for b in (2, 3):
                    turn_pass(b, b % 2, 2 * i)
                    gate_up_pass(b + 1, (b + 1) % 2, i, 2 * i)
                    down_pass(b, b % 2, i, 2 * i)
            for b in range(2 + 2 * LOOPS, NE):
                turn_pass(b, b % 2)
                if b + 1 < NE:
                    gate_up_pass(b + 1, (b + 1) % 2, 0)
                down_pass(b, b % 2, 0)
            n_extra = pe.value_load(r_ti.bitcast(I32)[0:1, 2 * NB:2 * NB + 1], min_val=0, max_val=EXTRA)
            with pe.Fori(0, EXTRA) as j:
                with pe.If(j < n_extra):
                    pe.wait_ge(S["extra_in"], 48 * j + 48)
                    pe.wait_ge(S["xw"], j + NE + 1)
                    gate_up(0, [slot(part).rearrange("p (c n) -> p c n", n=DE) for part in range(2)])
                    pe.wait_ge(S["hid"], j + NE + 1)
                    turn(0)
                    pe.wait_ge(S["hT_cp"], j + NE + 1)
                    down(0, slot(2).rearrange("p (c n) -> p c n", n=D))
            pe.wait_ge(S["ys_in"], 5 * 16)
            for m in range(DC):
                if m >= 4:
                    pe.wait_ge(S["moe_x"], m - 3)
                for s, (s0, n) in enumerate(STILE):
                    last = mm(pb[m % 4][:, 0:T2], y_s[0:n, s, 128 * m:128 * m + 128], r_SgT[0:n, s, :], start=s == 0, stop=s == len(STILE) - 1)
                last.then_inc(S["comb_mm"], 1)
                residual_norm("nfin", m, T2)

        @block.scalar
        def _(act):
            A = act.activation
            act.dma_start(cols[:, :], d["cols"]).then_inc(S["cols_in"], 16)
            act.dma_start(ka[:, :], d["k_a"]).then_inc(S["ka_in"], 16)
            act.dma_start(kg, d["k_g"]).then_inc(S["gla_in"], 16)
            act.dma_start(g_aw1[:, 0, :, :], d["gla_a_w1"][0].rearrange("(c p) n -> p c n", p=P)).then_inc(S["gla_in"], 16)
            act.dma_start(g_aw1[:, 1, :, :], d["gla_a_w1"][1].rearrange("(c p) n -> p c n", p=P)).then_inc(S["gla_in"], 16)
            for dr in range(2):
                act.dma_start(g_aw2[32 * dr:32 * dr + 16, :], d["gla_a_w2"][dr]).then_inc(S["gla_in"], 16)
            act.wait_ge(S["cols_in"], 16)
            A(sc[:, :], col("c2", 0, 2 * DC), ACT.Silu).then_inc(S["sc_ready"], 1)

            def copies(n, mmsem, evsem, bank, dst, func=ACT.Copy, scale=None, ahead=0):
                for u in range(n):
                    act.wait_ge(S[mmsem], ahead + u + 1)
                    o = dst(u)
                    b = bank(u)
                    A(o, b, func, **({} if scale is None else {"scale": scale(u)})).then_inc(S[evsem], 1)

            def square(q0, c, s, made=None):
                if made:
                    act.wait_ge(S[made[0]], made[1] + made[2] * (c + 1))
                if q0 + c >= 2:
                    act.wait_ge(S["sq_used"], q0 + c - 1)
                A(sq[:, (q0 + c) % 2, 0:s.shape[1]], s, ACT.Square).then_inc(S["sq_ready"], 1)

            def squares(name, chunks, src, made=None):
                q0, _ = norms[name]
                for c in range(chunks):
                    square(q0, c, src(c), made)

            def sqrt(name, chunks, bank, T):
                q0, i = norms[name]
                act.wait_ge(S["ones_set"], 6)
                act.wait_ge(S["sq_used"], q0 + chunks)
                if i >= 1:
                    act.wait_ge(S["norm_done"], i)
                A(rstd[:, 0:T], pb[bank][:, 0:T], ACT.Sqrt, bias=eps[:, 0:1]).then_inc(S["rs_sqrt"], 1)

            def h_rounded(l, c, T):
                act.wait_ge(S["mod_h"], DC * (2 * l + 1) + c + 1)
                A(h_hi[:, c, 0:T], hT[:, c, 0:T], ACT.Copy).then_inc(S["h_hi"], 1)

            def modulate(name, l, which, T):
                for c in range(DC):
                    act.wait_ge(S["mod_xr"], DC * (2 * l + which) + c + 1)
                    for hf in range(T // NT):
                        v = hT[:, c, NT * hf:NT * hf + NT]
                        last = A(v, v, ACT.Identity, bias=mod[:, l, 24 * which + c, hf:hf + 1], scale=modA[:, l, which, c, hf:hf + 1])
                    last.then_inc(S["mod_h"], 1)
                    if which and c >= 1:
                        h_rounded(l, c - 1, T)
                if which:
                    h_rounded(l, DC - 1, T)

            def ffn_w_in_hi(l, i):
                n = FIRST[f"ffn{l}"] + i // 2
                act.wait_ge(S[landed[n][0]], landed[n][1])
                if i >= 3:
                    act.wait_ge(S["ffn_in_mm"], 44 * l + 2 * (i - 2))
                A(w_hi[i % 3], halves_of(place[n], i % 2), ACT.Copy).then_inc(S["w_hi"], 1)

            def ffn_w_out_hi(l, m):
                n = FIRST[f"ffn{l}_out"] + m
                act.wait_ge(S[landed[n][0]], landed[n][1])
                if m < 2:
                    act.wait_ge(S["ffn_in_mm"], 44 * l + 42 + 2 * m)
                else:
                    act.wait_ge(S["ffn_out_mm"], 8 * l + m - 1)
                A(wo_hi[m % 2], place[n], ACT.Copy).then_inc(S["w_hi"], 1)

            def ffn_out_prepared(l, T):
                ffn_w_out_hi(l, 0)
                act.wait_ge(S["ffn_in_mm"], 44 * (l + 1))
                act.wait_ge(S["ffn_act"], 22 * (l + 1))
                for c in range(FC):
                    A(f_hi(c, T), f_act[:, c, 0:T], ACT.Copy).then_inc(S["f_hi"], 1)
                ffn_w_out_hi(l, 1)

            def ffn_out(l, T, name, made):
                q0, _ = norms[name]
                for m in range(DC):
                    if m + 2 < DC:
                        ffn_w_out_hi(l, m + 2)
                    square(q0, m, xT[:, m, 0:T], made)

            def ffn(l, T):
                for i in range(FC):
                    j, u = i // 2, i % 2
                    if i + 2 < FC:
                        ffn_w_in_hi(l, i + 2)
                    act.wait_ge(S["ffn_in_mm"], 44 * l + 4 * j + 2 * u + 1)
                    if i >= 4:
                        act.wait_ge(S["ffn_act"], 22 * l + i - 3)
                    A(f_t1[:, i % 4, 0:T], pb[(4 * j + 2 * u) % 8][:, 0:T], ACT.Identity, bias=col("fcb", FC * l + i),
                      scale=col("fcw", (3 * l + 1) * FC + i)).then_inc(S["ffn_mid"], 1)
                    act.wait_ge(S["ffn_conv"], 22 * l + i + 1)
                    A(f_t1[:, i % 4, 0:T], f_t1[:, i % 4, 0:T], ACT.Silu).then_inc(S["ffn_silu"], 1)
                ffn_out_prepared(l, T)

            for g in range(24):
                act.wait_ge(S["ada_mm"], g + 1)
                if g >= 2:
                    act.wait_ge(S["ada_tr"], g - 1)
                A(ada_row[:, g % 2, :], pb[g % 2][0:2, :], ACT.Copy).then_inc(S["ada_row"], 1)
            act.wait_ge(S["x_in"], 16)
            squares("n1_0", DC, lambda c: xT[:, c, :])
            sqrt("n1_0", DC, 4, TT)
            act.wait_ge(S["mod_ready"], 2)
            modulate("n1_0", 0, 0, TT)
            copies(8, "gla_qk_mm", "gla_qk_ev", lambda u: pb[u % 4][:, :], lambda u: g_qk[:, u, :], scale=lambda u: 128.0 ** -0.5 if u < 4 else 1.0)
            copies(8, "gla_v_mm", "gla_v_ev", lambda u: pb[u % 4][:, :], lambda u: g_v[:, u % 4, 512 * (u // 4):512 * (u // 4) + 512])
            copies(2, "low_mm", "low_ev", lambda u: pb[6 + u][32 * u:32 * u + 16, :], lambda u: g_low[32 * u:32 * u + 16, :])

            def gate_log(hd):
                h, dr = hd // 2, hd % 2
                e2 = g_e2[:, hd % 2, :]
                act.wait_ge(S["gl_mm"], hd + 1)
                if hd >= 2:
                    act.wait_ge(S["att_mm"], hd - 1)
                A(e2, pb[0][:, :], ACT.Abs, bias=col("gab", HEADS * dr + h)).then_inc(S["gl_abs"], 1)
                act.wait_ge(S["gl_abs"], hd + 1)
                A(e2, e2, ACT.Exp, scale=-1.0).then_inc(S["gl_exp"], 1)
                act.wait_ge(S["gl_exp"], hd + 1)
                A(e2, e2, ACT.Ln, bias=one1[:, 0:1]).then_inc(S["gl_ln"], 1)

            def decays(cf, hd):
                h, dr, p = hd // 2, hd % 2, hd % 2
                n = cf.base + hd
                tm, tg, tb, e2, dm, dk = (x[:, p, :] for x in (cf.tm, cf.tg, cf.tb, cf.e2, cf.dm, cf.dk))
                act.wait_ge(S["cum"], n + 1)
                if hd >= 2:
                    act.wait_ge(S["att_mm"], n - 1)
                A(e2, tg, ACT.Exp, scale=-cf.scale).then_inc(S["decay"], 1)
                A(tg, tg, ACT.Exp, scale=cf.scale).then_inc(S["decay"], 1)
                a, b = cf.m0, cf.m0 + cf.nc_ * CH
                A(dk[:, a:b], dm[:, a:b], ACT.Exp, scale=-cf.scale).then_inc(S["decay"], 1)
                A(dm[:, a:b], dm[:, a:b], ACT.Exp, scale=cf.scale).then_inc(S["decay"], 1)
                if hd >= 4:
                    act.wait_ge(S["o_mm"], n // 2 - 1)
                A(cf.e3[:, two(h, dr), :], tb, ACT.Exp, scale=cf.scale).then_inc(S["decay"], 1)
                A(tm, tm, ACT.Exp, scale=cf.scale).then_inc(S["decay"], 1)
                v = tb[:, cf.m0:cf.m0 + cf.nc_ * CH].rearrange("p (c n) -> p c n", n=CH)
                if cf.tail:
                    e = cf.tail[1] - 1 if dr == 0 else 0
                    A(cf.e5[:, two(h, dr), cf.nc_:cf.nc_ + 1], tb[:, e:e + 1], ACT.Exp, scale=cf.scale)
                A(cf.e5[:, two(h, dr), 0:cf.nc_], v[:, :, CH - 1 if dr == 0 else 0], ACT.Exp, scale=cf.scale).then_inc(S["decay"], 1)

            def keys_turned(cf, hd):
                n = cf.base + hd
                act.wait_ge(S["kd_tr"], n + 1)
                if hd >= 1:
                    act.wait_ge(S["u_mm"], u_ahead(cf, hd))
                for i, (t0, m) in enumerate(cf.tiles):
                    last = A(cf.kdt[0:m, i, :], pb[3][0:m, 128 * i:128 * i + 128], ACT.Copy)
                last.then_inc(S["kd_cp"], 1)

            def scan_read(cf, h):
                no = h if cf is G else HEADS + h
                act.wait_ge(S["o_mm"], no + 1)
                for e in range(cf.DV // 128):
                    A(cf.o(h, e), pb[6 + e][:, 0:cf.T], ACT.Copy).then_inc(S["o_ev"], 1)
                act.wait_ge(S["o_ev"], 2 * h + 2 if cf is G else 8 + h + 1)

            def scan_steps(cf):
                E = cf.DV // 128
                if cf is G:
                    gate_log(0)
                    gate_log(1)
                decays(cf, 0)
                decays(cf, 1)
                for hd in range(8):
                    keys_turned(cf, hd)
                    if hd >= 2 and hd % 2 == 0:
                        sqrt(cf.norm(hd // 2 - 1), E, 3, cf.T)
                    if cf is G:
                        if hd + 2 < 8:
                            gate_log(hd + 2)
                        act.wait_ge(S["gla_r_mm"], hd + 1)
                        if hd >= 2:
                            act.wait_ge(S["gate_y"], 2 * (hd // 2))
                        A(g_sr[:, hd % 2, :], pb[1][:, :], ACT.Silu).then_inc(S["gla_r_ev"], 1)
                    if hd + 2 < 8:
                        decays(cf, hd + 2)
                    if hd % 2:
                        scan_read(cf, hd // 2)
                        squares(cf.norm(hd // 2), E, lambda e: cf.o(hd // 2, e))
                sqrt(cf.norm(HEADS - 1), E, 3, cf.T)
            scan_steps(G)
            act.wait_ge(S["gate_y"], 8)
            for i in range(2):
                ffn_w_in_hi(0, i)
            squares("n2_0", DC, lambda c: xT[:, c, :], ("proj_x", 0, 2))
            sqrt("n2_0", DC, 7, TT)
            modulate("n2_0", 0, 1, TT)
            ffn(0, TT)
            ffn_out(0, TT, "n1_1", ("ffn_out_x", 0, 2))
            sqrt("n1_1", DC, 7, TT)
            modulate("n1_1", 1, 0, TT)
            copies(8, "na_q_mm", "na_q_ev", lambda u: pb[u % 4][:, 0:NT], lambda u: n_q[:, u, :], scale=lambda u: 64.0 ** -0.5)
            copies(8, "na_k_mm", "na_k_ev", lambda u: pb[u % 4][:, :], lambda u: n_k[:, u, :])
            copies(8, "na_v_mm", "na_v_ev", lambda u: pb[u % 4][:, :], lambda u: n_v[:, u % 4, 512 * (u // 4):512 * (u // 4) + 512])

            def na_exp(i):
                act.wait_ge(S["na_max"], i + 1)
                A(n_s[:, i % 3, :], n_s[:, i % 3, :], ACT.Exp, bias=n_mx[:, i % 3, 1:2], accum_out=n_rs[:, i % 3, 0:1]).then_inc(S["na_exp"], 1)

            def na_read(i):
                h, qt = i // 2, i % 2
                p0 = 64 * (h % 2)
                act.wait_ge(S["na_o_mm"], i + 1)
                A(n_o[p0:p0 + 64, h // 2, 128 * qt:128 * qt + 128], pb[4 + i % 2][p0:p0 + 64, 0:128], ACT.Copy).then_inc(S["na_o_ev"], 1)
            na_exp(0)
            for i in range(2 * NA_H):
                if i + 1 < 2 * NA_H:
                    na_exp(i + 1)
                act.wait_ge(S["na_tr"], i + 1)
                if i >= 2:
                    act.wait_ge(S["na_o_mm"], i - 1)
                A(n_pt[:, i % 2, :], pb[2 + i % 2][:, :], ACT.Copy).then_inc(S["na_pt"], 1)
                if i >= 1:
                    na_read(i - 1)
            na_read(2 * NA_H - 1)
            for i in range(2):
                ffn_w_in_hi(1, i)
            squares("n2_1", DC, lambda c: xT[:, c, 0:NT], ("proj_x", 2 * DC, 1))
            sqrt("n2_1", DC, 7, NT)
            modulate("n2_1", 1, 1, NT)
            ffn(1, NT)
            ffn_out(1, NT, "fin", ("ffn_out_x", 2 * DC, 1))
            sqrt("fin", DC, 7, NT)

            act.wait_ge(S["meta_in"], 16)
            squares("mix", DC, lambda c: zT[:, c, :], ("fin_h", 0, 1))
            sqrt("mix", DC, 7, T2)
            for u in range(12):
                act.wait_ge(S["hy_mm"], u + 1)
                A(hy_u[:, u, :], pb[u % 4][:, 0:T2], ACT.Identity, bias=col("cb2", u), scale=col("cw2", 12 + u)).then_inc(S["hy_mid"], 1)
            copies(4, "hg_mm", "hg_ev", lambda u: pb[u % 4][:, 0:T2], lambda u: q_q[:, u, :], func=ACT.Silu)
            act.wait_ge(S["lb_diff"], 1)
            A(lbv[:, 0:8], lbv[:, 0:8], ACT.Exp).then_inc(S["lb_exp"], 1)
            copies(8, "hg_mm", "hg_ev", lambda u: pb[u % 4][:, 0:T2], lambda u: q_lf[:, u, :], func=ACT.Sigmoid, ahead=4)
            copies(3, "hg_v_mm", "hg_v_ev", lambda u: pb[u][0:H.tiles[u][1], :], lambda u: q_v[0:H.tiles[u][1], u, :])
            copies(4, "hg_mm", "hg_ev", lambda u: pb[u % 4][:, 0:T2], lambda u: q_g[:, u, :], func=ACT.Silu, ahead=12)
            act.wait_ge(S["hg_k"], 8)
            for u in range(8):
                A(q_lf[:, u, :], q_lf[:, u, :], ACT.Ln).then_inc(S["hg_lf"], 1)
            scan_steps(H)
            for i in range(2):
                act.wait_ge(S["filt_arg"], i + 1)
                A(f_h[0:HID, :], f_k[0:HID, :], ACT.Sin).then_inc(S["filt_sin"], 1)
            for g in range(12):
                od, i = g // 6, g % 6
                m = FT[i % 3][1]
                act.wait_ge(S["spec_mm"], g + 1)
                A(spec[0:m, od, i, :], pb[4 + g % 2][0:m, :], ACT.Copy).then_inc(S["spec_ev"], 1)
            for od in range(2):
                for i, (t0, n) in enumerate(TTILE):
                    act.wait_ge(S["u_tr"], 3 * od + i + 1)
                    if od == 1 and i == 0:
                        act.wait_ge(S["dft_mm"], 3)
                    if od == 0 and i == 0:
                        act.wait_ge(S["spec_mm"], 12)
                    A(u_tok[0:n, i, :], pb[i][0:n, :], ACT.Copy).then_inc(S["u_cp"], 1)
            act.wait_ge(S["hy_z"], 2 * HC)
            squares("hyena", HC, lambda c: hy_u[:, c, :])
            sqrt("hyena", HC, 7, T2)
            squares("nffn", DC, lambda c: zT[:, c, :], ("proj_x", 3 * DC, 1))
            sqrt("nffn", DC, 7, T2)

            for i, (t0, n) in enumerate(TTILE):
                for hf in range(2):
                    act.wait_ge(S["h2_tr"], 2 * i + hf + 1)
                    A(r_h2[0:n, i, 512 * hf:512 * hf + 512], pb[2 * i + hf][0:n, :], ACT.Copy).then_inc(S["h2_cp"], 1)
            act.wait_ge(S["r_diff"], 1)
            A(r_oh[:, 4, :], r_oh[:, 4, :], ACT.Exp).then_inc(S["r_exp"], 1)
            act.wait_ge(S["r_diff"], 2)
            A(r_oh[:, 5, :], r_oh[:, 5, :], ACT.Exp).then_inc(S["r_exp"], 1)
            for c in range(DC):
                for hf in range(2):
                    g = 2 * c + hf
                    act.wait_ge(S["xg_mm"], g + 1)
                    A(xg[:, c, T2 * hf:T2 * hf + T2], pb[g % 4][:, 0:T2], ACT.Copy).then_inc(S["xg_ev"], 1)
            for s, (s0, m) in enumerate(STILE):
                act.wait_ge(S["sgt_tr"], s + 1)
                A(r_SgT[0:m, s, :], pb[4 + s % 2][0:m, 0:T2], ACT.Copy).then_inc(S["sgt_ev"], 1)

            act.wait_ge(S["tables"], 1)
            rows = r_ti.bitcast(I32)

            def silu(j):
                A(e_sg[0:64, j, :], pb[j][0:64, :], ACT.Silu).then_inc(S["silu"], 1)

            def turned(j):
                A(e_hT[:, j, :, :], pb[4][:, :].rearrange("p (a b) -> p a b", a=4)[:, :, 0:WIN], ACT.Copy).then_inc(S["hT_cp"], 1)

            def y_rows(j, row):
                for hf in range(2):
                    act.dma_start(ysort[bass.ds(row, WIN), 512 * hf:512 * hf + 512], e_y[64 * hf:64 * hf + 64, j, :]).then_inc(S["y_out"], 16)

            def silu_pass(b, j, i=0):
                act.wait_ge(S["gu_mm"], i + b + 1)
                if b >= 2:
                    act.wait_ge(S["hid"], i + b - 1)
                silu(j)

            def turned_pass(b, j, i=0):
                act.wait_ge(S["hid_tr"], i + b + 1)
                if b >= 2:
                    act.wait_ge(S["down_mm"], i + b - 1)
                turned(j)

            def y_pass(b, j, i=0):
                row = act.value_load(rows[0:1, bass.ds(i + b, 1)], min_val=0, max_val=SLOTS)
                act.wait_ge(S["y_cp"], i + b + 1)
                if b >= 1:
                    act.wait_ge(S["y_out"], 32 * i + 32 * b)
                y_rows(j, row)
            silu_pass(0, 0)
            for b in range(2):
                turned_pass(b, b % 2)
                silu_pass(b + 1, (b + 1) % 2)
                y_pass(b, b % 2)
            LOOPS = (NE - 4) // 2
            with act.Fori(0, LOOPS) as i:
                for b in (2, 3):
                    turned_pass(b, b % 2, 2 * i)
                    silu_pass(b + 1, (b + 1) % 2, 2 * i)
                    y_pass(b, b % 2, 2 * i)
            for b in range(2 + 2 * LOOPS, NE):
                turned_pass(b, b % 2)
                if b + 1 < NE:
                    silu_pass(b + 1, (b + 1) % 2)
                y_pass(b, b % 2)
            act.wait_ge(S["y_out"], 32 * NE)
            act.sem_inc(S["extra_free"], 1)
            n_extra = act.value_load(rows[0:1, 2 * NB:2 * NB + 1], min_val=0, max_val=EXTRA)
            with act.Fori(0, EXTRA) as j:
                with act.If(j < n_extra):
                    row = act.value_load(rows[0:1, bass.ds(j + NE, 1)], min_val=0, max_val=SLOTS)
                    act.wait_ge(S["gu_mm"], j + NE + 1)
                    silu(0)
                    act.wait_ge(S["hid_tr"], j + NE + 1)
                    turned(0)
                    act.wait_ge(S["y_cp"], j + NE + 1)
                    y_rows(0, row)
                    act.wait_ge(S["y_out"], 32 * j + 32 * (NE + 1))
                    act.sem_inc(S["extra_free"], 1)
            for s, (s0, n) in enumerate(STILE):
                act.dma_start(y_s[0:n, s, :], ysort[s0:s0 + n, :]).then_inc(S["ys_in"], 16)
            squares("nfin", DC, lambda c: zT[:, c, :], ("moe_x", 0, 1))
            sqrt("nfin", DC, 7, T2)
            act.wait_ge(S["nfin_h"], DC)
            act.dma_start(out.rearrange("(c p) t -> p c t", p=P), h2T[:, :, N_META:T2]).then_inc(S["stored"], 16)
            act.wait_ge(S["stored"], 16)

        @block.vector
        def _(dve):
            steps = [0]
            w_count = [0]

            def step(ins):
                steps[0] += 1
                ins.then_inc(S["dve_step"], 1)
                dve.wait_ge(S["dve_step"], steps[0])

            TTn, STT, TS = dve.tensor_tensor, dve.scalar_tensor_tensor, dve.tensor_scalar

            def rsq(name, T):
                q0, i = norms[name]
                dve.wait_ge(S["rs_sqrt"], i + 1)
                step(dve.reciprocal(rstd[:, 0:T], rstd[:, 0:T]))

            def norm_mod(name, k, T):
                rsq(name, T)
                for c in range(DC):
                    TTn(hT[:, c, 0:T], xT[:, c, 0:T], rstd[:, 0:T], ALU.mult).then_inc(S["mod_xr"], 1)
                dve.wait_ge(S["mod_xr"], DC * (k + 1))
                dve.sem_inc(S["norm_done"], 1)

            def norm_plain(name, T, chunks, dst, src, gain, done):
                rsq(name, T)
                for c in range(chunks):
                    STT(out=dst(c), in0=src(c), scalar=gain(c), in1=rstd[:, 0:T], op0=ALU.mult, op1=ALU.mult).then_inc(S[done], 1)
                dve.wait_ge(S[done], chunks)
                dve.sem_inc(S["norm_done"], 1)

            def residual(m, mmsem, done, bank, T, l, part, ahead=0):
                dve.wait_ge(S[mmsem], ahead + m + 1)
                for hf in range(T // NT):
                    v = xT[:, m, NT * hf:NT * hf + NT]
                    STT(out=v, in0=pb[bank][:, NT * hf:NT * hf + NT], scalar=mod[:, l, 8 * part + m, hf:hf + 1], in1=v,
                        op0=ALU.mult, op1=ALU.add).then_inc(S[done], 1)

            def taps(dst, src, w0, w2, halves, done):
                n = dst.shape[1] // halves
                dv = dst.rearrange("p (a n) -> p a n", n=n)
                sv = src.rearrange("p (a n) -> p a n", n=n)
                step(STT(out=dv[:, :, 1:n], in0=sv[:, :, 0:n - 1], scalar=w0, in1=dv[:, :, 1:n], op0=ALU.mult, op1=ALU.add))
                STT(out=dv[:, :, 0:n - 1], in0=sv[:, :, 1:n], scalar=w2, in1=dv[:, :, 0:n - 1], op0=ALU.mult, op1=ALU.add)\
                    .then_inc(S[done], 1)

            def w_rest(view, view_r, hi):
                w_count[0] += 1
                dve.wait_ge(S["w_hi"], w_count[0])
                TTn(view_r, view, hi.bitcast(F32), ALU.subtract).then_inc(S["w_lo"], 1)

            def ffn_w_in_lo(l, i):
                n = FIRST[f"ffn{l}"] + i // 2
                w_rest(halves_of(place[n], i % 2), halves_of(place_r[n], i % 2), w_hi[i % 3])

            def ffn_w_out_lo(l, m):
                n = FIRST[f"ffn{l}_out"] + m
                w_rest(place[n], place_r[n], wo_hi[m % 2])

            def ffn(l, T):
                for c in range(DC):
                    dve.wait_ge(S["h_hi"], DC * l + c + 1)
                    TTn(hT_r[:, c, 0:T], hT[:, c, 0:T], h_hi[:, c, 0:T].bitcast(F32), ALU.subtract).then_inc(S["h_lo"], 1)

                def conv(i):
                    j, u = i // 2, i % 2
                    dve.wait_ge(S["ffn_mid"], 22 * l + i + 1)
                    taps(f_t1[:, i % 4, 0:T], pb[(4 * j + 2 * u) % 8][:, 0:T], col("fcw", 3 * l * FC + i), col("fcw", (3 * l + 2) * FC + i),
                         T // NT, "ffn_conv")
                for i in range(FC):
                    j, u = i // 2, i % 2
                    if i + 2 < FC:
                        ffn_w_in_lo(l, i + 2)
                    conv(i)
                    dve.wait_ge(S["ffn_silu"], 22 * l + i + 1)
                    dve.wait_ge(S["ffn_in_mm"], 44 * l + 4 * j + 2 * u + 2)
                    TTn(f_act[:, i, 0:T], f_t1[:, i % 4, 0:T], pb[(4 * j + 2 * u + 1) % 8][:, 0:T], ALU.mult).then_inc(S["ffn_act"], 1)
                ffn_w_out_lo(l, 0)
                for c in range(FC):
                    dve.wait_ge(S["f_hi"], FC * l + c + 1)
                    TTn(f_lo[:, c, 0:T], f_act[:, c, 0:T], f_hi(c, T).bitcast(F32), ALU.subtract).then_inc(S["f_lo"], 1)
                ffn_w_out_lo(l, 1)
                for m in range(DC):
                    if m + 2 < DC:
                        ffn_w_out_lo(l, m + 2)
                    residual(m, "ffn_out_mm", "ffn_out_x", m % 4, T, l, 5, DC * l)

            dve.wait_ge(S["cols_in"], 16)
            for l in range(2):
                dve.wait_ge(S["ada_tr"], 12 * (l + 1))
                step(TTn(mod[:, l, :, :], pb[2 + l][:, 0:96].rearrange("p (a b) -> p a b", b=2),
                         col("ada_b", 48 * l, 48).unsqueeze(2).to_broadcast([P, 48, 2]), ALU.add))
                for w, nm in enumerate(("n1", "n2")):
                    g = col(nm, DC * l, DC).unsqueeze(2).to_broadcast([P, DC, 2])
                    last = STT(out=modA[:, l, w, :, :], in0=mod[:, l, 24 * w + 8:24 * w + 16, :], scalar=1.0, in1=g, op0=ALU.add, op1=ALU.mult)
                    if w == 0:
                        step(last)
                last.then_inc(S["mod_ready"], 1)

            norm_mod("n1_0", 0, TT)
            cos, sin = kg[:, 128:384], kg[:, 384:640]
            dve.wait_ge(S["gla_in"], 80)
            for u in range(8):
                v = g_qk[:, u, 0:NT]
                dve.wait_ge(S["rope_mm"], u + 1)
                TTn(g_tm[:, 0, 0:NT], pb[4 + u % 2][:, 0:NT], sin, ALU.mult).then_inc(S["rope_s"], 1)
                step(TTn(v, v, cos, ALU.mult))
                dve.wait_ge(S["rope_s"], u + 1)
                step(TTn(v, v, g_tm[:, 0, 0:NT], ALU.add))
            step(dve.memset(g_att, 0.0))

            def gate_min(hd):
                h, dr = hd // 2, hd % 2
                tm, tg = g_tm[:, hd % 2, :], g_tg[:, hd % 2, :]
                dve.wait_ge(S["gl_abs"], hd + 1)
                if hd >= 2:
                    dve.wait_ge(S["kd_tr"], hd - 1)
                TS(tm, pb[0][:, :], col("gab", HEADS * dr + h), 0.0, ALU.add, ALU.min).then_inc(S["gl_min"], 1)
                dve.wait_ge(S["gl_ln"], hd + 1)
                dve.wait_ge(S["gl_min"], hd + 1)
                if hd >= 2:
                    dve.wait_ge(S["att_mm"], hd - 1)
                step(TTn(tg, tm, g_e2[:, hd % 2, :], ALU.subtract))
                return tg

            def cumulate(cf, hd, src):
                dr, p = hd % 2, hd % 2
                n = cf.base + hd
                tm, tg, tb, dm = (x[:, p, :] for x in (cf.tm, cf.tg, cf.tb, cf.dm))
                if hd >= 2:
                    dve.wait_ge(S["decay"], 7 * (n - 1))
                step(dve.tensor_tensor_scan(tb, cf.scan, src, 0.0, ALU.mult, ALU.add))
                parts = [(cf.m0, cf.nc_, CH)] + ([(cf.tail[0], 1, cf.tail[1])] if cf.tail else [])

                def v(x, part):
                    o, k, w = part
                    return x[:, o:o + k * w].rearrange("p (c n) -> p c n", n=w)

                def at(x, part, i):
                    o, k, w = part
                    return v(x, part)[:, :, i:i + 1].to_broadcast([P, k, w])
                if hd >= 2:
                    dve.wait_ge(S["kd_tr"], n - 1)
                    dve.wait_ge(S["att_mm"], n - 1)
                if dr == 1:
                    for part in parts:
                        step(TTn(v(tm, part), at(tb, part, part[2] - 1), v(tb, part), ALU.subtract))
                    step(TTn(tb, tm, src, ALU.add))
                main = parts[0]
                step(TTn(v(dm, main), v(tb, main), at(tb, main, CH // 2 - dr), ALU.subtract))
                for part in parts:
                    end = part[2] - 1 if dr == 0 else 0
                    hp = (part[0], 2 * part[1], part[2] // 2) if part is main else part
                    step(TTn(v(tg, hp), v(tb, hp), at(tb, hp, hp[2] // 2), ALU.subtract))
                    last = TTn(v(tm, part), at(tb, part, end), v(tb, part), ALU.subtract)
                    if part is not parts[-1]:
                        step(last)
                last.then_inc(S["cum"], 1)

            def decayed(cf, hd):
                h, dr, p = hd // 2, hd % 2, hd % 2
                n = cf.base + hd
                a, z = cf.m0, cf.m0 + cf.nc_ * CH
                q, k = cf.q(h), cf.k(h, dr)
                for i, (b, x) in enumerate(((cf.e2[:, p, :], k), (cf.tg[:, p, :], q), (cf.dk[:, p, a:z], k[:, a:z]), (cf.dm[:, p, a:z], q[:, a:z]),
                                            (cf.e3[:, two(h, dr), :], q), (cf.tm[:, p, :], k))):
                    dve.wait_ge(S["decay"], 7 * n + i + 1)
                    if i in (2, 3):
                        STT(out=b, in0=b, scalar=1.0, in1=x, op0=ALU.min, op1=ALU.mult).then_inc(S["decayed"], 1)
                    else:
                        TTn(b, b, x, ALU.mult).then_inc(S["decayed"], 1)

            def mask_scores(cf, hd):
                h, dr = hd // 2, hd % 2
                n = cf.base + hd
                dve.wait_ge(S["att_mm"], n + 1)
                if hd >= 2:
                    dve.wait_ge(S["o_mm"], n // 2)
                k = cf.nc_ // 2
                for m, bank in ((m_half[dr], 2), (m_cross[dr], 7)):
                    step(dve.copy_predicated(cf.att[:, dr, 0:k * P].rearrange("p (a n) -> p a n", n=P),
                                             m.bitcast(U32).unsqueeze(1).to_broadcast([P, k, P]),
                                             pb[bank][:, 0:k * P].rearrange("p (a n) -> p a n", n=P)))
                if cf.tail:
                    w = cf.tail[1]
                    step(dve.copy_predicated(cf.att[0:w, dr, k * P:k * P + w], m_half[dr][0:w, 0:w].bitcast(U32), pb[2][0:w, k * P:k * P + w]))
                dve.sem_inc(S["att_cp"], 1)

            def states(cf, hd):
                h, dr = hd // 2, hd % 2
                dve.wait_ge(S["decay"], 7 * (cf.base + hd) + 7)
                od = cf.order[dr]
                for i, c in enumerate(od[:-1]):
                    u = u_ahead(cf, hd) + i
                    dve.wait_ge(S["u_mm"], u + 1)
                    nxt = cf.S[:, dr, od[i + 1], :]
                    if i == 0:
                        dve.tensor_copy(nxt, pb[4 + u % 2][:, 0:cf.DV]).then_inc(S["state"], 1)
                    else:
                        dve.wait_ge(S["state"], u)
                        STT(out=nxt, in0=cf.S[:, dr, c, :], scalar=cf.e5[:, two(h, dr), c:c + 1], in1=pb[4 + u % 2][:, 0:cf.DV],
                            op0=ALU.mult, op1=ALU.add).then_inc(S["state"], 1)

            def gated(cf, h, name, base):
                rsq(name, cf.T)
                E = cf.DV // 128
                for e in range(E):
                    step(STT(out=cf.y(h, e), in0=cf.o(h, e), scalar=cf.gain(h, e), in1=rstd[:, 0:cf.T], op0=ALU.mult, op1=ALU.mult))
                    if cf is G:
                        dve.wait_ge(S["gla_r_ev"], 2 * h + e + 1)
                    TTn(cf.y(h, e), cf.y(h, e), cf.gate(h, e), ALU.mult).then_inc(S["gate_y"], 1)
                dve.wait_ge(S["gate_y"], base + E * (h + 1))
                dve.sem_inc(S["norm_done"], 1)

            def scan_steps(cf, src, norm_base):
                cumulate(cf, 0, src(0))
                cumulate(cf, 1, src(1))
                decayed(cf, 0)
                for hd in range(8):
                    if hd + 1 < 8:
                        decayed(cf, hd + 1)
                    mask_scores(cf, hd)
                    if hd >= 2 and hd % 2 == 0:
                        gated(cf, hd // 2 - 1, cf.norm(hd // 2 - 1), norm_base)
                    states(cf, hd)
                    if hd + 2 < 8:
                        cumulate(cf, hd + 2, src(hd + 2))
                gated(cf, HEADS - 1, cf.norm(HEADS - 1), norm_base)
            scan_steps(G, gate_min, 0)
            for i in range(2):
                ffn_w_in_lo(0, i)
            for m in range(DC):
                residual(m, "proj_mm", "proj_x", m % 4, TT, 0, 2)
            norm_mod("n2_0", 1, TT)
            ffn(0, TT)
            dve.wait_ge(S["ffn_out_x"], 2 * DC)
            norm_mod("n1_1", 2, TT)

            def na_add(i):
                dve.wait_ge(S["na_s_mm"], i + 1)
                dve.wait_ge(S[f"na_bias_in{i % 4}"], 16 * (i // 4 + 1))
                if i >= 3:
                    dve.wait_ge(S["na_tr"], i - 2)
                TTn(n_s[:, i % 3, :], NA_BANK[i % 3][:, :], n_bias[:, i % 4, :], ALU.add).then_inc(S["na_add"], 1)
                dve.wait_ge(S["na_add"], i + 1)
                step(dve.tensor_reduce(n_mx[:, i % 3, 0:1], n_s[:, i % 3, :], AX_X, ALU.max))
                TS(n_mx[:, i % 3, 1:2], n_mx[:, i % 3, 0:1], -1.0, None, ALU.mult).then_inc(S["na_max"], 1)
            na_add(0)
            for i in range(2 * NA_H):
                if i + 1 < 2 * NA_H:
                    na_add(i + 1)
                dve.wait_ge(S["na_exp"], i + 1)
                step(dve.reciprocal(n_rs[:, i % 3, 1:2], n_rs[:, i % 3, 0:1]))
                TS(n_s[:, i % 3, :], n_s[:, i % 3, :], n_rs[:, i % 3, 1:2], None, ALU.mult).then_inc(S["na_p"], 1)
            for i in range(2):
                ffn_w_in_lo(1, i)
            for m in range(DC):
                residual(m, "proj_mm", "proj_x", m % 4, NT, 1, 2, DC)
            norm_mod("n2_1", 3, NT)
            ffn(1, NT)
            dve.wait_ge(S["ffn_out_x"], 3 * DC)
            norm_plain("fin", NT, DC, lambda c: zT[:, c, N_META:T2], lambda c: xT[:, c, 0:NT], lambda c: col("fin", c), "fin_h")
            norm_plain("mix", T2, DC, lambda c: h2T[:, c, :], lambda c: zT[:, c, :], lambda c: col("nmix", c), "mix_h")

            for u in range(12):
                dve.wait_ge(S["hy_mid"], u + 1)
                taps(hy_u[:, u, :], pb[u % 4][:, 0:T2], col("cw2", u), col("cw2", 24 + u), 1, "hy_conv")
            lb = col("lb", 0, 16).rearrange("p (a r c) -> p a r c", r=2, c=4)
            lv = lbv.rearrange("p (a c) -> p a c", c=4)
            step(TTn(lv[:, 0:2, :], lb[:, :, 1, :], lb[:, :, 0, :], ALU.subtract))
            dve.sem_inc(S["lb_diff"], 1)
            dve.wait_ge(S["lb_exp"], 1)
            step(TS(lv[:, 0:2, :], lv[:, 0:2, :], 1.0, None, ALU.add))
            step(dve.reciprocal(lv[:, 0:2, :], lv[:, 0:2, :]))
            step(TS(lv[:, 2:4, :], lv[:, 0:2, :], -1.0, 1.0, ALU.mult, ALU.add))
            for u in range(8):
                dve.wait_ge(S["hg_ev"], 4 + u + 1)
                step(TS(q_lf[:, u, :], q_lf[:, u, :], lbv[:, 8 + u:9 + u], lbv[:, u:u + 1], ALU.mult, ALU.add))
                TS(q_k[:, u, :], q_lf[:, u, :], -1.0, 1.0, ALU.mult, ALU.add).then_inc(S["hg_k"], 1)
            dve.wait_ge(S["b2_in"], 16)
            step(dve.memset(q_att, 0.0))
            dve.wait_ge(S["hg_v_ev"], 3)
            dve.wait_ge(S["hg_ev"], 16)
            dve.wait_ge(S["hg_lf"], 8)
            scan_steps(H, lambda hd: q_lf[:, 4 * (hd % 2) + hd // 2, :], 8)

            TWO_PI = 2 * np.pi
            HI = float(np.float32(6.28125))
            LO = float(np.float32(TWO_PI - HI))
            BIG = float(1.5 * 2 ** 23)
            fr = col("ffr", 0, rows=HID)
            for i in range(2):
                dve.wait_ge(S["filt_mm"], i + 1)
                a, k = f_hs[0:HID, 0, 0:T2], f_k[0:HID, :]
                step(TS(a, pb[i][0:HID, 0:T2], col("fb1" if i == 0 else "fb2", 0, rows=HID), fr, ALU.add, ALU.mult))
                step(TS(k, a, float(1 / TWO_PI), BIG, ALU.mult, ALU.add))
                step(TS(k, k, BIG, None, ALU.subtract))
                step(STT(out=a, in0=k, scalar=-HI, in1=a, op0=ALU.mult, op1=ALU.add))
                step(STT(out=k, in0=k, scalar=-LO, in1=a, op0=ALU.mult, op1=ALU.add))
                TS(k, k, 3.1415925, -3.1415925, ALU.min, ALU.max).then_inc(S["filt_arg"], 1)
            for od in range(2):
                for i, (t0, n) in enumerate(TTILE):
                    g = 3 * od + i
                    dve.wait_ge(S["filt3_mm"], g + 1)
                    if od == 1 and i == 0:
                        dve.wait_ge(S["spec_mm"], 6)
                    step(TTn(f_hs[0:n, i, :], pb[2][0:n, :], win[0:n, i, 0, :], ALU.mult))
                    step(TTn(f_b[0:n, :], pb[3][0:n, :], win[0:n, i, 1, :], ALU.mult))
                    step(TTn(f_hd[0:n, i, :], f_hs[0:n, i, :], f_b[0:n, :], ALU.subtract))
                    TTn(f_hs[0:n, i, :], f_hs[0:n, i, :], f_b[0:n, :], ALU.add).then_inc(S["filt_hd"], 1)
            for od in range(2):
                for i in range(3):
                    m = FT[i][1]
                    dve.wait_ge(S["dft_mm"], 3 * od + i + 1)
                    if od + i:
                        dve.wait_ge(S["yf"], 3 * od + i)
                    if od == 0 and i == 0:
                        dve.wait_ge(S["spec_ev"], 12)
                    if od == 1 and i == 0:
                        dve.wait_ge(S["idft_mm"], HC)
                    b = 3 + 2 * (i % 2)
                    ur, ui = pb[b][0:m, :], pb[b + 1][0:m, :]
                    hr, hi = spec[0:m, od, i, :], spec[0:m, od, 3 + i, :]
                    t0_, t1_ = hy_tmp[0:m, 0, :], hy_tmp[0:m, 1, :]
                    step(TTn(t0_, ur, hr, ALU.mult))
                    step(TTn(t1_, ui, hi, ALU.mult))
                    step(TTn(yf[0:m, i, :], t0_, t1_, ALU.subtract))
                    step(TTn(t0_, ur, hi, ALU.mult))
                    step(TTn(t1_, ui, hr, ALU.mult))
                    TTn(yf[0:m, 3 + i, :], t0_, t1_, ALU.add).then_inc(S["yf"], 1)
                for c in range(HC):
                    dve.wait_ge(S["idft_mm"], HC * od + c + 1)
                    if od == 0 and c == 0:
                        dve.wait_ge(S["u_tr"], 3)
                    v = hy_u[:, c, :]
                    step(STT(out=v, in0=v, scalar=col("skip", HC * od + c), in1=pb[c][:, 0:T2], op0=ALU.mult, op1=ALU.add))
                    TTn(v, v, hy_u[:, 4 * (od + 1) + c, :], ALU.mult).then_inc(S["hy_z"], 1)
            dve.wait_ge(S["hy_z"], 2 * HC)
            norm_plain("hyena", T2, HC, lambda c: y_cat[:, c, :], lambda c: hy_u[:, c, :], lambda c: col("hyn", c), "hyena_y")
            dve.sem_inc(S["hyena_done"], 1)
            for m in range(DC):
                dve.wait_ge(S["proj_mm"], 2 * DC + m + 1)
                TTn(zT[:, m, :], zT[:, m, :], pb[m % 4][:, 0:T2], ALU.add).then_inc(S["proj_x"], 1)
            dve.wait_ge(S["proj_x"], 4 * DC)
            norm_plain("nffn", T2, DC, lambda c: h2T[:, c, :], lambda c: zT[:, c, :], lambda c: col("nffn", c), "nffn_h")

            dve.wait_ge(S["zeroed"], 3)
            dve.wait_ge(S["route_in"], 32)
            dve.wait_ge(S["route_mm"], 1)
            for i, (t0, n) in enumerate(TTILE):
                step(dve.tensor_copy(r_lg[0:n, i, :], pb[7][0:n, 72 * i:72 * i + 72]))
            desc = kr[:, 0:8].unsqueeze(1).to_broadcast([P, 3, 8])
            valid = kr[:, 8:11]
            sm = [r_sm[:, i, :] for i in range(40)]
            oh = [r_oh[:, i, :].rearrange("p (t e) -> p t e", e=8) for i in range(6)]
            gl = r_lg[:, :, 0:NG]

            def b8(x):
                return x.unsqueeze(2).to_broadcast([P, 3, 8])

            def first_max(vals, mx, o, tmp):
                step(dve.tensor_reduce(mx, vals, AX_X, ALU.max))
                step(TTn(o, vals, b8(mx), ALU.is_ge))
                step(TTn(o, o, desc, ALU.mult))
                step(dve.tensor_reduce(tmp, o, AX_X, ALU.max))
                step(TTn(o, o, b8(tmp), ALU.is_equal))
            first_max(gl, sm[0], oh[0], sm[1])
            step(TTn(oh[4], gl, b8(sm[0]), ALU.subtract))
            dve.sem_inc(S["r_diff"], 1)
            dve.wait_ge(S["r_exp"], 1)
            step(dve.tensor_reduce(sm[2], oh[4], AX_X, ALU.add))
            step(dve.reciprocal(sm[3], sm[2]))
            t1 = r_t1.rearrange("p t (g e) -> p t g e", e=8)
            for i in range(3):
                step(TTn(t1[:, i, :, :], r_lg[:, i, NG:].rearrange("p (g e) -> p g e", e=8),
                         oh[0][:, i, :].unsqueeze(2).to_broadcast([P, 8, 8]), ALU.mult))
                step(dve.tensor_reduce(oh[5][:, i, :], t1[:, i, :, :].rearrange("p g e -> p e g"), AX_X, ALU.add))
            step(dve.tensor_reduce(sm[4], oh[5], AX_X, ALU.max))
            step(TTn(oh[5], oh[5], b8(sm[4]), ALU.subtract))
            dve.sem_inc(S["r_diff"], 1)
            dve.wait_ge(S["r_exp"], 2)
            step(dve.tensor_reduce(sm[5], oh[5], AX_X, ALU.add))
            step(dve.reciprocal(sm[6], sm[5]))
            step(TTn(oh[5], oh[5], b8(sm[6]), ALU.mult))
            first_max(oh[5], sm[7], oh[1], sm[8])
            step(STT(out=oh[5], in0=oh[1], scalar=-2.0, in1=oh[5], op0=ALU.mult, op1=ALU.add))
            first_max(oh[5], sm[9], oh[2], sm[10])
            step(TTn(sm[11], sm[7], sm[9], ALU.add))
            step(dve.reciprocal(sm[12], sm[11]))
            step(TTn(sm[12], sm[12], sm[3], ALU.mult))
            step(TTn(sm[13], sm[12], sm[7], ALU.mult))
            step(TTn(sm[14], sm[12], sm[9], ALU.mult))
            step(TTn(oh[0], oh[0], b8(valid), ALU.mult))
            for k in range(2):
                for i in range(3):
                    step(TTn(r_M[:, k, i, :].rearrange("p (g e) -> p g e", e=8), oh[0][:, i, :].unsqueeze(2).to_broadcast([P, 8, 8]),
                             oh[1 + k][:, i, :].unsqueeze(1).to_broadcast([P, 8, 8]), ALU.mult))
            TTn(r_M[:, 2, :, :], r_M[:, 0, :, :], r_M[:, 1, :, :], ALU.add).then_inc(S["route_M"], 1)
            dve.wait_ge(S["pos_mm"], 1)
            cnt, incl, start = r_cnt[:, 0, :], r_cnt[:, 1, :], r_cnt[:, 2, :]
            step(dve.tensor_copy(cnt, pb[6][:, 192:256]))
            step(dve.tensor_tensor_scan(incl, one1[:, 0:NE], cnt, 0.0, ALU.mult, ALU.add))
            step(TTn(start, incl, cnt, ALU.subtract))
            step(TTn(r_t2, pb[6][:, 0:192].rearrange("p (t e) -> p t e", e=NE), start.unsqueeze(1).to_broadcast([P, 3, NE]), ALU.add))
            iota = kr[:, 75:75 + SLOTS]
            for k in range(2):
                step(TTn(r_t1, r_t2, r_M[:, k, :, :], ALU.mult))
                step(dve.tensor_reduce(sm[15 + k], r_t1, AX_X, ALU.add))
                step(TTn(sm[15 + k], sm[15 + k], valid, ALU.add))
                step(TS(sm[15 + k], sm[15 + k], -1.0, None, ALU.add))
            for i in range(3):
                step(TS(r_Sg[:, i, :], iota, sm[15][:, i:i + 1], None, ALU.is_equal))
                step(STT(out=r_S[:, i, :], in0=iota, scalar=sm[16][:, i:i + 1], in1=r_Sg[:, i, :], op0=ALU.is_equal, op1=ALU.add))
            dve.sem_inc(S["route_S"], 1)
            ex, exn, tmp, w_ = r_cnt[0:1, 3, :], r_cnt[0:1, 4, :], r_cnt[0:1, 5, :], r_row[0:1, 0, :]
            c0, s0, eio = cnt[0:1, :], start[0:1, :], kr[0:1, 11:75]
            tab_r, tab_e = r_ti[0:1, 0:NB], r_ti[0:1, NB:2 * NB]
            step(TS(ex, c0, float(WIN), None, ALU.is_gt))
            for k in range(2, -(-T2 // WIN)):
                step(STT(out=ex, in0=c0, scalar=float(k * WIN), in1=ex, op0=ALU.is_gt, op1=ALU.add))
            step(dve.tensor_tensor_scan(exn, one1[0:1, 0:NE], ex, 0.0, ALU.mult, ALU.add))
            step(dve.tensor_copy(r_ti.bitcast(I32)[0:1, 2 * NB:2 * NB + 1], exn[:, NE - 1:NE]))
            step(TTn(exn, exn, ex, ALU.subtract))
            for j in range(EXTRA):
                a, b = r_row[0:1, 1, :], tmp
                step(TTn(w_, exn, ex, ALU.add))
                step(TS(w_, w_, float(j), None, ALU.is_gt))
                step(STT(out=w_, in0=exn, scalar=float(j), in1=w_, op0=ALU.is_le, op1=ALU.mult))
                step(TS(a, exn, float(-WIN), float(WIN * (j + 1)), ALU.mult, ALU.add))
                step(TS(b, c0, float(-WIN), None, ALU.add))
                step(TTn(a, a, b, ALU.min))
                step(TTn(a, a, s0, ALU.add))
                step(TTn(a, a, w_, ALU.mult))
                step(dve.tensor_reduce(r_sm[0:1, 24 + j, 0:1], a, AX_X, ALU.add))
                step(TTn(a, eio, w_, ALU.mult))
                step(dve.tensor_reduce(r_sm[0:1, 24 + j, 1:2], a, AX_X, ALU.add))
                step(dve.tensor_reduce(r_sm[0:1, 24 + j, 2:3], w_, AX_X, ALU.add))
                step(TS(r_sm[0:1, 24 + j, 2:3], r_sm[0:1, 24 + j, 2:3], -float(SLOTS), float(SLOTS), ALU.mult, ALU.add))
                step(TTn(r_sm[0:1, 24 + j, 0:1], r_sm[0:1, 24 + j, 0:1], r_sm[0:1, 24 + j, 2:3], ALU.add))
                step(dve.tensor_copy(tab_r.bitcast(I32)[:, NE + j:NE + j + 1], r_sm[0:1, 24 + j, 0:1]))
                step(dve.tensor_copy(tab_e.bitcast(I32)[:, NE + j:NE + j + 1], r_sm[0:1, 24 + j, 1:2]))
            step(dve.tensor_copy(tab_r.bitcast(I32)[:, 0:NE], s0))
            dve.sem_inc(S["tables"], 1)
            for i in range(3):
                step(TS(r_Sg[:, i, :], iota, sm[15][:, i:i + 1], sm[13][:, i:i + 1], ALU.is_equal, ALU.mult))
                for hf in range(2):
                    o = T2 * hf
                    step(TS(r_sel, iota[:, o:o + T2], sm[16][:, i:i + 1], sm[14][:, i:i + 1], ALU.is_equal, ALU.mult))
                    step(TTn(r_Sg[:, i, o:o + T2], r_Sg[:, i, o:o + T2], r_sel, ALU.add))
            dve.sem_inc(S["route_S"], 1)

            dve.wait_ge(S["xg_ev"], 16)
            dve.wait_ge(S["zeroed"], 3)
            dve.wait_ge(S["sgt_ev"], 5)
            dve.memset(e_hid[64:128, :, :], 0.0).then_inc(S["zeroed"], 1)
            rows = r_ti.bitcast(I32)

            def window(j, row):
                dve.tensor_copy(e_xw[:, j, :, :], xg[:, :, bass.ds(row, WIN)]).then_inc(S["xw"], 1)

            def hidden(j):
                TTn(e_hid[0:64, j, :], e_sg[0:64, j, :], pb[j][64:128, :], ALU.mult).then_inc(S["hid"], 1)

            def y_copy(j):
                dve.tensor_copy(e_y[:, j, :], pb[5 + j][:, :]).then_inc(S["y_cp"], 1)

            def window_pass(b, j, i=0):
                row = dve.value_load(rows[0:1, bass.ds(i + b, 1)], min_val=0, max_val=SLOTS)
                if b >= 2:
                    dve.wait_ge(S["gu_mm"], i + b - 1)
                window(j, row)

            def hidden_pass(b, j, i=0):
                dve.wait_ge(S["silu"], i + b + 1)
                if b >= 2:
                    dve.wait_ge(S["hid_tr"], i + b - 1)
                hidden(j)

            def y_copy_pass(b, j, i=0):
                dve.wait_ge(S["down_mm"], i + b + 1)
                if b >= 2:
                    dve.wait_ge(S["y_out"], 32 * i + 32 * (b - 1))
                y_copy(j)
            window_pass(0, 0)
            window_pass(1, 1)
            hidden_pass(0, 0)
            for b in range(2):
                window_pass(b + 2, b % 2)
                hidden_pass(b + 1, (b + 1) % 2)
                y_copy_pass(b, b % 2)
            LOOPS = (NE - 4) // 2
            with dve.Fori(0, LOOPS) as i:
                for b in (2, 3):
                    window_pass(b + 2, b % 2, 2 * i)
                    hidden_pass(b + 1, (b + 1) % 2, 2 * i)
                    y_copy_pass(b, b % 2, 2 * i)
            for b in range(2 + 2 * LOOPS, NE):
                if b + 2 < NE:
                    window_pass(b + 2, b % 2)
                if b + 1 < NE:
                    hidden_pass(b + 1, (b + 1) % 2)
                y_copy_pass(b, b % 2)
            n_extra = dve.value_load(rows[0:1, 2 * NB:2 * NB + 1], min_val=0, max_val=EXTRA)
            with dve.Fori(0, EXTRA) as j:
                with dve.If(j < n_extra):
                    row = dve.value_load(rows[0:1, bass.ds(j + NE, 1)], min_val=0, max_val=SLOTS)
                    dve.wait_ge(S["extra_free"], j + 1)
                    window(0, row)
                    dve.wait_ge(S["silu"], j + NE + 1)
                    hidden(0)
                    dve.wait_ge(S["down_mm"], j + NE + 1)
                    y_copy(0)
            for m in range(DC):
                dve.wait_ge(S["comb_mm"], m + 1)
                TTn(zT[:, m, :], zT[:, m, :], pb[m % 4][:, 0:T2], ALU.add).then_inc(S["moe_x"], 1)
            dve.wait_ge(S["moe_x"], DC)
            norm_plain("nfin", T2, DC, lambda c: h2T[:, c, :], lambda c: zT[:, c, :], lambda c: col("nfin", c), "nfin_h")


def channel_columns(i):
    def c(a, n=P):
        a = np.asarray(a, np.float32).reshape(-1, n)
        return np.pad(a, ((0, 0), (0, P - n)))
    parts = {"c2": np.stack([np.reshape(i["c"], (DC, P)), np.reshape(i["c_ctx"], (DC, P))], 1), "n1": i["norm1_g"], "n2": i["norm2_g"],
             "fin": i["final_g"], "ada_b": i["ada_b"], "fcw": i["ffn_conv_w"], "fcb": i["ffn_conv_b"], "gab": i["gla_a_b"],
             "gng": i["gla_norm_g"], "cw2": i["conv_w_2"], "cb2": i["conv_b_2"], "skip": i["filt_skip_2"], "hyn": i["hyena_norm_2"],
             "lb": np.stack([i["lb_fwd_2"], i["lb_bwd_2"]]), "hgn": i["hgrn_norm_2"], "nmix": i["norm_mix_2"],
             "nffn": i["norm_ffn_2"], "nfin": i["norm_final_2"], "fb1": i["filt_b1_2"], "fb2": i["filt_b2_2"], "ffr": i["filt_freq_2"]}
    return np.ascontiguousarray(np.concatenate([c(parts[n], HID if n in ("fb1", "fb2", "ffr") else P) for n, _ in COLS]).T)


def bias_windows(rpb):
    rows = NT // GRID
    out = np.full((NA_H, rows, GRID, rows, GRID), -1e30, np.float32)
    for r in range(rows):
        for k in range(rows):
            for c in range(GRID):
                s = min(max(c - NA_KW // 2, 0), GRID - NA_KW)
                out[:, r, c, k, s:s + NA_KW] = rpb[:, k - r + NA_KH - 1, s - c + NA_KW - 1:s - c + 2 * NA_KW - 1]
    return out.reshape(NA_H, 2, P, NT)


def constants():
    f = np.float32
    j = np.arange(CH)
    same = j[:, None] // (CH // 2) == j[None, :] // (CH // 2)
    masks = []
    for causal in (j[:, None] <= j[None, :], j[:, None] >= j[None, :]):
        masks += [np.kron(np.eye(2), causal & same).astype(f), np.kron(np.eye(2), causal & ~same).astype(f)]
    p = np.arange(P)
    k_a = np.concatenate([np.eye(P, dtype=f)] + masks + [(p[:, None] < p[None, :]).astype(f)], 1)
    perm = np.zeros((P, P), f)
    for q in range(P):
        if q % 64 < 32:
            perm[q + 32, q] = -1
        else:
            perm[q - 32, q] = 1
    half = P // 2
    inv = (1.0 / (f(10000.0) ** (np.arange(0, half, 2, dtype=f) / f(half)))).astype(f)
    pos = np.arange(NT)
    ang = np.where(p[:, None] < half, (pos // GRID)[None, :], (pos % GRID)[None, :]).astype(f) * inv[p % 32][:, None]
    scan = np.ones((P, TT), f)
    scan[:, ::CH] = 0
    k_g = np.concatenate([perm, np.cos(ang).astype(f), np.sin(ang).astype(f), scan], 1)
    scan2 = np.ones((P, T2), f)
    scan2[:, 0] = 0
    scan2[:, N_META::CH] = 0
    th = 2 * np.pi * ((np.arange(T2)[:, None] * np.arange(NF)[None, :]) % NFFT) / NFFT
    dft = np.concatenate([np.cos(th), -np.sin(th)], 1).astype(f)
    wt = np.full((NF, 1), 2.0 / NFFT)
    wt[0] = wt[-1] = 1.0 / NFFT
    idft = np.concatenate([wt * np.cos(th.T), -wt * np.sin(th.T)], 0).astype(f)
    t = np.arange(T2, dtype=f) / f(T2 - 1)
    bands = np.linspace(1e-4, (EMB - 1) // 2 - 1, (EMB - 1) // 2, dtype=f)
    a2 = (f(2.0 * np.pi / T2) * np.arange(T2, dtype=f))[:, None] * bands[None, :]
    z = np.concatenate([t[:, None], np.cos(a2), -np.sin(a2)], 1).astype(f)
    deltas = np.abs(np.linspace(np.log(1e-2) / 1.5, np.log(1e-2) / 0.3, HY, dtype=f))
    win = np.repeat(np.exp(-t[:, None] * deltas[None, :]).astype(f)[:, None, :], 2, 1)
    win[0, 1, :] = 0
    valid = np.zeros((P, 3), f)
    for i, (_, n) in enumerate(TTILE):
        valid[:n, i] = 1
    k_r = np.concatenate([np.tile(np.arange(8, 0, -1, dtype=f), (P, 1)), valid, np.tile(np.arange(NE, dtype=f), (P, 1)),
                          np.tile(np.arange(SLOTS, dtype=f), (P, 1))], 1)
    return {"k_a": k_a, "k_g": k_g, "k_scan2": scan2, "k_dft": dft, "k_idft": idft, "k_zT": z.T, "k_win": win, "k_route": k_r}


_PLAIN = ["ada_w", "ffn_w_in", "ffn_w_out"]
_FIRST = ["gla_w_in", "gla_w_out", "gla_a_w1", "gla_a_w2", "na_w_qkv", "na_w_out", "w_in_2", "w_out_2", "filt_w1_2", "filt_w2_2",
          "filt_w3_2", "w_gate_2", "w_up_2", "w_down_2"]


def kernel(**inputs):
    import concourse.bacc as bacc
    from concourse.bass_utils import run_bass_kernel_spmd as run

    i = {k: np.asarray(v) for k, v in inputs.items()}
    a = dict(constants())
    a["xT"] = np.concatenate([i["x"][0], i["ctx"][0]]).T
    a["metaT"] = i["meta_tokens_2"].T
    a["cols"] = channel_columns(i)
    a["na_bias"] = bias_windows(i["na_rpb"][0])
    a["w_route"] = np.concatenate([i["w_router_group_2"][0], i["w_router_expert_2"][0].reshape(D, NE)], 1)
    for n in _PLAIN:
        a[n] = i[n]
    for n in _FIRST:
        a[n] = i[n][0]
    nc = bacc.Bacc("TRN2", target_bir_lowering=False, num_devices=1)
    arrays = {f"in_{n}": np.ascontiguousarray(v) for n, v in a.items()}
    handles = {n: nc.dram_tensor(f"in_{n}", arrays[f"in_{n}"].shape, F32, kind="ExternalInput").ap() for n in a}
    out = nc.dram_tensor("out_yT", (D, NT), F32, kind="ExternalOutput").ap()
    build(nc, handles, out)
    r = run(nc, [arrays], core_ids=[0])
    return np.ascontiguousarray(r.results[0]["out_yT"].T)[None]
```

```python
from contextlib import ExitStack

import numpy as np

import concourse.bass as bass
from concourse import mybir

F32 = mybir.dt.float32
F32R = mybir.dt.float32r
I32 = mybir.dt.int32
U32 = mybir.dt.uint32
ALU = mybir.AluOpType
ACT = mybir.ActivationFunctionType
AX_X = mybir.AxisListType.X

P = 128
D = 1024
DC = D // P
NT = 256
TT = 512
D_FF = 2816
FC = D_FF // P
HEADS = 4
CH = 64
GRID = 64
NA_H, NA_KH, NA_KW = 16, 8, 16
N_META = 16
T2 = N_META + NT
NFFT = 2 * T2
NF = T2 + 1
HY = 512
HC = HY // P
EMB, HID = 33, 64
NE, NG, EPG = 64, 8, 8
DE = 512
W_GLA, W_FFN, W_NA = 8, FC + DC, 12
W_IN2 = W_GLA + 2 * W_FFN + W_NA
WIN = 64
SLOTS = 2 * T2
EXTRA = SLOTS // WIN
EPS = 1e-6
GATE_NORM = 16.0
FT = [(0, 128), (128, 128), (256, NF - 256)]
TTILE = [(0, 128), (128, 128), (256, T2 - 256)]
STILE = [(s, min(128, SLOTS - s)) for s in range(0, SLOTS, 128)]

COLS = [("c2", 2 * DC), ("n1", 2 * DC), ("n2", 2 * DC), ("fin", DC), ("ada_b", 2 * 48),
        ("fcw", 2 * 3 * FC), ("fcb", 2 * FC), ("gab", 2 * HEADS), ("gng", 2),
        ("cw2", 3 * 12), ("cb2", 12), ("skip", 2 * HC), ("hyn", HC), ("lb", 16), ("hgn", HEADS),
        ("nmix", DC), ("nffn", DC), ("nfin", DC), ("fb1", 1), ("fb2", 1), ("ffr", 1)]
COL = {}
NCOL = 0
for _name, _n in COLS:
    COL[_name] = (NCOL, _n)
    NCOL += _n

KA_N = 6 * 128
KG = {"perm": (0, 128), "cos": (128, 256), "sin": (384, 256), "scan": (640, 512)}
KG_N = 1152
KR = {"desc": (0, 8), "valid": (8, 3), "eio": (11, 64), "iota": (75, SLOTS)}
KR_N = 75 + SLOTS


ADA_N = 6 * D // 512


def first_block_slabs(d):
    def cols(w, c0, n):
        return w[:, c0:c0 + n].rearrange("(c p) n -> p c n", p=P)

    out = []
    def ada(l, s):
        out.append(([(0, 512, cols(d["ada_w"][l], 512 * s, 512))], DC, 512, ("ada_mm", ADA_N * l + s + 1)))

    for s in range(ADA_N):
        ada(0, s)

    def ffn(l):
        for j in range(FC // 2):
            out.append(([(0, 256, cols(d["ffn_w_in"][l], 256 * j, 256)),
                         (256, 256, cols(d["ffn_w_in"][l], D_FF + 256 * j, 256))], DC, 512, ("ffn_in_mm", 44 * l + 4 * j + 4)))
            if l == 0:
                ada(1, j)
        if l == 0:
            ada(1, ADA_N - 1)
        for m in range(DC):
            out.append(([(0, P, cols(d["ffn_w_out"][l], P * m, P))], FC, P, ("ffn_out_mm", 8 * l + m + 1)))

    def wide(w, names):
        for s, free in enumerate(names):
            out.append(([(0, 512, cols(w, 512 * s, 512))], DC, 512, free))

    wide(d["gla_w_in"], [("gla_qk_mm", 4), ("gla_qk_mm", 8), ("gla_v_mm", 8), ("gla_v_mm", 16),
                         ("gla_r_mm", 4), ("gla_r_mm", 8)])
    wide(d["gla_w_out"], [("proj_mm", 4), ("proj_mm", 8)])
    ffn(0)
    wide(d["na_w_qkv"], [("na_q_mm", 4), ("na_q_mm", 8), ("na_k_mm", 4), ("na_k_mm", 8), ("na_v_mm", 8), ("na_v_mm", 16)])
    wide(d["na_w_out"], [("proj_mm", 12), ("proj_mm", 16)])
    ffn(1)
    wide(d["w_in_2"], [("hy_mm", 4), ("hy_mm", 8), ("hy_mm", 12), ("hg_mm", 4), ("hg_mm", 8), ("hg_mm", 12),
                       ("hg_v_mm", 6), ("hg_mm", 16)])
    wide(d["w_out_2"], [("proj_mm", 20), ("proj_mm", 24)])
    return out


def build(nc, d, out):
    ctx = ExitStack()
    with ctx:
        def sb(name, shape, dt=F32):
            return ctx.enter_context(nc.sbuf_tensor("s_" + name, shape, dt))

        def sb_both(name, shape):
            with nc.sbuf_tensor("s_" + name, shape, F32) as plain:
                pass
            return plain, sb(name + "_r", shape, F32R)

        class Sems(dict):
            def __missing__(self, name):
                self[name] = ctx.enter_context(nc.semaphore(name))
                return self[name]

        S = Sems()
        pb = [ctx.enter_context(nc.psum_tensor(f"bank{i}", [P, 512], F32)) for i in range(8)]

        NRING = 4
        ring, ring_r = zip(*[sb_both(f"ring{k}", [P, 4096]) for k in range(NRING)])
        xT, xT_r = sb_both("xT", [P, DC, TT])
        hT, hT_r = sb_both("hT", [P, DC, TT])
        sq = sb("sq", [P, 2, TT])
        rstd = sb("rstd", [P, TT])
        cols = sb("cols", [P, NCOL])
        ka = sb("ka", [P, KA_N])
        ones = sb("ones", [P, 4, P])
        one1 = sb("one1", [P, P])
        eps = sb("eps", [P, 1])
        mod = sb("mod", [P, 2, 48, 2])
        modA = sb("modA", [P, 2, 2, DC, 2])
        AW = (nc.sbuf_bytes_remaining // 4 if not callable(nc.sbuf_bytes_remaining) else nc.sbuf_bytes_remaining() // 4) - 64
        arena, arena_r = sb_both("arena", [P, AW])

        def carve(start=0, tensor=None, limit=None):
            at = [start]
            flat = arena if tensor is None else tensor

            def take(*shape):
                n = int(np.prod(shape))
                v = flat[:, at[0]:at[0] + n]
                at[0] += n
                assert at[0] <= (limit or AW), (at[0], AW)
                if len(shape) == 2:
                    v = v.rearrange("p (a b) -> p a b", b=shape[1])
                if len(shape) == 3:
                    v = v.rearrange("p (a b c) -> p a b c", b=shape[1], c=shape[2])
                return v
            take.at = at
            return take

        def col(name, i, n=1, rows=P):
            o = COL[name][0] + i
            return cols[0:rows, o:o + n]

        ident = ka[:, 0:128]
        m_half = [ka[:, 128:256], ka[:, 384:512]]
        m_cross = [ka[:, 256:384], ka[:, 512:640]]
        striu = ka[:, 640:768]
        ON = {1024: ones[:, 0, :], 256: ones[:, 1, :], 128: ones[:, 2, :], 512: ones[:, 3, :]}

        NA_BANK = [pb[0], pb[1], pb[6]]

        t = carve()
        g_qk, g_v = t(8, TT), t(4, D)
        g_S_at = t.at[0]
        g_S = t(2, 8, 256)
        kg, g_low, g_aw2 = t(KG_N), t(TT), t(512)
        g_tm, g_tg_at = t(2, TT), t.at[0]
        g_tg, g_tb, g_e2, g_e3, g_dm, g_dk = t(2, TT), t(2, TT), t(2, TT), t(4, TT), t(2, TT), t(2, TT)
        g_e5, g_att, g_sr_at = t(4, 8), t(2, 4 * P), t.at[0]
        g_sr = t(2, TT)
        tr = carve(g_S_at, tensor=arena_r)
        g_h_hi = tr(DC, TT)
        tr.at[0] = g_tg_at
        g_h_lo, g_w_hi = tr(DC, TT), [tr(DC, 256) for _ in range(2)]
        assert tr.at[0] <= g_sr_at
        g_aw1 = g_sr.rearrange("p a b -> p (a b)")[:, 0:2 * DC * 16].rearrange("p (a b c) -> p a b c", b=DC, c=16)
        g_kdt = kg[:, 0:4 * P].rearrange("p (a b) -> p a b", b=P)
        ada_rows_sb = [g_S[:, 0, 0, :].rearrange("p (a b) -> p a b", b=P), rstd[:, 0:2 * P].rearrange("p (a b) -> p a b", b=P)]
        t = carve()
        f_act, f_t1 = t(FC, TT), t(4, TT)
        f_at = t.at[0]
        t = carve(tensor=arena_r)
        f_lo = t(FC, TT)
        t.at[0] = f_at
        h_hi = t(DC, TT)
        f_hi_rest = carve(f_at - 4 * TT, tensor=arena_r)(FC - DC, TT)
        W_HALF, W_OUT = DC * 256, FC * P
        w_at = AW - 3 * W_HALF
        assert f_at + DC * TT <= w_at and f_at - 4 * TT + (FC - DC) * TT <= w_at - 320
        w_hi = [arena_r[:, w_at + W_HALF * k:w_at + W_HALF * (k + 1)].rearrange("p (c a n) -> p c a n", a=2, n=P) for k in range(3)]
        wo_hi = [arena_r[:, o:o + W_OUT].rearrange("p (c n) -> p c n", n=P) for o in (AW - W_OUT, w_at)]

        ada_sc = arena[:, w_at - 320:w_at - 64].rearrange("p (c n) -> p c n", n=32)

        def half(w, k):
            return w[:, :, 256 * k:256 * k + 256]

        w_half = [w.rearrange("p c a n -> p c (a n)") for w in w_hi]
        GLA_DONE = [("gla_qk_mm", 2 * k + 2) for k in range(4)] + [("gla_v_mm", 4 * k + 4) for k in range(4)]
        NA_DONE = [("na_q_mm", 2 * k + 2) for k in range(4)] + [("na_k_mm", 2 * k + 2) for k in range(4)] + [("na_v_mm", 4 * k + 4) for k in range(4)]
        IN2_DONE = [("hy_mm", 2 * k + 2) for k in range(6)] + [("hg_mm", 2 * k + 2) for k in range(6)] \
            + [("hg_v_mm", 3 * k + 3) for k in range(2)] + [("hg_mm", 2 * k + 2) for k in range(6, 8)]

        def f_hi(c, T):
            return hT_r[:, c, 0:T] if c < DC else f_hi_rest[:, c - DC, 0:T]

        def halves_of(w, half):
            return w.rearrange("p c (a h n) -> p c a h n", a=2, h=2)[:, :, :, half, :]
        t = carve()
        n_q, n_k, n_v, n_o = t(DC, NT), t(DC, TT), t(4, D), t(DC, NT)
        n_bias, n_s, n_pt = t(4, TT), t(3, TT), t(2, TT)
        n_mx, n_rs = t(3, 4), t(3, 4)
        hflat = hT[:, :, :].rearrange("p a b -> p (a b)")
        xflat = xT[:, :, :].rearrange("p a b -> p (a b)")
        zT = hflat[:, 0:DC * T2].rearrange("p (a b) -> p a b", b=T2)
        h2T = xflat[:, 0:DC * T2].rearrange("p (a b) -> p a b", b=T2)
        w_dft = hflat[:, DC * T2:DC * T2 + 3 * 2 * NF].rearrange("p (a b) -> p a b", b=2 * NF)
        w_inv = xflat[:, DC * T2:DC * T2 + 6 * T2].rearrange("p (a b) -> p a b", b=T2)
        t = carve()
        y_cat, hy_u = t(DC, T2), t(12, T2)
        b2_at = t.at[0]
        q_q, q_k, q_lf, q_g, q_v = t(HEADS, T2), t(8, T2), t(8, T2), t(HEADS, T2), t(3, HY)
        q_scan, lbv = t(T2), t(16)
        q_at = t.at[0]
        q_tm, q_tg, q_tb, q_e2, q_e3, q_dm, q_dk = t(2, T2), t(2, T2), t(2, T2), t(2, T2), t(4, T2), t(2, T2), t(2, T2)
        q_e5, q_att, q_kdt, q_S = t(4, 8), t(2, 3 * P), t(3, P), t(2, 5, P)
        q_end = t.at[0]
        h2_hi = carve(q_at, tensor=arena_r)(DC, T2)
        assert q_at + DC * T2 <= w_at
        h2_lo = xT_r[:, :, :].rearrange("p a b -> p (a b)")[:, 0:DC * T2].rearrange("p (a b) -> p a b", b=T2)
        t = carve(b2_at)
        spec = t(2, 6, HY)
        spec_at = t.at[0]
        f_hs, f_hd = t(2, 3, HY), t(2, 3, HY)
        t = carve(q_end)
        fw3, f_a, f_h, f_z, f_w12, f_k = t(4, HY), t(T2), t(T2), t(T2), t(2, HID), t(T2)
        f_b = sq[:, 0, :]
        t = carve(spec_at)
        u_tok, yf, hy_tmp = t(3, HY), t(6, HY), t(2, HY)
        NB = NE + EXTRA
        tail = AW - 2 * 4096
        t = carve(limit=tail)
        r_at = t.at[0]
        r_h2, r_S, r_Sg = t(3, D), t(3, SLOTS), t(3, SLOTS)
        t2 = carve(r_at, limit=tail)
        e_xw, e_sg, e_hid = t2(2, DC, WIN), t2(2, DE), t2(2, DE)
        e_hT, e_y = t2(2, 4, WIN), t2(2, D // 2)
        t.at[0] = max(t.at[0], t2.at[0])
        r_SgT, xg_at = t(5, T2), t.at[0]
        xg = t(DC, SLOTS + WIN)
        r_sel = t(T2)
        t3 = carve(DC * T2, tensor=xflat, limit=DC * TT)
        kr, wr = t3(KR_N), t3(DC, NG + NE)
        r_lg, r_t1, r_t2 = t(3, NG + NE), t(3, NE), t(3, NE)
        r_sm = t(40, 3)
        r_oh = t(6, 24)
        r_M = t(3, 3, NE)
        r_cnt, r_row, r_ti = t(6, NE), t(2, NE), t(2 * NB + 1)
        y_s = carve(xg_at, limit=tail)(5, D)

        def slot(n):
            return ring[n][:, :] if n < NRING else arena[:, tail + 4096 * (n - NRING):tail + 4096 * (n - NRING + 1)]

        ysort = nc.dram_tensor("ysort", (SLOTS + 2 * WIN, D), F32, kind="Internal").ap()

        slabs = first_block_slabs(d)
        place, place_r, landed, free, owner, count = [], [], [], [], {}, {}
        for n, (parts, kc, w, f) in enumerate(slabs):
            s = n % NRING
            count[s] = count.get(s, 0) + 16 * len(parts)
            place.append(slot(s)[:, 0:kc * w].rearrange("p (c n) -> p c n", n=w))
            place_r.append(ring_r[s][:, 0:kc * w].rearrange("p (c n) -> p c n", n=w))
            landed.append((f"slab_in{s}", count[s]))
            free.append(owner.get(s))
            owner[s] = f
        FIRST = {}
        n = 0
        for name, k in (("ada", ADA_N), ("gla", 6), ("gla_out", 2), ("ffn0", FC // 2 + ADA_N), ("ffn0_out", DC), ("na", 6), ("na_out", 2),
                        ("ffn1", 11), ("ffn1_out", 8), ("in2", 8), ("out2", 2)):
            FIRST[name] = n
            n += k
        assert n == len(slabs)

        def in_slab(l, j):
            return FIRST[f"ffn{l}"] + (2 * j if l == 0 else j)

        def ada_bank(g):
            return pb[2 + g % 2] if g < ADA_N else pb[7]

        def ada_rows_bank(g):
            return pb[4 + g % 2] if g < ADA_N else pb[6]

        def ada_slab(g):
            s = g % ADA_N
            return FIRST["ada"] + s if g < ADA_N else FIRST["ffn0"] + min(2 * s + 1, FC // 2 + ADA_N - 1)

        win_slab = FIRST["in2"] + 6
        WIN_SLOT = win_slab % NRING
        win = slot(WIN_SLOT)[:, 0:3 * 2 * HY].rearrange("p (a b c) -> p a b c", b=2, c=HY)


        def eslot(b, part):
            i = 3 * b + part if (b == 0 and part < 2) else (3 * b - 1 + part if part < 2 else 3 * b + 4)
            return i % 6, i // 6
        e_in = [f"expert_in{i}" for i in range(6)]

        sems = S
        block = ctx.enter_context(nc.Block())

        class G:
            T, DV, m0, nc_, tail, scale, base = TT, 256, 0, 8, None, 1.0 / GATE_NORM, 0
            q = staticmethod(lambda h: g_qk[:, h, :])
            k = staticmethod(lambda h, dr: g_qk[:, 4 + h, :])
            S, tm, tg, tb, e2, e3, e5, att, kdt, dm, dk = g_S, g_tm, g_tg, g_tb, g_e2, g_e3, g_e5, g_att, g_kdt, g_dm, g_dk
            scan = kg[:, KG["scan"][0]:KG["scan"][0] + TT]
            tiles = [(128 * i, 128) for i in range(4)]
            chunks = [(CH * c, CH, c // 2, CH * (c % 2)) for c in range(8)]
            order = [[4, 5, 6, 7, 0, 1, 2, 3], [7, 6, 5, 4, 3, 2, 1, 0]]
            v = staticmethod(lambda tt, p0, n, h, e: g_v[p0:p0 + n, tt, 256 * h + 128 * e:256 * h + 128 * e + 128])
            vv = staticmethod(lambda tt, p0, n, h: g_v[p0:p0 + n, tt, 256 * h:256 * h + 256])
            o = staticmethod(lambda h, e: g_qk[:, 4 * e + h, :])
            y = staticmethod(lambda h, e: g_qk[:, 4 * e + h, :])
            gain = staticmethod(lambda h, e: col("gng", e))
            gate = staticmethod(lambda h, e: g_sr[:, e, :])
            norm = staticmethod(lambda h: f"gla{h}")

        class H:
            T, DV, m0, nc_, tail, scale, base = T2, 128, N_META, 4, (0, N_META), 1.0, 8
            q = staticmethod(lambda h: q_q[:, h, :])
            k = staticmethod(lambda h, dr: q_k[:, 4 * dr + h, :])
            S, tm, tg, tb, e2, e3, e5, att, kdt, dm, dk = q_S, q_tm, q_tg, q_tb, q_e2, q_e3, q_e5, q_att, q_kdt, q_dm, q_dk
            scan = q_scan
            tiles = [(N_META, 128), (N_META + 128, 128), (0, N_META)]
            chunks = [(N_META + CH * c, CH, c // 2, CH * (c % 2)) for c in range(4)] + [(0, N_META, 2, 0)]
            order = [[4, 0, 1, 2, 3], [3, 2, 1, 0, 4]]
            v = staticmethod(lambda tt, p0, n, h, e: q_v[p0:p0 + n, tt, 128 * h:128 * h + 128])
            vv = staticmethod(lambda tt, p0, n, h: q_v[p0:p0 + n, tt, 128 * h:128 * h + 128])
            o = staticmethod(lambda h, e: y_cat[:, 4 + h, :])
            y = staticmethod(lambda h, e: y_cat[:, 4 + h, :])
            gain = staticmethod(lambda h, e: col("hgn", h))
            gate = staticmethod(lambda h, e: q_g[:, h, :])
            norm = staticmethod(lambda h: f"hgrn{h}")

        NU = {G: 7, H: 4}

        def u_ahead(cf, hd):
            return (0 if cf is G else 8 * NU[G]) + hd * NU[cf]

        norms = {}
        seen = [0, 0]

        def two(h, dr):
            return 2 * (h % 2) + dr

        def norm_plan(name, chunks):
            norms[name] = (seen[0], seen[1])
            seen[0] += chunks
            seen[1] += 1
        norm_plan("n1_0", DC)
        for h in range(HEADS):
            norm_plan(f"gla{h}", 2)
        for name in ("n2_0", "n1_1", "n2_1", "fin", "mix"):
            norm_plan(name, DC)
        for h in range(HEADS):
            norm_plan(f"hgrn{h}", 1)
        norm_plan("hyena", HC)
        norm_plan("nffn", DC)
        norm_plan("nfin", DC)

        @block.sync
        def _(sp):
            for n, (parts, kc, w, f) in enumerate(slabs):
                if free[n]:
                    sp.wait_ge(S[free[n][0]], free[n][1])
                for o, wd, view in parts:
                    sp.dma_start(place[n][:, :, o:o + wd], view).then_inc(S[landed[n][0]], 16)

            def expert_slab(e, b, part, wait):
                s, k = eslot(b, part)
                dst = slot(s)
                src = [d["w_gate_2"], d["w_up_2"], d["w_down_2"]][part]
                if part < 2:
                    v = src[e, :, :].rearrange("(c p) n -> p c n", p=P)
                    dv = dst.rearrange("p (c n) -> p c n", n=DE)
                else:
                    v = src[e, :, :].rearrange("(c p) n -> p c n", p=P)
                    dv = dst.rearrange("p (c n) -> p c n", n=D)
                wait()
                sp.dma_start(dv, v).then_inc(S[e_in[s]], 16)

            def before_load(b, part):
                s, k = eslot(b, part)
                if k == 0:
                    if s == WIN_SLOT:
                        return lambda: sp.wait_ge(S["filt_hd"], 6)
                    if s < NRING:
                        last = max(i for i in range(len(slabs)) if i % NRING == s)
                        return lambda: sp.wait_ge(S[slabs[last][3][0]], slabs[last][3][1])
                    return lambda: sp.wait_ge(S["hyena_done"], 1)
                return None

            def used(b, part):
                i = 0 if (b, part) == (0, 0) else 1 if (b, part) == (0, 1) else (3 * b - 1 + part if part < 2 else 3 * b + 4)
                j = i - 6
                if j == 0 or j == 1:
                    return ("gu_mm", 1)
                bb, rr = divmod(j - 2, 3)
                return ("gu_mm", bb + 2) if rr < 2 else ("down_mm", bb + 1)

            def load(e, b, part):
                w = before_load(b, part)
                if w is None:
                    name, val = used(b, part)
                    w = lambda: sp.wait_ge(S[name], val)
                expert_slab(e, b, part, w)

            load(0, 0, 0)
            load(0, 0, 1)
            for b in range(2):
                load(b + 1, b + 1, 0)
                load(b + 1, b + 1, 1)
                load(b, b, 2)

            LOOPS = (NE - 4) // 2
            with sp.Fori(0, LOOPS) as i:
                for j in range(2):
                    b = 2 + j
                    for e0, part in ((b + 1, 0), (b + 1, 1), (b, 2)):
                        name, val = used(e0, part)
                        expert_slab(2 * i + e0, e0, part,
                                    lambda: sp.wait_ge(S[name], 2 * i + val))
            for b in range(2 + 2 * LOOPS, NE):
                for bb, part in ((b + 1, 0), (b + 1, 1), (b, 2)):
                    if bb < NE:
                        load(bb, bb, part)
            sp.wait_ge(S["tables"], 2)
            table = r_ti.bitcast(I32)
            n_extra = sp.value_load(table[0:1, 2 * NB:2 * NB + 1], min_val=0, max_val=EXTRA)
            with sp.Fori(0, EXTRA) as j:
                with sp.If(j < n_extra):
                    e = sp.value_load(table[0:1, bass.ds(j + NB + NE, 1)], min_val=0, max_val=NE - 1)
                    sp.wait_ge(S["extra_free"], j + 1)
                    for part, src in enumerate((d["w_gate_2"], d["w_up_2"], d["w_down_2"])):
                        v = src[bass.ds(e, 1), :, :].rearrange("o (c p) n -> p (o c) n", p=P)
                        sp.dma_start(slot(part).rearrange("p (c n) -> p c n", n=src.shape[2]), v).then_inc(S["extra_in"], 16)

        @block.gpsimd
        def _(pool):
            pool.dma_start(xT[:, :, :], d["xT"].rearrange("(c p) t -> p c t", p=P)).then_inc(S["x_in"], 16)
            for i, n in enumerate((1024, 256, 128, 512)):
                pool.memset(ones[:, i, :], 1.0 / n).then_inc(S["ones_set"], 1)
            pool.memset(one1[:, :], 1.0).then_inc(S["ones_set"], 1)
            pool.memset(ada_sc, 0.0).then_inc(S["sc_zero"], 1)
            pool.memset(eps[:, :], EPS).then_inc(S["ones_set"], 1)
            pool.wait_ge(S["gate_y"], 8)
            pool.memset(ada_sc, 0.0).then_inc(S["sc_zero"], 1)
            pool.wait_ge(S["na_v_mm"], 16)
            pool.memset(n_bias[:, :, :], 0.0).then_inc(S["zeroed"], 1)
            pool.wait_ge(S["zeroed"], 1)
            for i in range(2 * NA_H):
                if i >= 4:
                    pool.wait_ge(S["na_add"], i - 3)
                pool.dma_start(n_bias[:, i % 4, 0:NT], d["na_bias"][i // 2, i % 2]).then_inc(S[f"na_bias_in{i % 4}"], 16)
            pool.wait_ge(S["ffn_out_mm"], 2 * DC)
            pool.dma_start(zT[:, :, 0:N_META], d["metaT"].rearrange("(c p) t -> p c t", p=P)).then_inc(S["meta_in"], 16)
            pool.wait_ge(S["ffn_out_x"], 3 * DC)
            pool.dma_start(q_scan, d["k_scan2"]).then_inc(S["b2_in"], 16)
            pool.wait_ge(S["fin_h"], DC)
            for i, (t0, n) in enumerate(TTILE):
                pool.dma_start(w_dft[0:n, i, :], d["k_dft"][t0:t0 + n, :]).then_inc(S["dft_in"], 16)
            for i in range(6):
                f0, n = FT[i % 3]
                pool.dma_start(w_inv[0:n, i, :], d["k_idft"][(i // 3) * NF + f0:(i // 3) * NF + f0 + n, :]).then_inc(S["dft_in"], 16)
            pool.wait_ge(S["hg_mm"], 16)
            for i, (t0, n) in enumerate(TTILE):
                pool.dma_start(win[0:n, i, :, :], d["k_win"][t0:t0 + n, :, :]).then_inc(S["filt_in"], 16)
            pool.dma_start(fw3[0:HID, :, :], d["filt_w3_2"].rearrange("p (a n) -> p a n", n=HY)).then_inc(S["filt_in"], 16)
            pool.dma_start(f_z[0:EMB, :], d["k_zT"]).then_inc(S["filt_in"], 16)
            pool.dma_start(f_w12[0:EMB, 0, :], d["filt_w1_2"]).then_inc(S["filt_in"], 16)
            pool.dma_start(f_w12[0:HID, 1, :], d["filt_w2_2"]).then_inc(S["filt_in"], 16)
            pool.wait_ge(S["idft_mm"], 2 * HC)
            pool.dma_start(kr, d["k_route"]).then_inc(S["route_in"], 16)
            pool.dma_start(wr, d["w_route"].rearrange("(c p) n -> p c n", p=P)).then_inc(S["route_in"], 16)
            pool.wait_ge(S["proj_x"], 4 * DC)
            pool.memset(xg[:, :, SLOTS:SLOTS + WIN], 0.0).then_inc(S["zeroed"], 1)
            pool.memset(r_lg, 0.0).then_inc(S["zeroed"], 1)

        @block.tensor
        def _(pe):
            mm = pe.matmul

            def got(n):
                pe.wait_ge(S[landed[n][0]], landed[n][1])
                return place[n]

            def norm_chunk(name, c, chunks, bank, T, n):
                q0, _ = norms[name]
                pe.wait_ge(S["sq_ready"], q0 + c + 1)
                mm(pb[bank][:, 0:T], ON[n], sq[:, (q0 + c) % 2, 0:T], start=c == 0, stop=c == chunks - 1).then_inc(S["sq_used"], 1)

            def norm_sum(name, chunks, bank, T, n):
                for c in range(chunks):
                    norm_chunk(name, c, chunks, bank, T, n)

            def residual_norm(name, m, T):
                if m >= 1:
                    norm_chunk(name, m - 1, DC, 7, T, 1024)
                if m == DC - 1:
                    norm_chunk(name, m, DC, 7, T, 1024)

            def split_mm(out, w_hi_, w_lo_, x_hi_, x_lo_, start, stop):
                mm(out, w_hi_, x_hi_, start=start, stop=False)
                mm(out, w_hi_, x_lo_, start=False, stop=False)
                return mm(out, w_lo_, x_hi_, start=False, stop=stop)

            def ffn(l, T, norm):
                for i in range(FC):
                    wl = halves_of(place_r[in_slab(l, i // 2)], i % 2)
                    pe.wait_ge(S["w_lo"], W_GLA + (W_FFN + W_NA) * l + i + 1)
                    for a in range(2):
                        b = (2 * i + a) % 6
                        if i >= 3:
                            pe.wait_ge(S["ffn_act" if a else "ffn_conv"], 22 * l + i - 2)
                        for c in range(DC):
                            if i + a == 0:
                                pe.wait_ge(S["h_lo"], DC * (2 * l + 1) + c + 1)
                            last = split_mm(pb[b][:, 0:T], w_hi[i % 3][:, c, a, :], wl[:, c, a, :], h_hi[:, c, 0:T], hT_r[:, c, 0:T],
                                            c == 0, c == DC - 1)
                        last.then_inc(S["ffn_in_mm"], 1)
                    if l == 0:
                        if i % 2 == 0:
                            ada_rows(ADA_N + i // 2)
                        else:
                            ada_turn(ADA_N + i // 2)
                        if i == FC - 1:
                            ada_rows(2 * ADA_N - 1)
                pe.wait_ge(S["ffn_act"], 22 * l + FC)
                halves = 2 if T == TT else 1
                for m in range(DC):
                    pe.wait_ge(S["w_lo"], W_GLA + (W_FFN + W_NA) * l + FC + m + 1)
                    if m >= 4:
                        pe.wait_ge(S["ffn_out_x"], 16 * l + halves * (m - 3))
                    for c in range(FC):
                        if m == 0:
                            pe.wait_ge(S["f_lo"], FC * l + c + 1)
                        last = split_mm(pb[m % 4][:, 0:T], wo_hi[m % 2][:, c, :], place_r[FIRST[f"ffn{l}_out"] + m][:, c, :], f_hi(c, T), f_lo[:, c, 0:T],
                                        c == 0, c == FC - 1)
                    last.then_inc(S["ffn_out_mm"], 1)
                    if l == 0 and m == 0:
                        ada_turn(2 * ADA_N - 1)
                    if l == 0 and m == 1:
                        pe.wait_ge(S["ada_mod"], 2 * ADA_N)
                    residual_norm(norm, m, T)

            def project(slab, src, T, ahead, per, norm):
                for m in range(DC):
                    w = got(FIRST[slab] + m // 4)
                    if m >= 4:
                        pe.wait_ge(S["proj_x"], ahead + per * (m - 3))
                    for c in range(DC):
                        last = mm(pb[m % 4][:, 0:T], w[:, c, 128 * (m % 4):128 * (m % 4) + 128], src(c),
                                  start=c == 0, stop=c == DC - 1)
                    last.then_inc(S["proj_mm"], 1)
                    residual_norm(norm, m, T)

            def ada_rows(g):
                w = got(ada_slab(g))
                pe.wait_ge(S["sc_ready"], g // ADA_N + 1)
                if g >= 2:
                    pe.wait_ge(S["ada_row"], g - 1 if g < ADA_N else g)
                for c in range(DC):
                    for j in range(4):
                        last = mm(ada_rows_bank(g)[32 * j:32 * j + 32, 0:P], ada_sc[:, c, :], w[:, c, P * j:P * j + P], start=c == 0, stop=c == DC - 1,
                                  skip_group_check=True)
                last.then_inc(S["ada_mm"], 1)

            def ada_turn(g):
                pe.wait_ge(S["ada_row"], g + 1)
                if g >= 2:
                    pe.wait_ge(S["ada_mod"], g - 1 if g < ADA_N else g)
                pe.transpose(ada_bank(g)[:, 0:P], ada_rows_sb[g // ADA_N][:, g % 2, :], ident).then_inc(S["ada_tr"], 1)
            pe.wait_ge(S["ones_set"], 6)
            norm_sum("n1_0", DC, 7, TT, 1024)
            pe.wait_ge(S["ka_in"], 16)
            for g in range(ADA_N):
                ada_rows(g)
                if g >= 1:
                    ada_turn(g - 1)
            ada_turn(ADA_N - 1)

            def rope_turn(u):
                pe.wait_ge(S["gla_qk_ev"], u + 1)
                if u >= 2:
                    pe.wait_ge(S["rope_s"], u - 1)
                mm(pb[4 + u % 2][:, 0:NT], kg[:, 0:128], g_qk[:, u, 0:NT], start=True, stop=True).then_inc(S["rope_mm"], 1)
            pe.wait_ge(S["gla_in"], 80)
            for u in range(8):
                k = u // 2
                wh, wl, o = g_w_hi[k % 2], half(place_r[FIRST["gla"] + k // 2], k % 2), 128 * (u % 2)
                pe.wait_ge(S["w_lo"], k + 1)
                if u >= 4:
                    pe.wait_ge(S["gla_qk_ev"], u - 3)
                for c in range(DC):
                    if u == 0:
                        pe.wait_ge(S["h_lo"], c + 1)
                    last = split_mm(pb[u % 4][:, :], wh[:, c, o:o + 128], wl[:, c, o:o + 128], g_h_hi[:, c, :], g_h_lo[:, c, :], c == 0, c == DC - 1)
                last.then_inc(S["gla_qk_mm"], 1)
                if u >= 1:
                    rope_turn(u - 1)
            rope_turn(7)
            pe.wait_ge(S["gla_qk_ev"], 8)
            for k in range(4, 8):
                wh, wl = g_w_hi[k % 2], half(place_r[FIRST["gla"] + k // 2], k % 2)
                pe.wait_ge(S["w_lo"], k + 1)
                for u in range(4):
                    if k == 6:
                        pe.wait_ge(S["gla_v_ev"], u + 1)
                    for c in range(DC):
                        last = split_mm(pb[u][:, 256 * (k % 2):256 * (k % 2) + 256], g_h_hi[:, c, 128 * u:128 * u + 128], g_h_lo[:, c, 128 * u:128 * u + 128],
                                        wh[:, c, :], wl[:, c, :], c == 0, c == DC - 1)
                    last.then_inc(S["gla_v_mm"], 1)
            pe.wait_ge(S["rope_s"], 8)
            for dr in range(2):
                for c in range(DC):
                    last = mm(pb[6 + dr][32 * dr:32 * dr + 16, :], g_aw1[:, dr, c, :], hT[:, c, :], start=c == 0, stop=c == DC - 1)
                last.then_inc(S["low_mm"], 1)
            pe.wait_ge(S["low_ev"], 2)
            pe.wait_ge(S["gla_v_ev"], 8)

            def gate_logits(hd):
                h, dr = hd // 2, hd % 2
                if hd >= 1:
                    pe.wait_ge(S["gl_min"], hd)
                mm(pb[0][:, :], g_aw2[32 * dr:32 * dr + 16, 128 * h:128 * h + 128], g_low[32 * dr:32 * dr + 16, :], start=True, stop=True)\
                    .then_inc(S["gl_mm"], 1)

            def scan_head(cf, hd):
                h, dr, p = hd // 2, hd % 2, hd % 2
                n = cf.base + hd
                pe.wait_ge(S["decayed"], 6 * (n + 1))
                if n >= 1:
                    pe.wait_ge(S["att_cp"], n)
                for tt, (t0, m) in enumerate(cf.tiles):
                    last = mm(pb[2][0:m, P * tt:P * tt + m], cf.e2[:, p, t0:t0 + m], cf.tg[:, p, t0:t0 + m], start=True, stop=True)
                if n >= 1:
                    pe.wait_ge(S["kd_cp"], n)
                if hd >= 3 and dr:
                    pe.wait_ge(S["rstd_ready"], norms[cf.norm(h - 1)][1] + 1)
                for i, (t0, m) in enumerate(cf.tiles):
                    last = pe.transpose(pb[3][0:m, 128 * i:128 * i + 128], cf.tm[:, p, t0:t0 + m], ident)
                last.then_inc(S["kd_tr"], 1)
                if cf is G and h >= 1:
                    pe.wait_ge(S["o_ev"], 2 * h)
                for tt, (t0, m) in enumerate(cf.tiles[:cf.nc_ // 2]):
                    last = mm(pb[7][0:m, P * tt:P * tt + m], cf.dk[:, p, t0:t0 + m], cf.dm[:, p, t0:t0 + m], start=True, stop=True)
                last.then_inc(S["att_mm"], 1)

            def scan_norm(cf, h, hd):
                pe.wait_ge(S["kd_cp"], cf.base + hd + 1)
                norm_sum(cf.norm(h), cf.DV // 128, 3, cf.T, cf.DV)

            def scan_updates(cf, hd):
                h, dr = hd // 2, hd % 2
                pe.wait_ge(S["kd_cp"], cf.base + hd + 1)
                for i, c in enumerate(cf.order[dr][:-1]):
                    _, m, tt, p0 = cf.chunks[c]
                    u = u_ahead(cf, hd) + i
                    if u >= 2:
                        pe.wait_ge(S["state"], u - 1)
                    mm(pb[4 + u % 2][:, 0:cf.DV], cf.kdt[p0:p0 + m, tt, :], cf.vv(tt, p0, m, h), start=True, stop=True)\
                        .then_inc(S["u_mm"], 1)

            def scan_out(cf, h):
                pe.wait_ge(S["att_cp"], cf.base + 2 * h + 2)
                pe.wait_ge(S["state"], u_ahead(cf, 2 * h + 2))
                no = h if cf is G else HEADS + h
                for e in range(cf.DV // 128):
                    if no >= 1 and e == 0:
                        pe.wait_ge(S["o_ev"], 2 * h if cf is G else 8 + h)
                    for tt, (t0, tn) in enumerate(cf.tiles):
                        terms = [(t0, tn, cf.v(tt, 0, tn, h, e), cf.att[0:tn, dr, P * tt:P * tt + tn]) for dr in range(2)]
                        for ci, (c0, m, ct, _) in enumerate(cf.chunks):
                            for dr in range(2):
                                if ct == tt and ci != cf.order[dr][0]:
                                    terms.append((c0, m, cf.S[:, dr, ci, 128 * e:128 * e + 128], cf.e3[:, two(h, dr), c0:c0 + m]))
                        for i, (c0, m, l, r) in enumerate(terms):
                            last = mm(pb[6 + e][:, c0:c0 + m], l, r, start=i == 0, stop=i == len(terms) - 1, skip_group_check=True)
                last.then_inc(S["o_mm"], 1)

            gate_logits(0)
            gate_logits(1)
            for hd in range(8):
                scan_head(G, hd)
                if hd + 2 < 8:
                    gate_logits(hd + 2)
                if hd >= 1:
                    pe.wait_ge(S["gla_r_ev"], hd)
                w = got(FIRST["gla"] + 4 + hd // 4)
                for c in range(DC):
                    last = mm(pb[1][:, :], w[:, c, 128 * (hd % 4):128 * (hd % 4) + 128], hT[:, c, :], start=c == 0, stop=c == DC - 1)
                last.then_inc(S["gla_r_mm"], 1)
                if hd >= 2 and hd % 2 == 0:
                    scan_norm(G, hd // 2 - 1, hd)
                scan_updates(G, hd)
                if hd % 2:
                    scan_out(G, hd // 2)
            scan_norm(G, HEADS - 1, 7)
            pe.wait_ge(S["gate_y"], 8)
            project("gla_out", lambda k: g_qk[:, 4 * (k % 2) + k // 2, :], TT, 0, 2, "n2_0")
            pe.wait_ge(S["proj_x"], 2 * DC)
            pe.wait_ge(S["rstd_ready"], norms["n2_0"][1] + 1)
            ffn(0, TT, "n1_1")

            pe.wait_ge(S["rstd_ready"], norms["n1_1"][1] + 1)
            pe.wait_ge(S["ffn_out_x"], 2 * DC)
            for part, (name, T) in enumerate((("na_q", NT), ("na_k", TT))):
                for u in range(8):
                    k = 4 * part + u // 2
                    wh, wl, o = w_half[k % 3], half(place_r[FIRST["na"] + k // 2], k % 2), 128 * (u % 2)
                    pe.wait_ge(S["w_lo"], W_GLA + W_FFN + k + 1)
                    if u >= 4:
                        pe.wait_ge(S[name + "_ev"], u - 3)
                    elif part:
                        pe.wait_ge(S["na_q_ev"], u + 5)
                    for c in range(DC):
                        if part + u == 0:
                            pe.wait_ge(S["h_lo"], 2 * DC + c + 1)
                        last = split_mm(pb[u % 4][:, 0:T], wh[:, c, o:o + 128], wl[:, c, o:o + 128], h_hi[:, c, 0:T], hT_r[:, c, 0:T],
                                        c == 0, c == DC - 1)
                    last.then_inc(S[name + "_mm"], 1)
            for k in range(8, 12):
                wh, wl = w_half[k % 3], half(place_r[FIRST["na"] + k // 2], k % 2)
                pe.wait_ge(S["w_lo"], W_GLA + W_FFN + k + 1)
                for u in range(4):
                    if k == 8:
                        pe.wait_ge(S["na_k_ev"], u + 5)
                    elif k == 10:
                        pe.wait_ge(S["na_v_ev"], u + 1)
                    for c in range(DC):
                        last = split_mm(pb[u][:, 256 * (k % 2):256 * (k % 2) + 256], h_hi[:, c, 128 * u:128 * u + 128], hT_r[:, c, 128 * u:128 * u + 128],
                                        wh[:, c, :], wl[:, c, :], c == 0, c == DC - 1)
                    last.then_inc(S["na_v_mm"], 1)
            pe.wait_ge(S["na_v_ev"], 8)

            def na_scores(i):
                h, qt = i // 2, i % 2
                p0 = 64 * (h % 2)
                if i >= 3:
                    pe.wait_ge(S["na_add"], i - 2)
                mm(NA_BANK[i % 3][:, :], n_q[p0:p0 + 64, h // 2, 128 * qt:128 * qt + 128], n_k[p0:p0 + 64, h // 2, :], start=True, stop=True)\
                    .then_inc(S["na_s_mm"], 1)

            def na_out(i):
                h = i // 2
                pe.wait_ge(S["na_pt"], i + 1)
                if i >= 2:
                    pe.wait_ge(S["na_o_ev"], i - 1)
                p0 = 64 * (h % 2)
                for k in range(4):
                    last = mm(pb[4 + i % 2][p0:p0 + 64, 0:128], n_v[:, k, 64 * h:64 * h + 64], n_pt[:, i % 2, 128 * k:128 * k + 128], start=k == 0, stop=k == 3)
                last.then_inc(S["na_o_mm"], 1)
            na_scores(0)
            na_scores(1)
            for i in range(2 * NA_H):
                if i + 2 < 2 * NA_H:
                    na_scores(i + 2)
                pe.wait_ge(S["na_p"], i + 1)
                if i >= 2:
                    pe.wait_ge(S["na_pt"], i - 1)
                for k in range(4):
                    last = pe.transpose(pb[2 + i % 2][:, 128 * k:128 * k + 128], n_s[:, i % 3, 128 * k:128 * k + 128], ident)
                last.then_inc(S["na_tr"], 1)
                if i >= 1:
                    na_out(i - 1)
            na_out(2 * NA_H - 1)
            pe.wait_ge(S["na_o_ev"], 2 * NA_H)
            project("na_out", lambda k: n_o[:, k, :], NT, 2 * DC, 1, "n2_1")
            pe.wait_ge(S["proj_x"], 3 * DC)
            pe.wait_ge(S["rstd_ready"], norms["n2_1"][1] + 1)
            ffn(1, NT, "fin")

            pe.wait_ge(S["ffn_out_x"], 3 * DC)
            pe.wait_ge(S["rstd_ready"], norms["fin"][1] + 1)
            norm_sum("mix", DC, 7, T2, 1024)
            pe.wait_ge(S["rstd_ready"], norms["mix"][1] + 1)

            def in2(slab, units, name, ev, prev, ahead=0):
                for u in range(units):
                    k = 2 * slab + u // 2
                    wh, wl, o = w_half[k % 3], half(place_r[FIRST["in2"] + k // 2], k % 2), 128 * (u % 2)
                    pe.wait_ge(S["w_lo"], W_IN2 + k + 1)
                    if u >= 4:
                        pe.wait_ge(S[ev], ahead + u - 3)
                    elif prev:
                        pe.wait_ge(S[prev[0]], prev[1] - 3 + u)
                    for c in range(DC):
                        if slab + u == 0:
                            pe.wait_ge(S["h_lo"], 4 * DC + c + 1)
                        last = split_mm(pb[u % 4][:, 0:T2], wh[:, c, o:o + 128], wl[:, c, o:o + 128], h2_hi[:, c, :], h2_lo[:, c, :],
                                        c == 0, c == DC - 1)
                    last.then_inc(S[name], 1)
            in2(0, 12, "hy_mm", "hy_conv", None)
            in2(3, 4, "hg_mm", "hg_ev", ("hy_conv", 12))
            in2(4, 8, "hg_mm", "hg_ev", ("hg_ev", 4), 4)
            pe.wait_ge(S["hg_ev"], 12)
            for k in range(12, 14):
                wh, wl = w_half[k % 3], half(place_r[FIRST["in2"] + k // 2], k % 2)
                pe.wait_ge(S["w_lo"], W_IN2 + k + 1)
                for u, (t0, m) in enumerate(H.tiles):
                    for c in range(DC):
                        last = split_mm(pb[u][0:m, 256 * (k % 2):256 * (k % 2) + 256], h2_hi[:, c, t0:t0 + m], h2_lo[:, c, t0:t0 + m],
                                        wh[:, c, :], wl[:, c, :], c == 0, c == DC - 1)
                    last.then_inc(S["hg_v_mm"], 1)
            pe.wait_ge(S["hg_v_ev"], 3)
            in2(7, 4, "hg_mm", "hg_ev", None, 12)
            pe.wait_ge(S["hg_ev"], 16)
            for hd in range(8):
                scan_head(H, hd)
                if hd >= 2 and hd % 2 == 0:
                    scan_norm(H, hd // 2 - 1, hd)
                scan_updates(H, hd)
                if hd == 3:
                    pe.wait_ge(S["filt_in"], 7 * 16)
                    mm(pb[0][0:HID, 0:T2], f_w12[0:EMB, 0, :], f_z[0:EMB, :], start=True, stop=True).then_inc(S["filt_mm"], 1)
                if hd == 5:
                    pe.wait_ge(S["filt_sin"], 1)
                    mm(pb[1][0:HID, 0:T2], f_w12[0:HID, 1, :], f_h[0:HID, :], start=True, stop=True).then_inc(S["filt_mm"], 1)
                if hd % 2:
                    scan_out(H, hd // 2)
            scan_norm(H, HEADS - 1, 7)
            pe.wait_ge(S["rstd_ready"], norms["hgrn3"][1] + 1)

            pe.wait_ge(S["filt_sin"], 2)
            pe.wait_ge(S["dft_in"], 9 * 16)
            for od in range(2):
                for i, (t0, n) in enumerate(TTILE):
                    g = 3 * od + i
                    if g >= 2:
                        pe.wait_ge(S["filt_hd"], g - 1)
                    for dr in range(2):
                        last = mm(pb[2 * (g % 2) + dr][0:n, :], f_h[0:HID, t0:t0 + n], fw3[0:HID, 2 * dr + od, :], start=True, stop=True)
                    last.then_inc(S["filt3_mm"], 1)
            for od in range(2):
                pe.wait_ge(S["filt_hd"], 3 * od + 3)
                for i in range(6):
                    f0, m = FT[i % 3]
                    src = f_hs if i < 3 else f_hd
                    g = 6 * od + i
                    if g >= 2:
                        pe.wait_ge(S["spec_ev"], g - 1)
                    for k, (t0, n) in enumerate(TTILE):
                        last = mm(pb[4 + g % 2][0:m, :], w_dft[0:n, k, (i // 3) * NF + f0:(i // 3) * NF + f0 + m], src[0:n, od, k, :], start=k == 0, stop=k == 2)
                    last.then_inc(S["spec_mm"], 1)
            pe.wait_ge(S["spec_ev"], 12)
            for od in range(2):
                if od:
                    pe.wait_ge(S["hy_z"], HC)
                for i, (t0, n) in enumerate(TTILE):
                    for c in range(HC):
                        last = pe.transpose(pb[i][0:n, 128 * c:128 * c + 128], hy_u[:, c, t0:t0 + n], ident)
                    last.then_inc(S["u_tr"], 1)
                for i in range(3):
                    f0, m = FT[i]
                    pe.wait_ge(S["u_cp"], 3 * od + 3)
                    for ri in range(2):
                        b = 3 + 2 * (i % 2) + ri
                        g = 3 * od + i
                        if i == 2 or od:
                            pe.wait_ge(S["yf"], 3 * od + (i - 1 if i == 2 else 0))
                        for k, (t0, n) in enumerate(TTILE):
                            last = mm(pb[b][0:m, :], w_dft[0:n, k, ri * NF + f0:ri * NF + f0 + m], u_tok[0:n, k, :], start=k == 0, stop=k == 2)
                    last.then_inc(S["dft_mm"], 1)
                pe.wait_ge(S["yf"], 3 * od + 3)
                for c in range(HC):
                    for i in range(6):
                        f0, m = FT[i % 3]
                        last = mm(pb[c][:, 0:T2], yf[0:m, i, 128 * c:128 * c + 128], w_inv[0:m, i, :], start=i == 0, stop=i == 5)
                    last.then_inc(S["idft_mm"], 1)
            pe.wait_ge(S["hy_z"], 2 * HC)
            norm_sum("hyena", HC, 7, T2, 512)
            pe.wait_ge(S["rstd_ready"], norms["hyena"][1] + 1)
            pe.wait_ge(S["hyena_y"], HC)
            project("out2", lambda k: y_cat[:, k, :], T2, 3 * DC, 1, "nffn")
            pe.wait_ge(S["proj_x"], 4 * DC)

            pe.wait_ge(S["rstd_ready"], norms["nffn"][1] + 1)
            for i, (t0, n) in enumerate(TTILE):
                for hf in range(2):
                    for c in range(4):
                        if i == 0:
                            pe.wait_ge(S["nffn_h"], 4 * hf + c + 1)
                        last = pe.transpose(pb[2 * i + hf][0:n, 128 * c:128 * c + 128], h2T[:, 4 * hf + c, t0:t0 + n], ident)
                    last.then_inc(S["h2_tr"], 1)
            pe.wait_ge(S["route_in"], 32)
            for i, (t0, n) in enumerate(TTILE):
                for c in range(DC):
                    last = mm(pb[7][0:n, 72 * i:72 * i + 72], h2T[:, c, t0:t0 + n], wr[:, c, :], start=c == 0, stop=c == DC - 1)
            last.then_inc(S["route_mm"], 1)
            pe.wait_ge(S["route_M"], 1)
            pe.wait_ge(S["h2_cp"], 6)
            for i in range(3):
                for j in range(i + 1):
                    last = mm(pb[6][:, 64 * i:64 * i + 64], striu if j == i else one1[:, :], r_M[:, 2, j, :], start=j == 0, stop=j == i)
            for j in range(3):
                last = mm(pb[6][:, 192:256], one1[:, :], r_M[:, 2, j, :], start=j == 0, stop=j == 2)
            last.then_inc(S["pos_mm"], 1)
            pe.wait_ge(S["route_S"], 1)
            for c in range(DC):
                for hf in range(2):
                    g = 2 * c + hf
                    if g >= 4:
                        pe.wait_ge(S["xg_ev"], g - 3)
                    for k, (t0, n) in enumerate(TTILE):
                        last = mm(pb[g % 4][:, 0:T2], r_h2[0:n, k, 128 * c:128 * c + 128], r_S[0:n, k, T2 * hf:T2 * hf + T2], start=k == 0, stop=k == 2)
                    last.then_inc(S["xg_mm"], 1)
            pe.wait_ge(S["route_S"], 2)
            for s, (s0, m) in enumerate(STILE):
                if s >= 2:
                    pe.wait_ge(S["sgt_ev"], s - 1)
                for k, (t0, n) in enumerate(TTILE):
                    last = pe.transpose(pb[4 + s % 2][0:m, t0:t0 + n], r_Sg[0:n, k, s0:s0 + m], ident[0:n, 0:n])
                last.then_inc(S["sgt_tr"], 1)
            pe.wait_ge(S["xg_ev"], 16)
            pe.wait_ge(S["sgt_ev"], 5)

            pe.wait_ge(S["zeroed"], 4)

            def arrived(b, part, k):
                s, k0 = eslot(b, part)
                pe.wait_ge(S[e_in[s]], 16 * k + 16 * (k0 + 1))
                return slot(s)

            def gate_up(j, w):
                for c in range(DC):
                    for part in range(2):
                        last = mm(pb[j][64 * part:64 * part + 64, :], e_xw[:, j, c, :], w[part][:, c, :], start=c == 0, stop=c == DC - 1,
                                  skip_group_check=True)
                last.then_inc(S["gu_mm"], 1)

            def turn(j):
                for c in range(4):
                    last = pe.transpose(pb[4][:, 128 * c:128 * c + 128], e_hid[:, j, 128 * c:128 * c + 128], ident)
                last.then_inc(S["hid_tr"], 1)

            def down(j, w):
                for c in range(4):
                    for hf in range(2):
                        last = mm(pb[5 + j][64 * hf:64 * hf + 64, :], e_hT[:, j, c, :], w[:, c, 512 * hf:512 * hf + 512], start=c == 0, stop=c == 3,
                                  skip_group_check=True)
                last.then_inc(S["down_mm"], 1)

            def gate_up_pass(b, j, k, i=0):
                pe.wait_ge(S["xw"], i + b + 1)
                w = [arrived(b, part, k).rearrange("p (c n) -> p c n", n=DE) for part in range(2)]
                if b >= 2:
                    pe.wait_ge(S["hid"], i + b - 1)
                gate_up(j, w)

            def turn_pass(b, j, i=0):
                pe.wait_ge(S["hid"], i + b + 1)
                if b >= 1:
                    pe.wait_ge(S["hT_cp"], i + b)
                turn(j)

            def down_pass(b, j, k, i=0):
                w = arrived(b, 2, k).rearrange("p (c n) -> p c n", n=D)
                pe.wait_ge(S["hT_cp"], i + b + 1)
                if b >= 2:
                    pe.wait_ge(S["y_cp"], i + b - 1)
                down(j, w)
            gate_up_pass(0, 0, 0)
            for b in range(2):
                turn_pass(b, b % 2)
                gate_up_pass(b + 1, (b + 1) % 2, 0)
                down_pass(b, b % 2, 0)
            LOOPS = (NE - 4) // 2
            with pe.Fori(0, LOOPS) as i:
                for b in (2, 3):
                    turn_pass(b, b % 2, 2 * i)
                    gate_up_pass(b + 1, (b + 1) % 2, i, 2 * i)
                    down_pass(b, b % 2, i, 2 * i)
            for b in range(2 + 2 * LOOPS, NE):
                turn_pass(b, b % 2)
                if b + 1 < NE:
                    gate_up_pass(b + 1, (b + 1) % 2, 0)
                down_pass(b, b % 2, 0)
            pe.wait_ge(S["tables"], 2)
            n_extra = pe.value_load(r_ti.bitcast(I32)[0:1, 2 * NB:2 * NB + 1], min_val=0, max_val=EXTRA)
            with pe.Fori(0, EXTRA) as j:
                with pe.If(j < n_extra):
                    pe.wait_ge(S["extra_in"], 48 * j + 48)
                    pe.wait_ge(S["xw"], j + NE + 1)
                    gate_up(0, [slot(part).rearrange("p (c n) -> p c n", n=DE) for part in range(2)])
                    pe.wait_ge(S["hid"], j + NE + 1)
                    turn(0)
                    pe.wait_ge(S["hT_cp"], j + NE + 1)
                    down(0, slot(2).rearrange("p (c n) -> p c n", n=D))
            pe.wait_ge(S["ys_in"], 5 * 16)
            for m in range(DC):
                if m >= 4:
                    pe.wait_ge(S["moe_x"], m - 3)
                for s, (s0, n) in enumerate(STILE):
                    last = mm(pb[m % 4][:, 0:T2], y_s[0:n, s, 128 * m:128 * m + 128], r_SgT[0:n, s, :], start=s == 0, stop=s == len(STILE) - 1)
                last.then_inc(S["comb_mm"], 1)
                residual_norm("nfin", m, T2)

        @block.scalar
        def _(act):
            A = act.activation
            act.dma_start(cols[:, :], d["cols"]).then_inc(S["cols_in"], 16)
            act.dma_start(ka[:, :], d["k_a"]).then_inc(S["ka_in"], 16)
            act.dma_start(kg, d["k_g"]).then_inc(S["gla_in"], 16)
            act.dma_start(g_aw1[:, 0, :, :], d["gla_a_w1"][0].rearrange("(c p) n -> p c n", p=P)).then_inc(S["gla_in"], 16)
            act.dma_start(g_aw1[:, 1, :, :], d["gla_a_w1"][1].rearrange("(c p) n -> p c n", p=P)).then_inc(S["gla_in"], 16)
            for dr in range(2):
                act.dma_start(g_aw2[32 * dr:32 * dr + 16, :], d["gla_a_w2"][dr]).then_inc(S["gla_in"], 16)
            act.wait_ge(S["cols_in"], 16)

            def ada_condition(l):
                act.wait_ge(S["sc_zero"], l + 1)
                A(ada_sc[:, :, 0:2], col("c2", 0, 2 * DC).rearrange("p (c n) -> p c n", n=2), ACT.Silu).then_inc(S["sc_ready"], 1)

            def ada_read(g):
                act.wait_ge(S["ada_mm"], g + 1)
                if g >= 2:
                    act.wait_ge(S["ada_tr"], g - 1)
                A(ada_rows_sb[g // ADA_N][:, g % 2, :], ada_rows_bank(g)[:, 0:P], ACT.Copy).then_inc(S["ada_row"], 1)
            ada_condition(0)

            def copies(n, mmsem, evsem, bank, dst, func=ACT.Copy, scale=None, ahead=0):
                for u in range(n):
                    act.wait_ge(S[mmsem], ahead + u + 1)
                    o = dst(u)
                    b = bank(u)
                    A(o, b, func, **({} if scale is None else {"scale": scale(u)})).then_inc(S[evsem], 1)

            def copy(mmsem, count, evsem, bank, dst, func=ACT.Copy, **kw):
                act.wait_ge(S[mmsem], count)
                A(dst, bank, func, **kw).then_inc(S[evsem], 1)

            def square(q0, c, s, made=None):
                if made:
                    act.wait_ge(S[made[0]], made[1] + made[2] * (c + 1))
                if q0 + c >= 2:
                    act.wait_ge(S["sq_used"], q0 + c - 1)
                A(sq[:, (q0 + c) % 2, 0:s.shape[1]], s, ACT.Square).then_inc(S["sq_ready"], 1)

            def squares(name, chunks, src, made=None):
                q0, _ = norms[name]
                for c in range(chunks):
                    square(q0, c, src(c), made)

            def root_factor(name, chunks, bank, T):
                q0, i = norms[name]
                act.wait_ge(S["ones_set"], 6)
                act.wait_ge(S["sq_used"], q0 + chunks)
                if i >= 1:
                    act.wait_ge(S["norm_done"], i)
                A(rstd[:, 0:T], pb[bank][:, 0:T], ACT.Ln, bias=eps[:, 0:1]).then_inc(S["rstd_ln"], 1)
                act.wait_ge(S["rstd_ln"], i + 1)
                A(rstd[:, 0:T], rstd[:, 0:T], ACT.Exp, scale=-0.5).then_inc(S["rstd_ready"], 1)

            def h_rounded(k, c, T):
                act.wait_ge(S["mod_h"], DC * k + c + 1)
                A((h_hi if k else g_h_hi)[:, c, 0:T], hT[:, c, 0:T], ACT.Copy).then_inc(S["h_hi"], 1)

            def modulate(name, l, which, T):
                for c in range(DC):
                    act.wait_ge(S["mod_xr"], DC * (2 * l + which) + c + 1)
                    for hf in range(T // NT):
                        v = hT[:, c, NT * hf:NT * hf + NT]
                        last = A(v, v, ACT.Identity, bias=mod[:, l, 24 * which + c, hf:hf + 1], scale=modA[:, l, which, c, hf:hf + 1])
                    last.then_inc(S["mod_h"], 1)
                    if c >= 1:
                        h_rounded(2 * l + which, c - 1, T)
                h_rounded(2 * l + which, DC - 1, T)

            def ffn_w_in_hi(l, i):
                n = in_slab(l, i // 2)
                act.wait_ge(S[landed[n][0]], landed[n][1])
                if i >= 3:
                    act.wait_ge(S["ffn_in_mm"], 44 * l + 2 * (i - 2))
                A(w_hi[i % 3], halves_of(place[n], i % 2), ACT.Copy).then_inc(S["w_hi"], 1)

            def half_hi(k, slab, done, before=None):
                n = FIRST[slab] + k // 2
                act.wait_ge(S[landed[n][0]], landed[n][1])
                if k >= 3:
                    act.wait_ge(S[done[k - 3][0]], done[k - 3][1])
                elif before:
                    act.wait_ge(S[before[0]], before[1])
                A(w_half[k % 3], half(place[n], k % 2), ACT.Copy).then_inc(S["w_hi"], 1)

            def ffn_w_out_hi(l, m):
                n = FIRST[f"ffn{l}_out"] + m
                act.wait_ge(S[landed[n][0]], landed[n][1])
                if m < 2:
                    act.wait_ge(S["ffn_in_mm"], 44 * l + 42 + 2 * m)
                else:
                    act.wait_ge(S["ffn_out_mm"], 8 * l + m - 1)
                A(wo_hi[m % 2], place[n], ACT.Copy).then_inc(S["w_hi"], 1)

            def ffn_out_prepared(l, T):
                ffn_w_out_hi(l, 0)
                act.wait_ge(S["ffn_in_mm"], 44 * (l + 1))
                act.wait_ge(S["ffn_act"], 22 * (l + 1))
                for c in range(FC):
                    A(f_hi(c, T), f_act[:, c, 0:T], ACT.Copy).then_inc(S["f_hi"], 1)
                ffn_w_out_hi(l, 1)

            def ffn_out(l, T, name, made):
                q0, _ = norms[name]
                for m in range(DC):
                    if m + 2 < DC:
                        ffn_w_out_hi(l, m + 2)
                    square(q0, m, xT[:, m, 0:T], made)

            def ffn(l, T):
                if l == 0:
                    ada_condition(1)
                for i in range(FC):
                    if i + 2 < FC:
                        ffn_w_in_hi(l, i + 2)
                    act.wait_ge(S["ffn_in_mm"], 44 * l + 2 * i + 1)
                    if i >= 4:
                        act.wait_ge(S["ffn_act"], 22 * l + i - 3)
                    A(f_t1[:, i % 4, 0:T], pb[2 * i % 6][:, 0:T], ACT.Identity, bias=col("fcb", FC * l + i),
                      scale=col("fcw", (3 * l + 1) * FC + i)).then_inc(S["ffn_mid"], 1)
                    act.wait_ge(S["ffn_conv"], 22 * l + i + 1)
                    A(f_t1[:, i % 4, 0:T], f_t1[:, i % 4, 0:T], ACT.Silu).then_inc(S["ffn_silu"], 1)
                    if l == 0 and i % 2 == 0:
                        ada_read(ADA_N + i // 2)
                if l == 0:
                    ada_read(2 * ADA_N - 1)
                ffn_out_prepared(l, T)

            act.wait_ge(S["x_in"], 16)
            squares("n1_0", DC, lambda c: xT[:, c, :])
            root_factor("n1_0", DC, 7, TT)
            for g in range(ADA_N):
                ada_read(g)

            def gla_w_in_hi(k):
                n = FIRST["gla"] + k // 2
                act.wait_ge(S[landed[n][0]], landed[n][1])
                if k >= 2:
                    act.wait_ge(S[GLA_DONE[k - 2][0]], GLA_DONE[k - 2][1])
                A(g_w_hi[k % 2], half(place[n], k % 2), ACT.Copy).then_inc(S["w_hi"], 1)
            gla_w_in_hi(0)
            act.wait_ge(S["mod_ready"], 1)
            modulate("n1_0", 0, 0, TT)
            gla_w_in_hi(1)
            for u in range(8):
                copy("gla_qk_mm", u + 1, "gla_qk_ev", pb[u % 4][:, :], g_qk[:, u, :], scale=128.0 ** -0.5 if u < 4 else 1.0)
                if u % 2:
                    gla_w_in_hi(u // 2 + 2)
            for u in range(8):
                if u % 4 == 0:
                    gla_w_in_hi(6 + u // 4)
                copy("gla_v_mm", 8 * (u // 4) + 4 + u % 4 + 1, "gla_v_ev", pb[u % 4][:, :], g_v[:, u % 4, 512 * (u // 4):512 * (u // 4) + 512])
            copies(2, "low_mm", "low_ev", lambda u: pb[6 + u][32 * u:32 * u + 16, :], lambda u: g_low[32 * u:32 * u + 16, :])

            def gate_log(hd):
                h, dr = hd // 2, hd % 2
                e2 = g_e2[:, hd % 2, :]
                act.wait_ge(S["gl_mm"], hd + 1)
                if hd >= 2:
                    act.wait_ge(S["att_mm"], hd - 1)
                A(e2, pb[0][:, :], ACT.Abs, bias=col("gab", HEADS * dr + h)).then_inc(S["gl_abs"], 1)
                act.wait_ge(S["gl_abs"], hd + 1)
                A(e2, e2, ACT.Exp, scale=-1.0).then_inc(S["gl_exp"], 1)
                act.wait_ge(S["gl_exp"], hd + 1)
                A(e2, e2, ACT.Ln, bias=one1[:, 0:1]).then_inc(S["gl_ln"], 1)

            def decays(cf, hd):
                h, dr, p = hd // 2, hd % 2, hd % 2
                n = cf.base + hd
                tm, tg, tb, e2, dm, dk = (x[:, p, :] for x in (cf.tm, cf.tg, cf.tb, cf.e2, cf.dm, cf.dk))
                act.wait_ge(S["cum"], n + 1)
                if hd >= 2:
                    act.wait_ge(S["att_mm"], n - 1)
                A(e2, tg, ACT.Exp, scale=-cf.scale).then_inc(S["decay"], 1)
                A(tg, tg, ACT.Exp, scale=cf.scale).then_inc(S["decay"], 1)
                a, b = cf.m0, cf.m0 + cf.nc_ * CH
                A(dk[:, a:b], dm[:, a:b], ACT.Exp, scale=-cf.scale).then_inc(S["decay"], 1)
                A(dm[:, a:b], dm[:, a:b], ACT.Exp, scale=cf.scale).then_inc(S["decay"], 1)
                if hd >= 4:
                    act.wait_ge(S["o_mm"], n // 2 - 1)
                A(cf.e3[:, two(h, dr), :], tb, ACT.Exp, scale=cf.scale).then_inc(S["decay"], 1)
                A(tm, tm, ACT.Exp, scale=cf.scale).then_inc(S["decay"], 1)
                v = tb[:, cf.m0:cf.m0 + cf.nc_ * CH].rearrange("p (c n) -> p c n", n=CH)
                if cf.tail:
                    e = cf.tail[1] - 1 if dr == 0 else 0
                    A(cf.e5[:, two(h, dr), cf.nc_:cf.nc_ + 1], tb[:, e:e + 1], ACT.Exp, scale=cf.scale)
                A(cf.e5[:, two(h, dr), 0:cf.nc_], v[:, :, CH - 1 if dr == 0 else 0], ACT.Exp, scale=cf.scale).then_inc(S["decay"], 1)

            def keys_turned(cf, hd):
                n = cf.base + hd
                act.wait_ge(S["kd_tr"], n + 1)
                if hd >= 1:
                    act.wait_ge(S["u_mm"], u_ahead(cf, hd))
                for i, (t0, m) in enumerate(cf.tiles):
                    last = A(cf.kdt[0:m, i, :], pb[3][0:m, 128 * i:128 * i + 128], ACT.Copy)
                last.then_inc(S["kd_cp"], 1)

            def scan_read(cf, h):
                no = h if cf is G else HEADS + h
                act.wait_ge(S["o_mm"], no + 1)
                for e in range(cf.DV // 128):
                    A(cf.o(h, e), pb[6 + e][:, 0:cf.T], ACT.Copy).then_inc(S["o_ev"], 1)
                act.wait_ge(S["o_ev"], 2 * h + 2 if cf is G else 8 + h + 1)

            def scan_steps(cf):
                E = cf.DV // 128
                if cf is G:
                    gate_log(0)
                    gate_log(1)
                decays(cf, 0)
                decays(cf, 1)
                for hd in range(8):
                    keys_turned(cf, hd)
                    if hd >= 2 and hd % 2 == 0:
                        root_factor(cf.norm(hd // 2 - 1), E, 3, cf.T)
                    if cf is G:
                        if hd + 2 < 8:
                            gate_log(hd + 2)
                        act.wait_ge(S["gla_r_mm"], hd + 1)
                        if hd >= 2:
                            act.wait_ge(S["gate_y"], 2 * (hd // 2))
                        A(g_sr[:, hd % 2, :], pb[1][:, :], ACT.Silu).then_inc(S["gla_r_ev"], 1)
                    if hd + 2 < 8:
                        decays(cf, hd + 2)
                    if cf is H and hd in (4, 6):
                        act.wait_ge(S["filt_arg"], hd // 2 - 1)
                        A(f_h[0:HID, :], f_k[0:HID, :], ACT.Sin).then_inc(S["filt_sin"], 1)
                    if hd % 2:
                        scan_read(cf, hd // 2)
                        squares(cf.norm(hd // 2), E, lambda e: cf.o(hd // 2, e))
                root_factor(cf.norm(HEADS - 1), E, 3, cf.T)
            scan_steps(G)
            act.wait_ge(S["gate_y"], 8)
            for i in range(2):
                ffn_w_in_hi(0, i)
            squares("n2_0", DC, lambda c: xT[:, c, :], ("proj_x", 0, 2))
            root_factor("n2_0", DC, 7, TT)
            modulate("n2_0", 0, 1, TT)
            ffn(0, TT)
            ffn_out(0, TT, "n1_1", ("ffn_out_x", 0, 2))
            half_hi(0, "na", NA_DONE, ("ffn_out_mm", DC))
            root_factor("n1_1", DC, 7, TT)
            act.wait_ge(S["mod_ready"], 2)
            modulate("n1_1", 1, 0, TT)
            half_hi(1, "na", NA_DONE, ("ffn_out_mm", DC))
            for u in range(16):
                if u % 2 == 0:
                    half_hi(u // 2 + 2, "na", NA_DONE, ("ffn_out_mm", DC))
                if u < 8:
                    copy("na_q_mm", u + 1, "na_q_ev", pb[u % 4][:, 0:NT], n_q[:, u, :], scale=64.0 ** -0.5)
                else:
                    copy("na_k_mm", u - 7, "na_k_ev", pb[u % 4][:, :], n_k[:, u - 8, :])
            for u in range(8):
                if u % 4 == 0:
                    for k in range(2):
                        if 10 + u // 2 + k < 12:
                            half_hi(10 + u // 2 + k, "na", NA_DONE)
                copy("na_v_mm", 8 * (u // 4) + 4 + u % 4 + 1, "na_v_ev", pb[u % 4][:, :], n_v[:, u % 4, 512 * (u // 4):512 * (u // 4) + 512])

            def na_exp(i):
                act.wait_ge(S["na_max"], i + 1)
                A(n_s[:, i % 3, :], n_s[:, i % 3, :], ACT.Exp, bias=n_mx[:, i % 3, 1:2], accum_out=n_rs[:, i % 3, 0:1]).then_inc(S["na_exp"], 1)

            def na_read(i):
                h, qt = i // 2, i % 2
                p0 = 64 * (h % 2)
                act.wait_ge(S["na_o_mm"], i + 1)
                A(n_o[p0:p0 + 64, h // 2, 128 * qt:128 * qt + 128], pb[4 + i % 2][p0:p0 + 64, 0:128], ACT.Copy).then_inc(S["na_o_ev"], 1)
            na_exp(0)
            for i in range(2 * NA_H):
                if i + 1 < 2 * NA_H:
                    na_exp(i + 1)
                act.wait_ge(S["na_tr"], i + 1)
                if i >= 2:
                    act.wait_ge(S["na_o_mm"], i - 1)
                A(n_pt[:, i % 2, :], pb[2 + i % 2][:, :], ACT.Copy).then_inc(S["na_pt"], 1)
                if i >= 1:
                    na_read(i - 1)
            na_read(2 * NA_H - 1)
            for i in range(2):
                ffn_w_in_hi(1, i)
            squares("n2_1", DC, lambda c: xT[:, c, 0:NT], ("proj_x", 2 * DC, 1))
            root_factor("n2_1", DC, 7, NT)
            modulate("n2_1", 1, 1, NT)
            ffn(1, NT)
            ffn_out(1, NT, "fin", ("ffn_out_x", 2 * DC, 1))
            root_factor("fin", DC, 7, NT)

            act.wait_ge(S["meta_in"], 16)
            squares("mix", DC, lambda c: zT[:, c, :], ("fin_h", 0, 1))
            half_hi(0, "in2", IN2_DONE, ("ffn_out_mm", 2 * DC))
            root_factor("mix", DC, 7, T2)
            for c in range(DC):
                act.wait_ge(S["mix_h"], c + 1)
                A(h2_hi[:, c, :], h2T[:, c, :], ACT.Copy).then_inc(S["h_hi"], 1)

            def in2_ahead(u):
                if u % 2 == 0 and u // 2 + 2 < 16:
                    half_hi(u // 2 + 2, "in2", IN2_DONE, ("ffn_out_mm", 2 * DC))
            half_hi(1, "in2", IN2_DONE, ("ffn_out_mm", 2 * DC))
            for u in range(12):
                in2_ahead(u)
                act.wait_ge(S["hy_mm"], u + 1)
                A(hy_u[:, u, :], pb[u % 4][:, 0:T2], ACT.Identity, bias=col("cb2", u), scale=col("cw2", 12 + u)).then_inc(S["hy_mid"], 1)
            for u in range(4):
                in2_ahead(12 + u)
                copy("hg_mm", u + 1, "hg_ev", pb[u % 4][:, 0:T2], q_q[:, u, :], func=ACT.Silu)
            act.wait_ge(S["lb_diff"], 1)
            A(lbv[:, 0:8], lbv[:, 0:8], ACT.Exp).then_inc(S["lb_exp"], 1)
            for u in range(8):
                in2_ahead(16 + u)
                copy("hg_mm", 4 + u + 1, "hg_ev", pb[u % 4][:, 0:T2], q_lf[:, u, :], func=ACT.Sigmoid)
            for k in range(2):
                in2_ahead(24 + 2 * k)
            for u in range(3):
                copy("hg_v_mm", 3 + u + 1, "hg_v_ev", pb[u][0:H.tiles[u][1], :], q_v[0:H.tiles[u][1], u, :])
            for u in range(4):
                copy("hg_mm", 12 + u + 1, "hg_ev", pb[u % 4][:, 0:T2], q_g[:, u, :], func=ACT.Silu)
            act.wait_ge(S["hg_k"], 8)
            for u in range(8):
                A(q_lf[:, u, :], q_lf[:, u, :], ACT.Ln).then_inc(S["hg_lf"], 1)
            scan_steps(H)
            for g in range(12):
                od, i = g // 6, g % 6
                m = FT[i % 3][1]
                act.wait_ge(S["spec_mm"], g + 1)
                A(spec[0:m, od, i, :], pb[4 + g % 2][0:m, :], ACT.Copy).then_inc(S["spec_ev"], 1)
            for od in range(2):
                for i, (t0, n) in enumerate(TTILE):
                    act.wait_ge(S["u_tr"], 3 * od + i + 1)
                    if od == 1 and i == 0:
                        act.wait_ge(S["dft_mm"], 3)
                    if od == 0 and i == 0:
                        act.wait_ge(S["spec_mm"], 12)
                    A(u_tok[0:n, i, :], pb[i][0:n, :], ACT.Copy).then_inc(S["u_cp"], 1)
            act.wait_ge(S["hy_z"], 2 * HC)
            squares("hyena", HC, lambda c: hy_u[:, c, :])
            root_factor("hyena", HC, 7, T2)
            squares("nffn", DC, lambda c: zT[:, c, :], ("proj_x", 3 * DC, 1))
            root_factor("nffn", DC, 7, T2)

            for i, (t0, n) in enumerate(TTILE):
                for hf in range(2):
                    act.wait_ge(S["h2_tr"], 2 * i + hf + 1)
                    A(r_h2[0:n, i, 512 * hf:512 * hf + 512], pb[2 * i + hf][0:n, :], ACT.Copy).then_inc(S["h2_cp"], 1)
            act.wait_ge(S["r_diff"], 1)
            A(r_oh[:, 4, :], r_oh[:, 4, :], ACT.Exp).then_inc(S["r_exp"], 1)
            act.wait_ge(S["r_diff"], 2)
            A(r_oh[:, 5, :], r_oh[:, 5, :], ACT.Exp).then_inc(S["r_exp"], 1)
            for c in range(DC):
                for hf in range(2):
                    g = 2 * c + hf
                    act.wait_ge(S["xg_mm"], g + 1)
                    A(xg[:, c, T2 * hf:T2 * hf + T2], pb[g % 4][:, 0:T2], ACT.Copy).then_inc(S["xg_ev"], 1)
            for s, (s0, m) in enumerate(STILE):
                act.wait_ge(S["sgt_tr"], s + 1)
                A(r_SgT[0:m, s, :], pb[4 + s % 2][0:m, 0:T2], ACT.Copy).then_inc(S["sgt_ev"], 1)

            act.wait_ge(S["tables"], 1)
            rows = r_ti.bitcast(I32)

            def silu(j):
                A(e_sg[0:64, j, :], pb[j][0:64, :], ACT.Silu).then_inc(S["silu"], 1)

            def turned(j):
                A(e_hT[:, j, :, :], pb[4][:, :].rearrange("p (a b) -> p a b", a=4)[:, :, 0:WIN], ACT.Copy).then_inc(S["hT_cp"], 1)

            def y_rows(j, row):
                for hf in range(2):
                    act.dma_start(ysort[bass.ds(row, WIN), 512 * hf:512 * hf + 512], e_y[64 * hf:64 * hf + 64, j, :]).then_inc(S["y_out"], 16)

            def silu_pass(b, j, i=0):
                act.wait_ge(S["gu_mm"], i + b + 1)
                if b >= 2:
                    act.wait_ge(S["hid"], i + b - 1)
                silu(j)

            def turned_pass(b, j, i=0):
                act.wait_ge(S["hid_tr"], i + b + 1)
                if b >= 2:
                    act.wait_ge(S["down_mm"], i + b - 1)
                turned(j)

            def y_pass(b, j, i=0):
                row = act.value_load(rows[0:1, bass.ds(i + b, 1)], min_val=0, max_val=SLOTS)
                act.wait_ge(S["y_cp"], i + b + 1)
                if b >= 1:
                    act.wait_ge(S["y_out"], 32 * i + 32 * b)
                y_rows(j, row)
            silu_pass(0, 0)
            for b in range(2):
                turned_pass(b, b % 2)
                silu_pass(b + 1, (b + 1) % 2)
                y_pass(b, b % 2)
            LOOPS = (NE - 4) // 2
            with act.Fori(0, LOOPS) as i:
                for b in (2, 3):
                    turned_pass(b, b % 2, 2 * i)
                    silu_pass(b + 1, (b + 1) % 2, 2 * i)
                    y_pass(b, b % 2, 2 * i)
            for b in range(2 + 2 * LOOPS, NE):
                turned_pass(b, b % 2)
                if b + 1 < NE:
                    silu_pass(b + 1, (b + 1) % 2)
                y_pass(b, b % 2)
            act.wait_ge(S["y_out"], 32 * NE)
            act.sem_inc(S["extra_free"], 1)
            act.wait_ge(S["tables"], 2)
            n_extra = act.value_load(rows[0:1, 2 * NB:2 * NB + 1], min_val=0, max_val=EXTRA)
            with act.Fori(0, EXTRA) as j:
                with act.If(j < n_extra):
                    row = act.value_load(rows[0:1, bass.ds(j + NE, 1)], min_val=0, max_val=SLOTS)
                    act.wait_ge(S["gu_mm"], j + NE + 1)
                    silu(0)
                    act.wait_ge(S["hid_tr"], j + NE + 1)
                    turned(0)
                    act.wait_ge(S["y_cp"], j + NE + 1)
                    y_rows(0, row)
                    act.wait_ge(S["y_out"], 32 * j + 32 * (NE + 1))
                    act.sem_inc(S["extra_free"], 1)
            for s, (s0, n) in enumerate(STILE):
                act.dma_start(y_s[0:n, s, :], ysort[s0:s0 + n, :]).then_inc(S["ys_in"], 16)
            squares("nfin", DC, lambda c: zT[:, c, :], ("moe_x", 0, 1))
            root_factor("nfin", DC, 7, T2)
            act.wait_ge(S["nfin_h"], DC)
            act.dma_start(out.rearrange("(c p) t -> p c t", p=P), h2T[:, :, N_META:T2]).then_inc(S["stored"], 16)
            act.wait_ge(S["stored"], 16)

        @block.vector
        def _(dve):
            steps = [0]
            w_count = [0]

            def step(ins):
                steps[0] += 1
                ins.then_inc(S["dve_step"], 1)
                dve.wait_ge(S["dve_step"], steps[0])

            TTn, STT, TS = dve.tensor_tensor, dve.scalar_tensor_tensor, dve.tensor_scalar

            def rsq(name, T):
                q0, i = norms[name]
                dve.wait_ge(S["rstd_ready"], i + 1)

            def norm_mod(name, k, T):
                rsq(name, T)
                for c in range(DC):
                    TTn(hT[:, c, 0:T], xT[:, c, 0:T], rstd[:, 0:T], ALU.mult).then_inc(S["mod_xr"], 1)
                dve.wait_ge(S["mod_xr"], DC * (k + 1))
                dve.sem_inc(S["norm_done"], 1)

            def norm_plain(name, T, chunks, dst, src, gain, done):
                rsq(name, T)
                for c in range(chunks):
                    STT(out=dst(c), in0=src(c), scalar=gain(c), in1=rstd[:, 0:T], op0=ALU.mult, op1=ALU.mult).then_inc(S[done], 1)
                dve.wait_ge(S[done], chunks)
                dve.sem_inc(S["norm_done"], 1)

            def residual(m, mmsem, done, bank, T, l, part, ahead=0):
                dve.wait_ge(S[mmsem], ahead + m + 1)
                for hf in range(T // NT):
                    v = xT[:, m, NT * hf:NT * hf + NT]
                    STT(out=v, in0=pb[bank][:, NT * hf:NT * hf + NT], scalar=mod[:, l, 8 * part + m, hf:hf + 1], in1=v,
                        op0=ALU.mult, op1=ALU.add).then_inc(S[done], 1)

            def taps(dst, src, w0, w2, halves, done):
                n = dst.shape[1] // halves
                dv = dst.rearrange("p (a n) -> p a n", n=n)
                sv = src.rearrange("p (a n) -> p a n", n=n)
                step(STT(out=dv[:, :, 1:n], in0=sv[:, :, 0:n - 1], scalar=w0, in1=dv[:, :, 1:n], op0=ALU.mult, op1=ALU.add))
                STT(out=dv[:, :, 0:n - 1], in0=sv[:, :, 1:n], scalar=w2, in1=dv[:, :, 0:n - 1], op0=ALU.mult, op1=ALU.add)\
                    .then_inc(S[done], 1)

            def w_rest(view, view_r, hi):
                w_count[0] += 1
                dve.wait_ge(S["w_hi"], w_count[0])
                TTn(view_r, view, hi.bitcast(F32), ALU.subtract).then_inc(S["w_lo"], 1)

            def h_rest(k, c, x, x_r, hi):
                dve.wait_ge(S["h_hi"], DC * k + c + 1)
                TTn(x_r, x, hi.bitcast(F32), ALU.subtract).then_inc(S["h_lo"], 1)

            def half_lo(k, slab):
                n = FIRST[slab] + k // 2
                w_rest(half(place[n], k % 2), half(place_r[n], k % 2), w_half[k % 3])

            def ffn_w_in_lo(l, i):
                n = in_slab(l, i // 2)
                w_rest(halves_of(place[n], i % 2), halves_of(place_r[n], i % 2), w_hi[i % 3])

            def ffn_w_out_lo(l, m):
                n = FIRST[f"ffn{l}_out"] + m
                w_rest(place[n], place_r[n], wo_hi[m % 2])

            def ffn(l, T):
                for c in range(DC):
                    h_rest(2 * l + 1, c, hT[:, c, 0:T], hT_r[:, c, 0:T], h_hi[:, c, 0:T])

                def conv(i):
                    dve.wait_ge(S["ffn_mid"], 22 * l + i + 1)
                    taps(f_t1[:, i % 4, 0:T], pb[2 * i % 6][:, 0:T], col("fcw", 3 * l * FC + i), col("fcw", (3 * l + 2) * FC + i),
                         T // NT, "ffn_conv")
                for i in range(FC):
                    if i + 2 < FC:
                        ffn_w_in_lo(l, i + 2)
                    conv(i)
                    dve.wait_ge(S["ffn_silu"], 22 * l + i + 1)
                    dve.wait_ge(S["ffn_in_mm"], 44 * l + 2 * i + 2)
                    TTn(f_act[:, i, 0:T], f_t1[:, i % 4, 0:T], pb[2 * i % 6 + 1][:, 0:T], ALU.mult).then_inc(S["ffn_act"], 1)
                    if l == 0 and i % 2:
                        ada_column(ADA_N + i // 2)
                ffn_w_out_lo(l, 0)
                for c in range(FC):
                    dve.wait_ge(S["f_hi"], FC * l + c + 1)
                    TTn(f_lo[:, c, 0:T], f_act[:, c, 0:T], f_hi(c, T).bitcast(F32), ALU.subtract).then_inc(S["f_lo"], 1)
                ffn_w_out_lo(l, 1)
                for m in range(DC):
                    if m + 2 < DC:
                        ffn_w_out_lo(l, m + 2)
                    residual(m, "ffn_out_mm", "ffn_out_x", m % 4, T, l, 5, DC * l)
                    if l == 0 and m == 0:
                        ada_column(2 * ADA_N - 1)
                        ada_gains(1)

            def ada_column(g):
                l, s = g // ADA_N, g % ADA_N
                dve.wait_ge(S["ada_tr"], g + 1)
                v = ada_bank(g)[:, 0:P].rearrange("p (j n) -> p j n", n=32)[:, :, 0:2]
                TTn(mod[:, l, 4 * s:4 * s + 4, :], v, col("ada_b", 48 * l + 4 * s, 4).unsqueeze(2).to_broadcast([P, 4, 2]), ALU.add)\
                    .then_inc(S["ada_mod"], 1)

            def ada_gains(l):
                dve.wait_ge(S["ada_mod"], ADA_N * (l + 1))
                for w, nm in enumerate(("n1", "n2")):
                    g = col(nm, DC * l, DC).unsqueeze(2).to_broadcast([P, DC, 2])
                    last = STT(out=modA[:, l, w, :, :], in0=mod[:, l, 24 * w + 8:24 * w + 16, :], scalar=1.0, in1=g, op0=ALU.add, op1=ALU.mult)
                    if w == 0:
                        step(last)
                last.then_inc(S["mod_ready"], 1)

            norm_mod("n1_0", 0, TT)
            dve.wait_ge(S["cols_in"], 16)
            for g in range(ADA_N):
                ada_column(g)
            ada_gains(0)

            def gla_w_in_lo(k):
                n = FIRST["gla"] + k // 2
                w_rest(half(place[n], k % 2), half(place_r[n], k % 2), g_w_hi[k % 2])
            gla_w_in_lo(0)
            for c in range(DC):
                h_rest(0, c, hT[:, c, :], g_h_lo[:, c, :], g_h_hi[:, c, :])
            gla_w_in_lo(1)
            cos, sin = kg[:, 128:384], kg[:, 384:640]
            dve.wait_ge(S["gla_in"], 80)
            for u in range(8):
                if u % 2 == 0:
                    gla_w_in_lo(u // 2 + 2)
                v = g_qk[:, u, 0:NT]
                dve.wait_ge(S["rope_mm"], u + 1)
                TTn(g_tm[:, 0, 0:NT], pb[4 + u % 2][:, 0:NT], sin, ALU.mult).then_inc(S["rope_s"], 1)
                step(TTn(v, v, cos, ALU.mult))
                dve.wait_ge(S["rope_s"], u + 1)
                step(TTn(v, v, g_tm[:, 0, 0:NT], ALU.add))
            for k in range(6, 8):
                gla_w_in_lo(k)
            dve.wait_ge(S["gla_v_mm"], 16)
            step(dve.memset(g_att, 0.0))

            def gate_min(hd):
                h, dr = hd // 2, hd % 2
                tm, tg = g_tm[:, hd % 2, :], g_tg[:, hd % 2, :]
                dve.wait_ge(S["gl_abs"], hd + 1)
                if hd >= 2:
                    dve.wait_ge(S["kd_tr"], hd - 1)
                TS(tm, pb[0][:, :], col("gab", HEADS * dr + h), 0.0, ALU.add, ALU.min).then_inc(S["gl_min"], 1)
                dve.wait_ge(S["gl_ln"], hd + 1)
                dve.wait_ge(S["gl_min"], hd + 1)
                if hd >= 2:
                    dve.wait_ge(S["att_mm"], hd - 1)
                step(TTn(tg, tm, g_e2[:, hd % 2, :], ALU.subtract))
                return tg

            def cumulate(cf, hd, src):
                dr, p = hd % 2, hd % 2
                n = cf.base + hd
                tm, tg, tb, dm = (x[:, p, :] for x in (cf.tm, cf.tg, cf.tb, cf.dm))
                if hd >= 2:
                    dve.wait_ge(S["decay"], 7 * (n - 1))
                step(dve.tensor_tensor_scan(tb, cf.scan, src, 0.0, ALU.mult, ALU.add))
                parts = [(cf.m0, cf.nc_, CH)] + ([(cf.tail[0], 1, cf.tail[1])] if cf.tail else [])

                def v(x, part):
                    o, k, w = part
                    return x[:, o:o + k * w].rearrange("p (c n) -> p c n", n=w)

                def at(x, part, i):
                    o, k, w = part
                    return v(x, part)[:, :, i:i + 1].to_broadcast([P, k, w])
                if hd >= 2:
                    dve.wait_ge(S["kd_tr"], n - 1)
                    dve.wait_ge(S["att_mm"], n - 1)
                if dr == 1:
                    for part in parts:
                        step(TTn(v(tm, part), at(tb, part, part[2] - 1), v(tb, part), ALU.subtract))
                    step(TTn(tb, tm, src, ALU.add))
                main = parts[0]
                step(TTn(v(dm, main), v(tb, main), at(tb, main, CH // 2 - dr), ALU.subtract))
                for part in parts:
                    end = part[2] - 1 if dr == 0 else 0
                    hp = (part[0], 2 * part[1], part[2] // 2) if part is main else part
                    step(TTn(v(tg, hp), v(tb, hp), at(tb, hp, hp[2] // 2), ALU.subtract))
                    last = TTn(v(tm, part), at(tb, part, end), v(tb, part), ALU.subtract)
                    if part is not parts[-1]:
                        step(last)
                last.then_inc(S["cum"], 1)

            def decayed(cf, hd):
                h, dr, p = hd // 2, hd % 2, hd % 2
                n = cf.base + hd
                a, z = cf.m0, cf.m0 + cf.nc_ * CH
                q, k = cf.q(h), cf.k(h, dr)
                for i, (b, x) in enumerate(((cf.e2[:, p, :], k), (cf.tg[:, p, :], q), (cf.dk[:, p, a:z], k[:, a:z]), (cf.dm[:, p, a:z], q[:, a:z]),
                                            (cf.e3[:, two(h, dr), :], q), (cf.tm[:, p, :], k))):
                    dve.wait_ge(S["decay"], 7 * n + i + 1)
                    if i in (2, 3):
                        STT(out=b, in0=b, scalar=1.0, in1=x, op0=ALU.min, op1=ALU.mult).then_inc(S["decayed"], 1)
                    else:
                        TTn(b, b, x, ALU.mult).then_inc(S["decayed"], 1)

            def mask_scores(cf, hd):
                h, dr = hd // 2, hd % 2
                n = cf.base + hd
                dve.wait_ge(S["att_mm"], n + 1)
                if hd >= 2:
                    dve.wait_ge(S["o_mm"], n // 2)
                k = cf.nc_ // 2
                for m, bank in ((m_half[dr], 2), (m_cross[dr], 7)):
                    step(dve.copy_predicated(cf.att[:, dr, 0:k * P].rearrange("p (a n) -> p a n", n=P),
                                             m.bitcast(U32).unsqueeze(1).to_broadcast([P, k, P]),
                                             pb[bank][:, 0:k * P].rearrange("p (a n) -> p a n", n=P)))
                if cf.tail:
                    w = cf.tail[1]
                    step(dve.copy_predicated(cf.att[0:w, dr, k * P:k * P + w], m_half[dr][0:w, 0:w].bitcast(U32), pb[2][0:w, k * P:k * P + w]))
                dve.sem_inc(S["att_cp"], 1)

            def states(cf, hd):
                h, dr = hd // 2, hd % 2
                dve.wait_ge(S["decay"], 7 * (cf.base + hd) + 7)
                od = cf.order[dr]
                for i, c in enumerate(od[:-1]):
                    u = u_ahead(cf, hd) + i
                    dve.wait_ge(S["u_mm"], u + 1)
                    nxt = cf.S[:, dr, od[i + 1], :]
                    if i == 0:
                        dve.tensor_copy(nxt, pb[4 + u % 2][:, 0:cf.DV]).then_inc(S["state"], 1)
                    else:
                        dve.wait_ge(S["state"], u)
                        STT(out=nxt, in0=cf.S[:, dr, c, :], scalar=cf.e5[:, two(h, dr), c:c + 1], in1=pb[4 + u % 2][:, 0:cf.DV],
                            op0=ALU.mult, op1=ALU.add).then_inc(S["state"], 1)

            def gated(cf, h, name, base):
                rsq(name, cf.T)
                E = cf.DV // 128
                for e in range(E):
                    step(STT(out=cf.y(h, e), in0=cf.o(h, e), scalar=cf.gain(h, e), in1=rstd[:, 0:cf.T], op0=ALU.mult, op1=ALU.mult))
                    if cf is G:
                        dve.wait_ge(S["gla_r_ev"], 2 * h + e + 1)
                    TTn(cf.y(h, e), cf.y(h, e), cf.gate(h, e), ALU.mult).then_inc(S["gate_y"], 1)
                dve.wait_ge(S["gate_y"], base + E * (h + 1))
                dve.sem_inc(S["norm_done"], 1)

            def sine_argument(i):
                TWO_PI = 2 * np.pi
                HI = float(np.float32(6.28125))
                LO = float(np.float32(TWO_PI - HI))
                BIG = float(1.5 * 2 ** 23)
                fr = col("ffr", 0, rows=HID)
                dve.wait_ge(S["filt_mm"], i + 1)
                a, k = f_a[0:HID, :], f_k[0:HID, :]
                step(TS(a, pb[i][0:HID, 0:T2], col("fb1" if i == 0 else "fb2", 0, rows=HID), fr, ALU.add, ALU.mult))
                step(TS(k, a, float(1 / TWO_PI), BIG, ALU.mult, ALU.add))
                step(TS(k, k, BIG, None, ALU.subtract))
                step(STT(out=a, in0=k, scalar=-HI, in1=a, op0=ALU.mult, op1=ALU.add))
                step(STT(out=k, in0=k, scalar=-LO, in1=a, op0=ALU.mult, op1=ALU.add))
                TS(k, k, 3.1415925, -3.1415925, ALU.min, ALU.max).then_inc(S["filt_arg"], 1)

            def scan_steps(cf, src, norm_base):
                cumulate(cf, 0, src(0))
                cumulate(cf, 1, src(1))
                decayed(cf, 0)
                for hd in range(8):
                    if hd + 1 < 8:
                        decayed(cf, hd + 1)
                    mask_scores(cf, hd)
                    if hd >= 2 and hd % 2 == 0:
                        gated(cf, hd // 2 - 1, cf.norm(hd // 2 - 1), norm_base)
                    states(cf, hd)
                    if hd + 2 < 8:
                        cumulate(cf, hd + 2, src(hd + 2))
                    if cf is H and hd in (3, 5):
                        sine_argument((hd - 3) // 2)
                gated(cf, HEADS - 1, cf.norm(HEADS - 1), norm_base)
            scan_steps(G, gate_min, 0)
            for i in range(2):
                ffn_w_in_lo(0, i)
            for m in range(DC):
                residual(m, "proj_mm", "proj_x", m % 4, TT, 0, 2)
            norm_mod("n2_0", 1, TT)
            ffn(0, TT)
            dve.wait_ge(S["ffn_out_x"], 2 * DC)
            half_lo(0, "na")
            norm_mod("n1_1", 2, TT)
            for c in range(DC):
                h_rest(2, c, hT[:, c, :], hT_r[:, c, :], h_hi[:, c, :])
            for k in range(1, 12):
                half_lo(k, "na")

            def na_add(i):
                dve.wait_ge(S["na_s_mm"], i + 1)
                dve.wait_ge(S[f"na_bias_in{i % 4}"], 16 * (i // 4 + 1))
                if i >= 3:
                    dve.wait_ge(S["na_tr"], i - 2)
                TTn(n_s[:, i % 3, :], NA_BANK[i % 3][:, :], n_bias[:, i % 4, :], ALU.add).then_inc(S["na_add"], 1)
                dve.wait_ge(S["na_add"], i + 1)
                step(dve.tensor_reduce(n_mx[:, i % 3, 0:1], n_s[:, i % 3, :], AX_X, ALU.max))
                TS(n_mx[:, i % 3, 1:2], n_mx[:, i % 3, 0:1], -1.0, None, ALU.mult).then_inc(S["na_max"], 1)
            na_add(0)
            for i in range(2 * NA_H):
                if i + 1 < 2 * NA_H:
                    na_add(i + 1)
                dve.wait_ge(S["na_exp"], i + 1)
                step(dve.reciprocal(n_rs[:, i % 3, 1:2], n_rs[:, i % 3, 0:1]))
                TS(n_s[:, i % 3, :], n_s[:, i % 3, :], n_rs[:, i % 3, 1:2], None, ALU.mult).then_inc(S["na_p"], 1)
            for i in range(2):
                ffn_w_in_lo(1, i)
            for m in range(DC):
                residual(m, "proj_mm", "proj_x", m % 4, NT, 1, 2, DC)
            norm_mod("n2_1", 3, NT)
            ffn(1, NT)
            dve.wait_ge(S["ffn_out_x"], 3 * DC)
            norm_plain("fin", NT, DC, lambda c: zT[:, c, N_META:T2], lambda c: xT[:, c, 0:NT], lambda c: col("fin", c), "fin_h")
            half_lo(0, "in2")
            norm_plain("mix", T2, DC, lambda c: h2T[:, c, :], lambda c: zT[:, c, :], lambda c: col("nmix", c), "mix_h")
            for c in range(DC):
                h_rest(4, c, h2T[:, c, :], h2_lo[:, c, :], h2_hi[:, c, :])
            half_lo(1, "in2")

            for u in range(12):
                if u % 2 == 0:
                    half_lo(u // 2 + 2, "in2")
                dve.wait_ge(S["hy_mid"], u + 1)
                taps(hy_u[:, u, :], pb[u % 4][:, 0:T2], col("cw2", u), col("cw2", 24 + u), 1, "hy_conv")
            for k in range(8, 10):
                half_lo(k, "in2")
            lb = col("lb", 0, 16).rearrange("p (a r c) -> p a r c", r=2, c=4)
            lv = lbv.rearrange("p (a c) -> p a c", c=4)
            step(TTn(lv[:, 0:2, :], lb[:, :, 1, :], lb[:, :, 0, :], ALU.subtract))
            dve.sem_inc(S["lb_diff"], 1)
            dve.wait_ge(S["lb_exp"], 1)
            step(TS(lv[:, 0:2, :], lv[:, 0:2, :], 1.0, None, ALU.add))
            step(dve.reciprocal(lv[:, 0:2, :], lv[:, 0:2, :]))
            step(TS(lv[:, 2:4, :], lv[:, 0:2, :], -1.0, 1.0, ALU.mult, ALU.add))
            for u in range(8):
                if u % 2 == 0:
                    half_lo(10 + u // 2, "in2")
                dve.wait_ge(S["hg_ev"], 4 + u + 1)
                step(TS(q_lf[:, u, :], q_lf[:, u, :], lbv[:, 8 + u:9 + u], lbv[:, u:u + 1], ALU.mult, ALU.add))
                TS(q_k[:, u, :], q_lf[:, u, :], -1.0, 1.0, ALU.mult, ALU.add).then_inc(S["hg_k"], 1)
            for k in range(14, 16):
                half_lo(k, "in2")
            dve.wait_ge(S["b2_in"], 16)
            dve.wait_ge(S["hg_v_ev"], 3)
            dve.wait_ge(S["hg_ev"], 16)
            step(dve.memset(q_att, 0.0))
            dve.wait_ge(S["hg_lf"], 8)
            scan_steps(H, lambda hd: q_lf[:, 4 * (hd % 2) + hd // 2, :], 8)

            for od in range(2):
                for i, (t0, n) in enumerate(TTILE):
                    g = 3 * od + i
                    dve.wait_ge(S["filt3_mm"], g + 1)
                    b = 2 * (g % 2)
                    step(TTn(f_hs[0:n, od, i, :], pb[b][0:n, :], win[0:n, i, 0, :], ALU.mult))
                    step(TTn(f_b[0:n, :], pb[b + 1][0:n, :], win[0:n, i, 1, :], ALU.mult))
                    step(TTn(f_hd[0:n, od, i, :], f_hs[0:n, od, i, :], f_b[0:n, :], ALU.subtract))
                    TTn(f_hs[0:n, od, i, :], f_hs[0:n, od, i, :], f_b[0:n, :], ALU.add).then_inc(S["filt_hd"], 1)
            for od in range(2):
                for i in range(3):
                    m = FT[i][1]
                    dve.wait_ge(S["dft_mm"], 3 * od + i + 1)
                    if od + i:
                        dve.wait_ge(S["yf"], 3 * od + i)
                    if od == 0 and i == 0:
                        dve.wait_ge(S["spec_ev"], 12)
                    if od == 1 and i == 0:
                        dve.wait_ge(S["idft_mm"], HC)
                    b = 3 + 2 * (i % 2)
                    ur, ui = pb[b][0:m, :], pb[b + 1][0:m, :]
                    hr, hi = spec[0:m, od, i, :], spec[0:m, od, 3 + i, :]
                    t0_, t1_ = hy_tmp[0:m, 0, :], hy_tmp[0:m, 1, :]
                    step(TTn(t0_, ur, hr, ALU.mult))
                    step(TTn(t1_, ui, hi, ALU.mult))
                    step(TTn(yf[0:m, i, :], t0_, t1_, ALU.subtract))
                    step(TTn(t0_, ur, hi, ALU.mult))
                    step(TTn(t1_, ui, hr, ALU.mult))
                    TTn(yf[0:m, 3 + i, :], t0_, t1_, ALU.add).then_inc(S["yf"], 1)
                for c in range(HC):
                    dve.wait_ge(S["idft_mm"], HC * od + c + 1)
                    if od == 0 and c == 0:
                        dve.wait_ge(S["u_tr"], 3)
                    v = hy_u[:, c, :]
                    step(STT(out=v, in0=v, scalar=col("skip", HC * od + c), in1=pb[c][:, 0:T2], op0=ALU.mult, op1=ALU.add))
                    TTn(v, v, hy_u[:, 4 * (od + 1) + c, :], ALU.mult).then_inc(S["hy_z"], 1)
            dve.wait_ge(S["hy_z"], 2 * HC)
            norm_plain("hyena", T2, HC, lambda c: y_cat[:, c, :], lambda c: hy_u[:, c, :], lambda c: col("hyn", c), "hyena_y")
            dve.sem_inc(S["hyena_done"], 1)
            for m in range(DC):
                dve.wait_ge(S["proj_mm"], 2 * DC + m + 1)
                TTn(zT[:, m, :], zT[:, m, :], pb[m % 4][:, 0:T2], ALU.add).then_inc(S["proj_x"], 1)
            dve.wait_ge(S["proj_x"], 4 * DC)
            norm_plain("nffn", T2, DC, lambda c: h2T[:, c, :], lambda c: zT[:, c, :], lambda c: col("nffn", c), "nffn_h")

            dve.wait_ge(S["zeroed"], 3)
            dve.wait_ge(S["route_in"], 32)
            dve.wait_ge(S["route_mm"], 1)
            for i, (t0, n) in enumerate(TTILE):
                step(dve.tensor_copy(r_lg[0:n, i, :], pb[7][0:n, 72 * i:72 * i + 72]))
            desc = kr[:, 0:8].unsqueeze(1).to_broadcast([P, 3, 8])
            valid = kr[:, 8:11]
            sm = [r_sm[:, i, :] for i in range(40)]
            oh = [r_oh[:, i, :].rearrange("p (t e) -> p t e", e=8) for i in range(6)]
            gl = r_lg[:, :, 0:NG]

            def b8(x):
                return x.unsqueeze(2).to_broadcast([P, 3, 8])

            def first_max(vals, mx, o, tmp):
                step(dve.tensor_reduce(mx, vals, AX_X, ALU.max))
                step(TTn(o, vals, b8(mx), ALU.is_ge))
                step(TTn(o, o, desc, ALU.mult))
                step(dve.tensor_reduce(tmp, o, AX_X, ALU.max))
                step(TTn(o, o, b8(tmp), ALU.is_equal))
            first_max(gl, sm[0], oh[0], sm[1])
            step(TTn(oh[4], gl, b8(sm[0]), ALU.subtract))
            dve.sem_inc(S["r_diff"], 1)
            dve.wait_ge(S["r_exp"], 1)
            step(dve.tensor_reduce(sm[2], oh[4], AX_X, ALU.add))
            step(dve.reciprocal(sm[3], sm[2]))
            t1 = r_t1.rearrange("p t (g e) -> p t g e", e=8)
            for i in range(3):
                step(TTn(t1[:, i, :, :], r_lg[:, i, NG:].rearrange("p (g e) -> p g e", e=8),
                         oh[0][:, i, :].unsqueeze(2).to_broadcast([P, 8, 8]), ALU.mult))
                step(dve.tensor_reduce(oh[5][:, i, :], t1[:, i, :, :].rearrange("p g e -> p e g"), AX_X, ALU.add))
            step(dve.tensor_reduce(sm[4], oh[5], AX_X, ALU.max))
            step(TTn(oh[5], oh[5], b8(sm[4]), ALU.subtract))
            dve.sem_inc(S["r_diff"], 1)
            dve.wait_ge(S["r_exp"], 2)
            step(dve.tensor_reduce(sm[5], oh[5], AX_X, ALU.add))
            step(dve.reciprocal(sm[6], sm[5]))
            step(TTn(oh[5], oh[5], b8(sm[6]), ALU.mult))
            first_max(oh[5], sm[7], oh[1], sm[8])
            step(STT(out=oh[5], in0=oh[1], scalar=-2.0, in1=oh[5], op0=ALU.mult, op1=ALU.add))
            first_max(oh[5], sm[9], oh[2], sm[10])
            step(TTn(sm[11], sm[7], sm[9], ALU.add))
            step(dve.reciprocal(sm[12], sm[11]))
            step(TTn(sm[12], sm[12], sm[3], ALU.mult))
            step(TTn(sm[13], sm[12], sm[7], ALU.mult))
            step(TTn(sm[14], sm[12], sm[9], ALU.mult))
            step(TTn(oh[0], oh[0], b8(valid), ALU.mult))
            for k in range(2):
                for i in range(3):
                    step(TTn(r_M[:, k, i, :].rearrange("p (g e) -> p g e", e=8), oh[0][:, i, :].unsqueeze(2).to_broadcast([P, 8, 8]),
                             oh[1 + k][:, i, :].unsqueeze(1).to_broadcast([P, 8, 8]), ALU.mult))
            TTn(r_M[:, 2, :, :], r_M[:, 0, :, :], r_M[:, 1, :, :], ALU.add).then_inc(S["route_M"], 1)
            dve.wait_ge(S["pos_mm"], 1)
            cnt, incl, start = r_cnt[:, 0, :], r_cnt[:, 1, :], r_cnt[:, 2, :]
            step(dve.tensor_copy(cnt, pb[6][:, 192:256]))
            step(dve.tensor_tensor_scan(incl, one1[:, 0:NE], cnt, 0.0, ALU.mult, ALU.add))
            step(TTn(start, incl, cnt, ALU.subtract))
            step(TTn(r_t2, pb[6][:, 0:192].rearrange("p (t e) -> p t e", e=NE), start.unsqueeze(1).to_broadcast([P, 3, NE]), ALU.add))
            iota = kr[:, 75:75 + SLOTS]
            for k in range(2):
                step(TTn(r_t1, r_t2, r_M[:, k, :, :], ALU.mult))
                step(dve.tensor_reduce(sm[15 + k], r_t1, AX_X, ALU.add))
                step(TTn(sm[15 + k], sm[15 + k], valid, ALU.add))
                step(TS(sm[15 + k], sm[15 + k], -1.0, None, ALU.add))
            for i in range(3):
                step(TS(r_Sg[:, i, :], iota, sm[15][:, i:i + 1], None, ALU.is_equal))
                step(STT(out=r_S[:, i, :], in0=iota, scalar=sm[16][:, i:i + 1], in1=r_Sg[:, i, :], op0=ALU.is_equal, op1=ALU.add))
            dve.sem_inc(S["route_S"], 1)
            c0, s0, eio = cnt[0:1, :], start[0:1, :], kr[0:1, 11:75]
            tab_r, tab_e = r_ti[0:1, 0:NB], r_ti[0:1, NB:2 * NB]
            dve.tensor_copy(tab_r.bitcast(I32)[:, 0:NE], s0).then_inc(S["tables"], 1)
            for i in range(3):
                step(TS(r_Sg[:, i, :], iota, sm[15][:, i:i + 1], sm[13][:, i:i + 1], ALU.is_equal, ALU.mult))
                for hf in range(2):
                    o = T2 * hf
                    step(TS(r_sel, iota[:, o:o + T2], sm[16][:, i:i + 1], sm[14][:, i:i + 1], ALU.is_equal, ALU.mult))
                    step(TTn(r_Sg[:, i, o:o + T2], r_Sg[:, i, o:o + T2], r_sel, ALU.add))
            dve.sem_inc(S["route_S"], 1)

            def extra_tables():
                ex, exn, tmp, w_ = r_cnt[0:1, 3, :], r_cnt[0:1, 4, :], r_cnt[0:1, 5, :], r_row[0:1, 0, :]
                step(TS(ex, c0, float(WIN), None, ALU.is_gt))
                for k in range(2, -(-T2 // WIN)):
                    step(STT(out=ex, in0=c0, scalar=float(k * WIN), in1=ex, op0=ALU.is_gt, op1=ALU.add))
                step(dve.tensor_tensor_scan(exn, one1[0:1, 0:NE], ex, 0.0, ALU.mult, ALU.add))
                step(dve.tensor_copy(r_ti.bitcast(I32)[0:1, 2 * NB:2 * NB + 1], exn[:, NE - 1:NE]))
                step(TTn(exn, exn, ex, ALU.subtract))
                for j in range(EXTRA):
                    a, b = r_row[0:1, 1, :], tmp
                    step(TTn(w_, exn, ex, ALU.add))
                    step(TS(w_, w_, float(j), None, ALU.is_gt))
                    step(STT(out=w_, in0=exn, scalar=float(j), in1=w_, op0=ALU.is_le, op1=ALU.mult))
                    step(TS(a, exn, float(-WIN), float(WIN * (j + 1)), ALU.mult, ALU.add))
                    step(TS(b, c0, float(-WIN), None, ALU.add))
                    step(TTn(a, a, b, ALU.min))
                    step(TTn(a, a, s0, ALU.add))
                    step(TTn(a, a, w_, ALU.mult))
                    step(dve.tensor_reduce(r_sm[0:1, 24 + j, 0:1], a, AX_X, ALU.add))
                    step(TTn(a, eio, w_, ALU.mult))
                    step(dve.tensor_reduce(r_sm[0:1, 24 + j, 1:2], a, AX_X, ALU.add))
                    step(dve.tensor_reduce(r_sm[0:1, 24 + j, 2:3], w_, AX_X, ALU.add))
                    step(TS(r_sm[0:1, 24 + j, 2:3], r_sm[0:1, 24 + j, 2:3], -float(SLOTS), float(SLOTS), ALU.mult, ALU.add))
                    step(TTn(r_sm[0:1, 24 + j, 0:1], r_sm[0:1, 24 + j, 0:1], r_sm[0:1, 24 + j, 2:3], ALU.add))
                    step(dve.tensor_copy(tab_r.bitcast(I32)[:, NE + j:NE + j + 1], r_sm[0:1, 24 + j, 0:1]))
                    step(dve.tensor_copy(tab_e.bitcast(I32)[:, NE + j:NE + j + 1], r_sm[0:1, 24 + j, 1:2]))
                dve.sem_inc(S["tables"], 1)

            dve.wait_ge(S["tables"], 1)
            dve.wait_ge(S["xg_ev"], 16)
            dve.wait_ge(S["zeroed"], 3)
            dve.wait_ge(S["sgt_ev"], 5)
            dve.memset(e_hid[64:128, :, :], 0.0).then_inc(S["zeroed"], 1)
            rows = r_ti.bitcast(I32)

            def window(j, row):
                dve.tensor_copy(e_xw[:, j, :, :], xg[:, :, bass.ds(row, WIN)]).then_inc(S["xw"], 1)

            def hidden(j):
                TTn(e_hid[0:64, j, :], e_sg[0:64, j, :], pb[j][64:128, :], ALU.mult).then_inc(S["hid"], 1)

            def y_copy(j):
                dve.tensor_copy(e_y[:, j, :], pb[5 + j][:, :]).then_inc(S["y_cp"], 1)

            def window_pass(b, j, i=0):
                row = dve.value_load(rows[0:1, bass.ds(i + b, 1)], min_val=0, max_val=SLOTS)
                if b >= 2:
                    dve.wait_ge(S["gu_mm"], i + b - 1)
                window(j, row)

            def hidden_pass(b, j, i=0):
                dve.wait_ge(S["silu"], i + b + 1)
                if b >= 2:
                    dve.wait_ge(S["hid_tr"], i + b - 1)
                hidden(j)

            def y_copy_pass(b, j, i=0):
                dve.wait_ge(S["down_mm"], i + b + 1)
                if b >= 2:
                    dve.wait_ge(S["y_out"], 32 * i + 32 * (b - 1))
                y_copy(j)
            window_pass(0, 0)
            window_pass(1, 1)
            hidden_pass(0, 0)
            for b in range(2):
                window_pass(b + 2, b % 2)
                hidden_pass(b + 1, (b + 1) % 2)
                y_copy_pass(b, b % 2)
            LOOPS = (NE - 4) // 2
            for a, z in ((0, LOOPS // 2), (LOOPS // 2, LOOPS)):
                if a:
                    extra_tables()
                with dve.Fori(a, z) as i:
                    for b in (2, 3):
                        window_pass(b + 2, b % 2, 2 * i)
                        hidden_pass(b + 1, (b + 1) % 2, 2 * i)
                        y_copy_pass(b, b % 2, 2 * i)
            for b in range(2 + 2 * LOOPS, NE):
                if b + 2 < NE:
                    window_pass(b + 2, b % 2)
                if b + 1 < NE:
                    hidden_pass(b + 1, (b + 1) % 2)
                y_copy_pass(b, b % 2)
            dve.wait_ge(S["tables"], 2)
            n_extra = dve.value_load(rows[0:1, 2 * NB:2 * NB + 1], min_val=0, max_val=EXTRA)
            with dve.Fori(0, EXTRA) as j:
                with dve.If(j < n_extra):
                    row = dve.value_load(rows[0:1, bass.ds(j + NE, 1)], min_val=0, max_val=SLOTS)
                    dve.wait_ge(S["extra_free"], j + 1)
                    window(0, row)
                    dve.wait_ge(S["silu"], j + NE + 1)
                    hidden(0)
                    dve.wait_ge(S["down_mm"], j + NE + 1)
                    y_copy(0)
            for m in range(DC):
                dve.wait_ge(S["comb_mm"], m + 1)
                TTn(zT[:, m, :], zT[:, m, :], pb[m % 4][:, 0:T2], ALU.add).then_inc(S["moe_x"], 1)
            dve.wait_ge(S["moe_x"], DC)
            norm_plain("nfin", T2, DC, lambda c: h2T[:, c, :], lambda c: zT[:, c, :], lambda c: col("nfin", c), "nfin_h")


def channel_columns(i):
    def c(a, n=P):
        a = np.asarray(a, np.float32).reshape(-1, n)
        return np.pad(a, ((0, 0), (0, P - n)))
    parts = {"c2": np.stack([np.reshape(i["c"], (DC, P)), np.reshape(i["c_ctx"], (DC, P))], 1), "n1": i["norm1_g"], "n2": i["norm2_g"],
             "fin": i["final_g"], "ada_b": i["ada_b"], "fcw": i["ffn_conv_w"], "fcb": i["ffn_conv_b"], "gab": i["gla_a_b"],
             "gng": i["gla_norm_g"], "cw2": i["conv_w_2"], "cb2": i["conv_b_2"], "skip": i["filt_skip_2"], "hyn": i["hyena_norm_2"],
             "lb": np.stack([i["lb_fwd_2"], i["lb_bwd_2"]]), "hgn": i["hgrn_norm_2"], "nmix": i["norm_mix_2"],
             "nffn": i["norm_ffn_2"], "nfin": i["norm_final_2"], "fb1": i["filt_b1_2"], "fb2": i["filt_b2_2"], "ffr": i["filt_freq_2"]}
    return np.ascontiguousarray(np.concatenate([c(parts[n], HID if n in ("fb1", "fb2", "ffr") else P) for n, _ in COLS]).T)


def bias_windows(rpb):
    rows = NT // GRID
    out = np.full((NA_H, rows, GRID, rows, GRID), -1e30, np.float32)
    for r in range(rows):
        for k in range(rows):
            for c in range(GRID):
                s = min(max(c - NA_KW // 2, 0), GRID - NA_KW)
                out[:, r, c, k, s:s + NA_KW] = rpb[:, k - r + NA_KH - 1, s - c + NA_KW - 1:s - c + 2 * NA_KW - 1]
    return out.reshape(NA_H, 2, P, NT)


def constants():
    f = np.float32
    j = np.arange(CH)
    same = j[:, None] // (CH // 2) == j[None, :] // (CH // 2)
    masks = []
    for causal in (j[:, None] <= j[None, :], j[:, None] >= j[None, :]):
        masks += [np.kron(np.eye(2), causal & same).astype(f), np.kron(np.eye(2), causal & ~same).astype(f)]
    p = np.arange(P)
    k_a = np.concatenate([np.eye(P, dtype=f)] + masks + [(p[:, None] < p[None, :]).astype(f)], 1)
    perm = np.zeros((P, P), f)
    for q in range(P):
        if q % 64 < 32:
            perm[q + 32, q] = -1
        else:
            perm[q - 32, q] = 1
    half = P // 2
    inv = (1.0 / (f(10000.0) ** (np.arange(0, half, 2, dtype=f) / f(half)))).astype(f)
    pos = np.arange(NT)
    ang = np.where(p[:, None] < half, (pos // GRID)[None, :], (pos % GRID)[None, :]).astype(f) * inv[p % 32][:, None]
    scan = np.ones((P, TT), f)
    scan[:, ::CH] = 0
    k_g = np.concatenate([perm, np.cos(ang).astype(f), np.sin(ang).astype(f), scan], 1)
    scan2 = np.ones((P, T2), f)
    scan2[:, 0] = 0
    scan2[:, N_META::CH] = 0
    th = 2 * np.pi * ((np.arange(T2)[:, None] * np.arange(NF)[None, :]) % NFFT) / NFFT
    dft = np.concatenate([np.cos(th), -np.sin(th)], 1).astype(f)
    wt = np.full((NF, 1), 2.0 / NFFT)
    wt[0] = wt[-1] = 1.0 / NFFT
    idft = np.concatenate([wt * np.cos(th.T), -wt * np.sin(th.T)], 0).astype(f)
    t = np.arange(T2, dtype=f) / f(T2 - 1)
    bands = np.linspace(1e-4, (EMB - 1) // 2 - 1, (EMB - 1) // 2, dtype=f)
    a2 = (f(2.0 * np.pi / T2) * np.arange(T2, dtype=f))[:, None] * bands[None, :]
    z = np.concatenate([t[:, None], np.cos(a2), -np.sin(a2)], 1).astype(f)
    deltas = np.abs(np.linspace(np.log(1e-2) / 1.5, np.log(1e-2) / 0.3, HY, dtype=f))
    win = np.repeat(np.exp(-t[:, None] * deltas[None, :]).astype(f)[:, None, :], 2, 1)
    win[0, 1, :] = 0
    valid = np.zeros((P, 3), f)
    for i, (_, n) in enumerate(TTILE):
        valid[:n, i] = 1
    k_r = np.concatenate([np.tile(np.arange(8, 0, -1, dtype=f), (P, 1)), valid, np.tile(np.arange(NE, dtype=f), (P, 1)),
                          np.tile(np.arange(SLOTS, dtype=f), (P, 1))], 1)
    return {"k_a": k_a, "k_g": k_g, "k_scan2": scan2, "k_dft": dft, "k_idft": idft, "k_zT": z.T, "k_win": win, "k_route": k_r}


_PLAIN = ["ada_w", "ffn_w_in", "ffn_w_out"]
_FIRST = ["gla_w_in", "gla_w_out", "gla_a_w1", "gla_a_w2", "na_w_qkv", "na_w_out", "w_in_2", "w_out_2", "filt_w1_2", "filt_w2_2",
          "filt_w3_2", "w_gate_2", "w_up_2", "w_down_2"]


def kernel(**inputs):
    import concourse.bacc as bacc
    from concourse.bass_utils import run_bass_kernel_spmd as run

    i = {k: np.asarray(v) for k, v in inputs.items()}
    a = dict(constants())
    a["xT"] = np.concatenate([i["x"][0], i["ctx"][0]]).T
    a["metaT"] = i["meta_tokens_2"].T
    a["cols"] = channel_columns(i)
    a["na_bias"] = bias_windows(i["na_rpb"][0])
    a["w_route"] = np.concatenate([i["w_router_group_2"][0], i["w_router_expert_2"][0].reshape(D, NE)], 1)
    for n in _PLAIN:
        a[n] = i[n]
    for n in _FIRST:
        a[n] = i[n][0]
    nc = bacc.Bacc("TRN2", target_bir_lowering=False, num_devices=1)
    arrays = {f"in_{n}": np.ascontiguousarray(v) for n, v in a.items()}
    handles = {n: nc.dram_tensor(f"in_{n}", arrays[f"in_{n}"].shape, F32, kind="ExternalInput").ap() for n in a}
    out = nc.dram_tensor("out_yT", (D, NT), F32, kind="ExternalOutput").ap()
    build(nc, handles, out)
    r = run(nc, [arrays], core_ids=[0])
    return np.ascontiguousarray(r.results[0]["out_yT"].T)[None]
```
